# Optimizing a Trainium2 kernel written in Bass

```python
import jax, jax.numpy as jnp
from jax import lax
import numpy as np
import math

D_MODEL = 1024
BATCH = 1
SEQ = 256
DEPTH = 2

GRID_W = 64
CTX_LEN = 256
HEAD_DIM = 64
FOURIER_GROUPS = 4
FOURIER_GROUP_CH = 64
FOURIER_W = FOURIER_GROUPS * FOURIER_GROUP_CH
G_HEADS = 8
G_KV = 2
G_GROUP = G_HEADS // G_KV
W_HEADS = 4
W_KV = 2
W_GROUP = W_HEADS // W_KV
WINDOW = 128
Q_BLOCK = 128
N_BRANCH = 3
SPLIT_SIZES = (FOURIER_W,
               G_HEADS * HEAD_DIM, G_KV * HEAD_DIM, G_KV * HEAD_DIM,
               W_HEADS * HEAD_DIM, W_KV * HEAD_DIM, W_KV * HEAD_DIM,
               N_BRANCH * D_MODEL)
IN_W = sum(SPLIT_SIZES)
ROPE_THETA = 10000.0
N_EXPERTS = 16
CAPACITY_FACTOR = 2
EXPERT_FF = D_MODEL
EPS = 1e-6
NEG_INF = -1e30


def rms_norm(x, g):
    xf = x.astype(jnp.float32)
    y = xf * lax.rsqrt(jnp.mean(jnp.square(xf), axis=-1, keepdims=True) + EPS)
    return (y * g.astype(jnp.float32)).astype(x.dtype)

def modulate(h, shift, scale):
    return h * (1 + scale[:, None, :]) + shift[:, None, :]

def heads(z, n):
    return z.reshape(z.shape[:-1] + (n, HEAD_DIM))

def split_proj(z):
    points = np.cumsum(SPLIT_SIZES)[:-1].tolist()
    return jnp.split(z, points, axis=-1)

def axial_rope_angles(n_tokens):
    rows = n_tokens // GRID_W
    r, col = jnp.meshgrid(jnp.arange(rows), jnp.arange(GRID_W), indexing="ij")
    half = HEAD_DIM // 2
    inv = ROPE_THETA ** (-jnp.arange(0, half, 2, dtype=jnp.float32) / half)
    ang = jnp.concatenate([r.reshape(-1, 1).astype(jnp.float32) * inv,
                           col.reshape(-1, 1).astype(jnp.float32) * inv], axis=-1)
    return jnp.cos(ang), jnp.sin(ang)

def apply_rope(x, cos, sin):
    xf = x.astype(jnp.float32).reshape(x.shape[:-1] + (HEAD_DIM // 2, 2))
    x0, x1 = xf[..., 0], xf[..., 1]
    cs, sn = cos[None, :, None, :], sin[None, :, None, :]
    out = jnp.stack([x0 * cs - x1 * sn, x0 * sn + x1 * cs], axis=-1)
    return out.reshape(x.shape).astype(x.dtype)

def attend(q, k, v):
    s = jnp.einsum("bqhgd,bkhd->bhgqk", q, k).astype(jnp.float32) * (HEAD_DIM ** -0.5)
    p = jax.nn.softmax(s, axis=-1).astype(v.dtype)
    return jnp.einsum("bhgqk,bkhd->bqhgd", p, v)

def global_attention(q_l, k_l, v_l, k_c, v_c):
    B, T = q_l.shape[:2]
    nb = T // Q_BLOCK
    k_all = jnp.concatenate([k_c, k_l], axis=1)
    v_all = jnp.concatenate([v_c, v_l], axis=1)
    qb = q_l.reshape(B, nb, Q_BLOCK, G_KV, G_GROUP, HEAD_DIM).transpose(1, 0, 2, 3, 4, 5)
    ob = lax.map(lambda qq: attend(qq, k_all, v_all), qb)
    return ob.transpose(1, 0, 2, 3, 4, 5).reshape(B, T, G_HEADS * HEAD_DIM)

def window_attention(q_l, k_l, v_l, k_c, v_c, sink):
    B, T = q_l.shape[:2]
    L = k_c.shape[1]
    nb = T // Q_BLOCK
    q = q_l.reshape(B, nb, Q_BLOCK, W_KV, W_GROUP, HEAD_DIM)

    def band(t):
        tp = jnp.pad(t, ((0, 0), (Q_BLOCK, Q_BLOCK), (0, 0), (0, 0)))
        tp = tp.reshape(B, nb + 2, Q_BLOCK, W_KV, HEAD_DIM)
        return jnp.concatenate([tp[:, :-2], tp[:, 1:-1], tp[:, 2:]], axis=2)

    kb, vb = band(k_l), band(v_l)
    scale = HEAD_DIM ** -0.5
    s_c = jnp.einsum("bnqhgd,bkhd->bnhgqk", q, k_c).astype(jnp.float32) * scale
    s_b = jnp.einsum("bnqhgd,bnkhd->bnhgqk", q, kb).astype(jnp.float32) * scale
    qpos = jnp.arange(Q_BLOCK)[:, None]
    kpos = jnp.arange(3 * Q_BLOCK)[None, :]
    rel = qpos - kpos + Q_BLOCK
    key_abs = (jnp.arange(nb)[:, None, None] - 1) * Q_BLOCK + kpos[None]
    valid = (jnp.abs(rel)[None] <= WINDOW) & (key_abs >= 0) & (key_abs < T)
    s_b = jnp.where(valid[None, :, None, None], s_b, NEG_INF)
    s_sink = jnp.broadcast_to(sink.astype(jnp.float32).reshape(1, 1, W_KV, W_GROUP, 1, 1),
                              s_c.shape[:-1] + (1,))
    p = jax.nn.softmax(jnp.concatenate([s_c, s_b, s_sink], axis=-1), axis=-1).astype(v_l.dtype)
    o = (jnp.einsum("bnhgqk,bkhd->bnqhgd", p[..., :L], v_c)
         + jnp.einsum("bnhgqk,bnkhd->bnqhgd", p[..., L:L + 3 * Q_BLOCK], vb))
    return o.reshape(B, T, W_HEADS * HEAD_DIM)

def sink_attention_ctx(q_c, k_c, v_c, sink):
    B, L = q_c.shape[:2]
    q = q_c.reshape(B, L, W_KV, W_GROUP, HEAD_DIM)
    s = jnp.einsum("bqhgd,bkhd->bhgqk", q, k_c).astype(jnp.float32) * (HEAD_DIM ** -0.5)
    s_sink = jnp.broadcast_to(sink.astype(jnp.float32).reshape(1, W_KV, W_GROUP, 1, 1),
                              s.shape[:-1] + (1,))
    p = jax.nn.softmax(jnp.concatenate([s, s_sink], axis=-1), axis=-1)[..., :L].astype(v_c.dtype)
    o = jnp.einsum("bhgqk,bkhd->bqhgd", p, v_c)
    return o.reshape(B, L, W_HEADS * HEAD_DIM)

def fourier_mix(u):
    B, N, _ = u.shape
    g = u.astype(jnp.float32).reshape(B, N, FOURIER_GROUPS, FOURIER_GROUP_CH)
    f = jnp.fft.fft2(g, axes=(1, 3), norm="ortho").real
    return f.reshape(B, N, FOURIER_W).astype(u.dtype)

def gated_merge(gate_cols, f_mix, o_g, o_w, w_br_fourier, w_br_global, w_br_window, w_out):
    g = jax.nn.sigmoid(gate_cols).reshape(gate_cols.shape[:-1] + (N_BRANCH, D_MODEL))
    m = (g[..., 0, :] * (f_mix @ w_br_fourier)
         + g[..., 1, :] * (o_g @ w_br_global)
         + g[..., 2, :] * (o_w @ w_br_window))
    return m @ w_out

def mixer_sublayer(h, hc, cos, sin, w_in, q_norm_g, k_norm_g, sink,
                   w_br_fourier, w_br_global, w_br_window, w_out, need_ctx):
    B, T, _ = h.shape
    L = hc.shape[1]
    lf, lgq, lgk, lgv, lwq, lwk, lwv, lgate = split_proj(h @ w_in)
    cf, cgq, cgk, cgv, cwq, cwk, cwv, cgate = split_proj(hc @ w_in)
    kc_g = rms_norm(heads(cgk, G_KV), k_norm_g)
    vc_g = heads(cgv, G_KV)
    kc_w = heads(cwk, W_KV)
    vc_w = heads(cwv, W_KV)
    q_g = apply_rope(rms_norm(heads(lgq, G_HEADS), q_norm_g), cos, sin)
    k_g = apply_rope(rms_norm(heads(lgk, G_KV), k_norm_g), cos, sin)
    o_g = global_attention(q_g, k_g, heads(lgv, G_KV), kc_g, vc_g)
    q_w = apply_rope(heads(lwq, W_HEADS), cos, sin)
    k_w = apply_rope(heads(lwk, W_KV), cos, sin)
    o_w = window_attention(q_w, k_w, heads(lwv, W_KV), kc_w, vc_w, sink)
    y = gated_merge(lgate, fourier_mix(lf), o_g, o_w,
                    w_br_fourier, w_br_global, w_br_window, w_out)
    if not need_ctx:
        return y, None
    qc_g = rms_norm(heads(cgq, G_HEADS), q_norm_g).reshape(B, L, G_KV, G_GROUP, HEAD_DIM)
    oc_g = attend(qc_g, kc_g, vc_g).reshape(B, L, G_HEADS * HEAD_DIM)
    oc_w = sink_attention_ctx(heads(cwq, W_HEADS), kc_w, vc_w, sink)
    yc = gated_merge(cgate, fourier_mix(cf), oc_g, oc_w,
                     w_br_fourier, w_br_global, w_br_window, w_out)
    return y, yc

def expert_choice_ffn(h, w_router, w_gate_e, w_up_e, w_down_e):
    B, N, _ = h.shape
    cap = CAPACITY_FACTOR * N // N_EXPERTS
    aff = jax.nn.softmax((h @ w_router).astype(jnp.float32), axis=-1)
    top_aff, top_idx = lax.top_k(aff.transpose(0, 2, 1), cap)
    bidx = jnp.arange(B)[:, None, None]
    xg = h[bidx, top_idx]
    a = jnp.einsum("becd,edf->becf", xg, w_gate_e)
    u = jnp.einsum("becd,edf->becf", xg, w_up_e)
    out = jnp.einsum("becf,efd->becd", jax.nn.silu(a) * u, w_down_e) * top_aff[..., None].astype(h.dtype)
    return jnp.zeros_like(h).at[bidx, top_idx].add(out)

def first_inputs(seed: int = 0) -> dict:
    key = jax.random.key(seed)
    ks = jax.random.split(key, 24)
    D, F, E = D_MODEL, EXPERT_FF, N_EXPERTS
    nrm = jax.random.normal
    f32 = jnp.float32
    return {
        "x": nrm(ks[0], (BATCH, SEQ, D), f32),
        "c": nrm(ks[1], (BATCH, D), f32),
        "ctx": nrm(ks[2], (BATCH, CTX_LEN, D), f32),
        "c_ctx": nrm(ks[3], (D,), f32),
        "w_ada": nrm(ks[4], (DEPTH, D, 6 * D), f32) * (0.5 * D ** -0.5),
        "b_ada": nrm(ks[5], (DEPTH, 6 * D), f32) * 0.01,
        "norm1_g": 1.0 + 0.05 * nrm(ks[6], (DEPTH, D), f32),
        "w_in": nrm(ks[7], (DEPTH, D, IN_W), f32) * D ** -0.5,
        "q_norm_g": 1.0 + 0.05 * nrm(ks[8], (DEPTH, HEAD_DIM), f32),
        "k_norm_g": 1.0 + 0.05 * nrm(ks[9], (DEPTH, HEAD_DIM), f32),
        "sink": 0.5 * nrm(ks[10], (DEPTH, W_HEADS), f32),
        "w_br_fourier": nrm(ks[11], (DEPTH, FOURIER_W, D), f32) * FOURIER_W ** -0.5,
        "w_br_global": nrm(ks[12], (DEPTH, G_HEADS * HEAD_DIM, D), f32) * (G_HEADS * HEAD_DIM) ** -0.5,
        "w_br_window": nrm(ks[13], (DEPTH, W_HEADS * HEAD_DIM, D), f32) * (W_HEADS * HEAD_DIM) ** -0.5,
        "w_out": nrm(ks[14], (DEPTH, D, D), f32) * D ** -0.5,
        "norm2_g": 1.0 + 0.05 * nrm(ks[15], (DEPTH, D), f32),
        "w_router": nrm(ks[16], (DEPTH, D, E), f32) * D ** -0.5,
        "w_gate_e": nrm(ks[17], (DEPTH, E, D, F), f32) * D ** -0.5,
        "w_up_e": nrm(ks[18], (DEPTH, E, D, F), f32) * D ** -0.5,
        "w_down_e": nrm(ks[19], (DEPTH, E, F, D), f32) * F ** -0.5,
        "final_g": 1.0 + 0.05 * nrm(ks[20], (D,), f32),
    }

def first_block(x, c, ctx, c_ctx, w_ada, b_ada, norm1_g, w_in, q_norm_g, k_norm_g, sink,
              w_br_fourier, w_br_global, w_br_window, w_out, norm2_g, w_router,
              w_gate_e, w_up_e, w_down_e, final_g):
    T = x.shape[1]
    cos, sin = axial_rope_angles(T)
    xc = ctx
    silu_c = jax.nn.silu(c)
    silu_cc = jax.nn.silu(c_ctx)[None]
    for l in range(DEPTH):
        need_ctx = l < DEPTH - 1
        mod = silu_c @ w_ada[l] + b_ada[l]
        mod_c = silu_cc @ w_ada[l] + b_ada[l]
        sh1, sc1, g1, sh2, sc2, g2 = jnp.split(mod, 6, axis=-1)
        csh1, csc1, cg1, csh2, csc2, cg2 = jnp.split(mod_c, 6, axis=-1)
        h = modulate(rms_norm(x, norm1_g[l]), sh1, sc1)
        hc = modulate(rms_norm(xc, norm1_g[l]), csh1, csc1)
        y, yc = mixer_sublayer(h, hc, cos, sin, w_in[l], q_norm_g[l], k_norm_g[l], sink[l],
                               w_br_fourier[l], w_br_global[l], w_br_window[l], w_out[l], need_ctx)
        x = x + g1[:, None, :] * y
        h = modulate(rms_norm(x, norm2_g[l]), sh2, sc2)
        x = x + g2[:, None, :] * expert_choice_ffn(h, w_router[l], w_gate_e[l], w_up_e[l], w_down_e[l])
        if need_ctx:
            xc = xc + cg1[:, None, :] * yc
            hc = modulate(rms_norm(xc, norm2_g[l]), csh2, csc2)
            xc = xc + cg2[:, None, :] * expert_choice_ffn(hc, w_router[l], w_gate_e[l], w_up_e[l], w_down_e[l])
    return rms_norm(x, final_g)


DEPTH_2 = 1

CHUNK = 64

GLA_HEADS = 4
GLA_DK = 64
GLA_DV = 128
GLA_INNER = GLA_HEADS * GLA_DV
GLA_RANK = 16
GLA_GATE_NORM = 16.0

SSD_HEADS = 8
SSD_P = 64
SSD_N = 64
SSD_GROUPS = 2
SSD_INNER = SSD_HEADS * SSD_P
SSD_CONV_DIM = SSD_INNER + 2 * SSD_GROUPS * SSD_N
CONV_K = 3

D_MIX = GLA_INNER + SSD_INNER
D_FF = -(-8 * D_MODEL // (3 * 256)) * 256

PROJ_SIZES = (GLA_HEADS * GLA_DK, GLA_HEADS * GLA_DK, GLA_INNER, GLA_INNER, 2 * GLA_RANK,
              SSD_INNER, SSD_CONV_DIM, 2 * SSD_HEADS)
D_IN_PROJ = sum(PROJ_SIZES)
PROJ_SPLITS = tuple(int(s) for s in np.cumsum(PROJ_SIZES)[:-1])


def rms_norm_2(x, g):
    xf = x.astype(jnp.float32)
    y = xf * lax.rsqrt(jnp.mean(xf * xf, axis=-1, keepdims=True) + EPS)
    return (y * g).astype(x.dtype)

def modulate_2(h, shift, scale):
    return h * (1 + scale[:, None]) + shift[:, None]

def _flip(*arrs):
    return tuple(a[:, ::-1] for a in arrs)

def _chunks(a):
    b, t = a.shape[:2]
    return jnp.moveaxis(a.reshape(b, t // CHUNK, CHUNK, *a.shape[2:]), 1, 0)

def _unchunk(a):
    a = jnp.moveaxis(a, 0, 1)
    return a.reshape(a.shape[0], a.shape[1] * a.shape[2], *a.shape[3:])

def _grid_dwconv(u, w, grid_hw):
    b, t, ch = u.shape
    img = u.reshape(b, grid_hw[0], grid_hw[1], ch)
    out = lax.conv_general_dilated(img, w[:, :, None, :].astype(u.dtype), (1, 1), "SAME",
                                   dimension_numbers=("NHWC", "HWIO", "NHWC"),
                                   feature_group_count=ch)
    return out.reshape(b, t, ch)

def _gla_scan(q, k, v, g, s0):
    mask = jnp.tril(jnp.ones((CHUNK, CHUNK), bool))

    def step(s, inp):
        qc, kc, vc, gc = inp
        cum = jnp.cumsum(gc.astype(jnp.float32), axis=1)
        inter = jnp.einsum("blhk,bhkv->blhv", qc * jnp.exp(cum), s)
        diff = cum[:, :, None] - cum[:, None, :]
        decay = jnp.exp(jnp.where(mask[None, :, :, None, None], diff, -jnp.inf))
        att = jnp.einsum("bihk,bjhk,bijhk->bhij", qc, kc, decay)
        intra = jnp.einsum("bhij,bjhv->bihv", att, vc)
        tot = cum[:, -1]
        s_new = s * jnp.exp(tot)[..., None] + jnp.einsum(
            "blhk,blhv->bhkv", kc * jnp.exp(tot[:, None] - cum), vc)
        return s_new, inter + intra

    s_fin, out = lax.scan(step, s0, (_chunks(q), _chunks(k), _chunks(v), _chunks(g)))
    return _unchunk(out), s_fin

def _ssd_scan(xs, dt, a, bm, cm, s0):
    mask = jnp.tril(jnp.ones((CHUNK, CHUNK), bool))

    def step(s, inp):
        xc, dtc, ac, bc, cc = inp
        cum = jnp.cumsum(ac.astype(jnp.float32), axis=1)
        seg = cum[:, :, None] - cum[:, None, :]
        lmat = jnp.exp(jnp.where(mask[None, :, :, None], seg, -jnp.inf))
        scores = jnp.einsum("bihn,bjhn,bijh->bhij", cc, bc, lmat)
        intra = jnp.einsum("bhij,bjhp->bihp", scores, xc * dtc[..., None])
        inter = jnp.einsum("bihn,bhpn->bihp", cc, s) * jnp.exp(cum)[..., None]
        tot = cum[:, -1]
        w = (jnp.exp(tot[:, None] - cum) * dtc)[..., None]
        s_new = s * jnp.exp(tot)[:, :, None, None] + jnp.einsum("blhn,blhp->bhpn", bc * w, xc)
        return s_new, inter + intra

    s_fin, out = lax.scan(step, s0, (_chunks(xs), _chunks(dt), _chunks(a), _chunks(bm), _chunks(cm)))
    return _unchunk(out), s_fin

def _bidir(scan_fn, ctx_f, ctx_b, lat_f, lat_b, s0):
    yc_f, sc_f = scan_fn(*ctx_f, s0)
    yl_f, _ = scan_fn(*lat_f, sc_f)
    yc_b, sc_b = scan_fn(*_flip(*ctx_b), s0)
    yl_b, _ = scan_fn(*_flip(*lat_b), sc_b)
    return yc_f + yc_b[:, ::-1], yl_f + yl_b[:, ::-1]

def _stream_features(h, grid_hw, w_in, conv_w, conv_b, gla_wg_f, gla_bg_f, gla_wg_b, gla_bg_b,
                     a_log_f, a_log_b, dt_bias_f, dt_bias_b):
    b, t, _ = h.shape
    q, k, v, r, lr, z, xbc, dt_raw = jnp.split(h @ w_in, PROJ_SPLITS, axis=-1)
    heads = lambda arr, n: arr.reshape(b, t, n, -1)
    lr_f, lr_b = jnp.split(lr, 2, axis=-1)
    g_f = heads(jax.nn.log_sigmoid(lr_f @ gla_wg_f + gla_bg_f) / GLA_GATE_NORM, GLA_HEADS)
    g_b = heads(jax.nn.log_sigmoid(lr_b @ gla_wg_b + gla_bg_b) / GLA_GATE_NORM, GLA_HEADS)
    xbc = jax.nn.silu(_grid_dwconv(xbc, conv_w, grid_hw) + conv_b)
    xs, bm, cm = jnp.split(xbc, [SSD_INNER, SSD_INNER + SSD_GROUPS * SSD_N], axis=-1)
    rep = SSD_HEADS // SSD_GROUPS
    dt_f_raw, dt_b_raw = jnp.split(dt_raw, 2, axis=-1)
    dt_f = jax.nn.softplus(dt_f_raw + dt_bias_f)
    dt_b = jax.nn.softplus(dt_b_raw + dt_bias_b)
    return {
        "q": heads(q, GLA_HEADS) * GLA_DK ** -0.5,
        "k": heads(k, GLA_HEADS),
        "v": heads(v, GLA_HEADS),
        "r": r, "g_f": g_f, "g_b": g_b,
        "xs": heads(xs, SSD_HEADS),
        "bm": jnp.repeat(heads(bm, SSD_GROUPS), rep, axis=2),
        "cm": jnp.repeat(heads(cm, SSD_GROUPS), rep, axis=2),
        "dt_f": dt_f, "a_f": dt_f * -jnp.exp(a_log_f),
        "dt_b": dt_b, "a_b": dt_b * -jnp.exp(a_log_b),
        "z": z,
    }

def _merge_heads(f, y_gla, y_ssd, gla_norm, d_skip, ssd_norm, w_out):
    b, t = y_gla.shape[:2]
    o_gla = rms_norm_2(y_gla, gla_norm) * jax.nn.silu(f["r"]).reshape(b, t, GLA_HEADS, GLA_DV)
    y = (y_ssd + d_skip[:, None] * f["xs"]).reshape(b, t, SSD_INNER) * jax.nn.silu(f["z"])
    o_ssd = rms_norm_2(y.reshape(b, t, SSD_GROUPS, -1), ssd_norm.reshape(SSD_GROUPS, -1))
    o = jnp.concatenate([o_gla.reshape(b, t, GLA_INNER), o_ssd.reshape(b, t, SSD_INNER)], axis=-1)
    return o @ w_out

def hybrid_mixer(h_ctx, h_lat, rows, w_in, conv_w, conv_b, gla_wg_f, gla_bg_f, gla_wg_b, gla_bg_b,
                 gla_norm, a_log_f, a_log_b, dt_bias_f, dt_bias_b, d_skip, ssd_norm, w_out):
    per_stream = (w_in, conv_w, conv_b, gla_wg_f, gla_bg_f, gla_wg_b, gla_bg_b,
                  a_log_f, a_log_b, dt_bias_f, dt_bias_b)
    fc = _stream_features(h_ctx, (1, h_ctx.shape[1]), *per_stream)
    fl = _stream_features(h_lat, (rows, GRID_W), *per_stream)
    b = h_lat.shape[0]
    gla0 = jnp.zeros((b, GLA_HEADS, GLA_DK, GLA_DV), jnp.float32)
    ssd0 = jnp.zeros((b, SSD_HEADS, SSD_P, SSD_N), jnp.float32)
    gla_in = lambda f, d: (f["q"], f["k"], f["v"], f["g_" + d])
    ssd_in = lambda f, d: (f["xs"], f["dt_" + d], f["a_" + d], f["bm"], f["cm"])
    gla_c, gla_l = _bidir(_gla_scan, gla_in(fc, "f"), gla_in(fc, "b"),
                          gla_in(fl, "f"), gla_in(fl, "b"), gla0)
    ssd_c, ssd_l = _bidir(_ssd_scan, ssd_in(fc, "f"), ssd_in(fc, "b"),
                          ssd_in(fl, "f"), ssd_in(fl, "b"), ssd0)
    y_ctx = _merge_heads(fc, gla_c, ssd_c, gla_norm, d_skip, ssd_norm, w_out)
    y_lat = _merge_heads(fl, gla_l, ssd_l, gla_norm, d_skip, ssd_norm, w_out)
    return y_ctx, y_lat

def swiglu(h, w_gate, w_up, w_down):
    return (jax.nn.silu(h @ w_gate) * (h @ w_up)) @ w_down

def second_inputs(seed: int = 0) -> dict:
    key = jax.random.key(seed)
    ks = jax.random.split(key, 28)
    f32 = jnp.float32
    nrm = lambda k, shape, scale: jax.random.normal(k, shape, f32) * scale
    gain = lambda k, shape: 1.0 + 0.1 * jax.random.normal(k, shape, f32)

    def dt_bias(k):
        dt = jnp.exp(jax.random.uniform(k, (DEPTH_2, SSD_HEADS), f32, math.log(1e-3), math.log(1e-1)))
        return dt + jnp.log(-jnp.expm1(-dt))

    def a_log(k):
        return jnp.log(jax.random.uniform(k, (DEPTH_2, SSD_HEADS), f32, 1.0, 16.0))

    return {
        "x": nrm(ks[0], (BATCH, SEQ, D_MODEL), 1.0),
        "c": nrm(ks[1], (BATCH, D_MODEL), 1.0),
        "ctx": nrm(ks[2], (BATCH, CTX_LEN, D_MODEL), 1.0),
        "c_ctx": nrm(ks[3], (D_MODEL,), 0.5),
        "w_mod": nrm(ks[4], (DEPTH_2, D_MODEL, 6 * D_MODEL), D_MODEL ** -0.5),
        "b_mod": nrm(ks[5], (DEPTH_2, 6 * D_MODEL), 0.02),
        "norm_mix_pre": gain(ks[6], (DEPTH_2, D_MODEL)),
        "norm_mix_post": gain(ks[7], (DEPTH_2, D_MODEL)),
        "norm_ffn_pre": gain(ks[8], (DEPTH_2, D_MODEL)),
        "norm_ffn_post": gain(ks[9], (DEPTH_2, D_MODEL)),
        "w_in": nrm(ks[10], (DEPTH_2, D_MODEL, D_IN_PROJ), D_MODEL ** -0.5),
        "conv_w": nrm(ks[11], (DEPTH_2, CONV_K, CONV_K, SSD_CONV_DIM), (CONV_K * CONV_K) ** -0.5),
        "conv_b": nrm(ks[12], (DEPTH_2, SSD_CONV_DIM), 0.02),
        "gla_wg_f": nrm(ks[13], (DEPTH_2, GLA_RANK, GLA_HEADS * GLA_DK), GLA_RANK ** -0.5),
        "gla_bg_f": nrm(ks[14], (DEPTH_2, GLA_HEADS * GLA_DK), 0.1),
        "gla_wg_b": nrm(ks[15], (DEPTH_2, GLA_RANK, GLA_HEADS * GLA_DK), GLA_RANK ** -0.5),
        "gla_bg_b": nrm(ks[16], (DEPTH_2, GLA_HEADS * GLA_DK), 0.1),
        "gla_norm": gain(ks[17], (DEPTH_2, GLA_DV)),
        "a_log_f": a_log(ks[18]),
        "a_log_b": a_log(ks[19]),
        "dt_bias_f": dt_bias(ks[20]),
        "dt_bias_b": dt_bias(ks[21]),
        "d_skip": gain(ks[22], (DEPTH_2, SSD_HEADS)),
        "ssd_norm": gain(ks[23], (DEPTH_2, SSD_INNER)),
        "w_out": nrm(ks[24], (DEPTH_2, D_MIX, D_MODEL), D_MIX ** -0.5),
        "w_gate": nrm(ks[25], (DEPTH_2, D_MODEL, D_FF), D_MODEL ** -0.5),
        "w_up": nrm(ks[26], (DEPTH_2, D_MODEL, D_FF), D_MODEL ** -0.5),
        "w_down": nrm(ks[27], (DEPTH_2, D_FF, D_MODEL), D_FF ** -0.5),
    }

def second_block(x, c, ctx, c_ctx, w_mod, b_mod, norm_mix_pre, norm_mix_post, norm_ffn_pre, norm_ffn_post,
              w_in, conv_w, conv_b, gla_wg_f, gla_bg_f, gla_wg_b, gla_bg_b, gla_norm,
              a_log_f, a_log_b, dt_bias_f, dt_bias_b, d_skip, ssd_norm, w_out, w_gate, w_up, w_down):
    rows = x.shape[1] // GRID_W
    x_lat, x_ctx = x, ctx
    for layer in range(DEPTH_2):
        m_lat = jnp.split(jax.nn.silu(c) @ w_mod[layer] + b_mod[layer], 6, axis=-1)
        m_ctx = jnp.split(jax.nn.silu(c_ctx)[None] @ w_mod[layer] + b_mod[layer], 6, axis=-1)

        h_lat = modulate_2(rms_norm_2(x_lat, norm_mix_pre[layer]), m_lat[0], m_lat[1])
        h_ctx = modulate_2(rms_norm_2(x_ctx, norm_mix_pre[layer]), m_ctx[0], m_ctx[1])
        y_ctx, y_lat = hybrid_mixer(
            h_ctx, h_lat, rows, w_in[layer], conv_w[layer], conv_b[layer],
            gla_wg_f[layer], gla_bg_f[layer], gla_wg_b[layer], gla_bg_b[layer], gla_norm[layer],
            a_log_f[layer], a_log_b[layer], dt_bias_f[layer], dt_bias_b[layer],
            d_skip[layer], ssd_norm[layer], w_out[layer])

        x_lat = x_lat + m_lat[2][:, None] * rms_norm_2(y_lat, norm_mix_post[layer])
        f_lat = swiglu(modulate_2(rms_norm_2(x_lat, norm_ffn_pre[layer]), m_lat[3], m_lat[4]),
                       w_gate[layer], w_up[layer], w_down[layer])
        x_lat = x_lat + m_lat[5][:, None] * rms_norm_2(f_lat, norm_ffn_post[layer])

        if layer + 1 < DEPTH_2:
            x_ctx = x_ctx + m_ctx[2][:, None] * rms_norm_2(y_ctx, norm_mix_post[layer])
            f_ctx = swiglu(modulate_2(rms_norm_2(x_ctx, norm_ffn_pre[layer]), m_ctx[3], m_ctx[4]),
                           w_gate[layer], w_up[layer], w_down[layer])
            x_ctx = x_ctx + m_ctx[5][:, None] * rms_norm_2(f_ctx, norm_ffn_post[layer])
    return x_lat


def setup_inputs(seed=0):
    out = dict(first_inputs(seed))
    for name, value in second_inputs(seed + 1).items():
        if name != "x":
            out[name + "_2"] = value
    return out


def reference(
    x, c, ctx, c_ctx, w_ada, b_ada, norm1_g, w_in, q_norm_g, k_norm_g, sink, w_br_fourier,
    w_br_global, w_br_window, w_out, norm2_g, w_router, w_gate_e, w_up_e, w_down_e, final_g,
    c_2, ctx_2, c_ctx_2, w_mod_2, b_mod_2, norm_mix_pre_2, norm_mix_post_2, norm_ffn_pre_2,
    norm_ffn_post_2, w_in_2, conv_w_2, conv_b_2, gla_wg_f_2, gla_bg_f_2, gla_wg_b_2, gla_bg_b_2,
    gla_norm_2, a_log_f_2, a_log_b_2, dt_bias_f_2, dt_bias_b_2, d_skip_2, ssd_norm_2, w_out_2,
    w_gate_2, w_up_2, w_down_2,
):
    x = first_block(
        x, c, ctx, c_ctx, w_ada, b_ada, norm1_g, w_in, q_norm_g, k_norm_g, sink, w_br_fourier,
        w_br_global, w_br_window, w_out, norm2_g, w_router, w_gate_e, w_up_e, w_down_e, final_g,
    )
    return second_block(
        x, c_2, ctx_2, c_ctx_2, w_mod_2, b_mod_2, norm_mix_pre_2, norm_mix_post_2,
        norm_ffn_pre_2, norm_ffn_post_2, w_in_2, conv_w_2, conv_b_2, gla_wg_f_2, gla_bg_f_2,
        gla_wg_b_2, gla_bg_b_2, gla_norm_2, a_log_f_2, a_log_b_2, dt_bias_f_2, dt_bias_b_2,
        d_skip_2, ssd_norm_2, w_out_2, w_gate_2, w_up_2, w_down_2,
    )


_drawn_inputs = setup_inputs


def setup_inputs(seed=0):
    import zlib

    import numpy as np

    out = dict(_drawn_inputs(seed))
    spreads = {}
    factors = {'b_ada': 3.889,
     'norm1_g': 3.868,
     'q_norm_g': 8.0,
     'k_norm_g': 8.0,
     'sink': 8.0,
     'norm2_g': 2.735,
     'conv_b_2': 5.67,
     'gla_bg_f_2': 4.813,
     'gla_bg_b_2': 4.282,
     'd_skip_2': 4.48}
    for name, (base, spread) in spreads.items():
        noise = np.random.default_rng([zlib.crc32(name.encode()), seed]).standard_normal(out[name].shape)
        drawn = base * np.exp(spread * noise) if base else spread * noise
        out[name] = __import__('jax').numpy.asarray(drawn.astype(out[name].dtype))
    for name, factor in factors.items():
        out[name] = (out[name] * factor).astype(out[name].dtype)
    return out
```

```python
from contextlib import ExitStack

import numpy as np

import concourse.bass as bass
from concourse import mybir

F32 = mybir.dt.float32
ACT = mybir.ActivationFunctionType
ALU = mybir.AluOpType
AX = mybir.AxisListType.X

P = 128
D = 1024
KD = D // P
SEQ = 256
TILES = 4
DEPTH = 2
E = 16
CAP = 2 * SEQ // E
HD = 64
EPS = 1e-6
RING = 4
POOL = 4
SLOT = KD * 512
SCALE = HD ** -0.5

Z_W = 1536
GQ, GK, GV, WQ, WK, WV = 256, 768, 896, 1024, 1280, 1408
B_Q, B_K, B_V, B_R, B_LR, B_Z, B_X, B_DT, B_END = 0, 256, 512, 1024, 1536, 1568, 2080, 2848, 2864
D_FF = 2816
FB = D_FF // P


CONST = {}


def constants():
    parts, at = [], 0

    def put(name, a):
        nonlocal at
        a = np.asarray(a, np.float64).reshape(a.shape[0], -1)
        full = np.zeros((P, a.shape[1]))
        full[: a.shape[0]] = a
        CONST[name] = (at, a.shape[1])
        at += a.shape[1]
        parts.append(full)

    put("ident", np.eye(P))
    n = np.arange(SEQ)
    ang = 2 * np.pi * ((n[:, None] * n[None]) % SEQ) / SEQ
    norm = 1 / np.sqrt(SEQ * HD)
    cs = np.concatenate([np.cos(ang), np.sin(ang)], 1) * norm
    put("dft_pos", cs.reshape(2, P, 512).transpose(1, 0, 2))
    c = np.arange(HD)
    ang = 2 * np.pi * ((c[:, None] * c[None]) % HD) / HD
    put("dft_cos", np.kron(np.eye(2), np.cos(ang)))
    put("dft_nsin", -np.kron(np.eye(2), np.sin(ang)))
    mask = np.zeros((2, P, 512))
    q, k = np.arange(SEQ)[:, None], np.arange(SEQ)[None]
    mask[:, :, :SEQ] = np.where(abs(q - k) <= 128, 0, -1e30 / SCALE).reshape(2, P, SEQ)
    put("band", mask.transpose(1, 0, 2))
    t = np.arange(SEQ)
    inv = np.float32(10000.0) ** (-np.arange(0, 32, 2, dtype=np.float32) / np.float32(32))
    ang = np.concatenate([(t // 64).astype(np.float32)[:, None] * inv, (t % 64).astype(np.float32)[:, None] * inv], 1)
    put("rope_cos", np.cos(ang).reshape(2, P, 32).transpose(1, 0, 2))
    put("rope_sin", np.sin(ang).reshape(2, P, 32).transpose(1, 0, 2))
    put("iota", np.tile(np.arange(CAP), (P, 1)))
    j, i = np.arange(P)[:, None], np.arange(P)[None]
    put("after", j <= i)
    put("before", j >= i)
    put("twice", 2.0 * np.eye(P))
    lev = []
    for l in range(1, 8):
        half = 1 << (l - 1)
        lev.append(((j >> l) == (i >> l)) & (((j // half) & 1) != ((i // half) & 1)))
    put("levels", np.stack(lev, 1))
    return np.concatenate(parts, 1).astype(np.float32)


class Tally:

    def __init__(self):
        self.n, self.per, self.i = {}, None, None

    def step(self, name, k=1):
        self.n[name] = self.n.get(name, 0) + k
        return self.value(name)

    def value(self, name, less=0):
        v = self.n.get(name, 0) - less
        return v if self.per is None else v + self.i * self.per[name]

    def enter(self, i, per):
        self.i, self.per, self.start = i, per, dict(self.n)

    def leave(self, turns):
        for name, k in self.per.items():
            got = self.n.get(name, 0) - self.start.get(name, 0)
            assert got == k, (name, got, k)
            self.n[name] = self.start.get(name, 0) + k * turns
        self.per = None


def stream_of(t):
    return t // 2


def build(nc: bass.Bass, A, out):
    with ExitStack() as ctx:
        def sb(name, *shape):
            return ctx.enter_context(nc.sbuf_tensor(name, [P, *shape], F32))

        class Sems:
            def __init__(self):
                self.made = {}

            def __call__(self, name):
                if name not in self.made:
                    self.made[name] = ctx.enter_context(nc.semaphore(name))
                return self.made[name]

        S = Sems()

        X = sb("x_tokens", TILES, D)
        ring = sb("weight_ring", RING, SLOT)
        const = sb("const", sum(n for _, n in CONST.values()))
        gate_rows = sb("gate_rows", 2, D)
        arena = sb("arena", 23552)
        vec_in = sb("vec_in", 4, P)
        vecs = sb("vecs", 4, P)
        silu_c = sb("silu_c", 3, KD, 2)
        mod_cols = sb("mod_cols", 2, 2, KD, 2)
        w_router = sb("w_router", 2, KD, E)
        qk_gain = sb("qk_gain", 2, 2, HD)
        sinks = sb("sinks", 2, 4)
        small = sb("small", 256)
        banks = [ctx.enter_context(nc.psum_tensor(f"bank{i}", [P, 512], F32)) for i in range(2 * POOL)]
        pool_banks = {"D": banks[:POOL], "A": banks[POOL:]}

        def bank_of(pool, n):
            return pool_banks[pool][(n - 1) % POOL]

        def C(name, *dims):
            at, n = CONST[name]
            v = const[:, at:at + n]
            if len(dims) == 2:
                v = v.rearrange("p (a b) -> p a b", a=dims[0])
            return v

        def area(at, *dims):
            n = int(np.prod(dims))
            v = arena[:, at:at + n]
            if len(dims) == 2:
                v = v.rearrange("p (a b) -> p a b", a=dims[0])
            if len(dims) == 3:
                v = v.rearrange("p (a b c) -> p a b c", a=dims[0], b=dims[1])
            return v

        ident = C("ident")
        zero = small[:, 0:1]
        flag, flag_a = small[:, 2:3], small[:, 3:4]
        ones = small[:, 1:2]
        ss, inv, rstd = small[:, 4:8], small[:, 8:12], small[:, 12:16]

        hT = area(0, KD, 512)
        xn = area(4096, TILES, D)
        Z = area(4096, TILES, Z_W)
        qT = area(10240, 12, SEQ)
        kT = area(13312, 4, 512)
        probs = area(15360, 4, 512)
        probsT = area(17408, 4, 512)
        oT = area(19456, 6, 512)
        fT = area(22528, 2, 512)
        head_sq = area(15360, 640)
        rope_tmp = area(17408, 4, 320)
        four = area(15360, 2, 512)
        m_sum = area(4096, TILES, D)
        mT = area(0, KD, 512)
        sig = area(15360, 4, 512)
        prod = area(10240, 4, 512)
        gate_b = area(17408, 2, D)
        head_ss = small[:, 16:26]
        head_inv = small[:, 26:36]
        head_rstd = small[:, 36:46]
        row_max, row_neg, row_sum, sink_e, row_inv = (small[:, 48 + 4 * i:52 + 4 * i] for i in range(5))
        xn2 = area(0, TILES, D)
        h2T = area(4096, KD, 512)
        xgT = area(4096, KD, E, 64)
        pick = area(12288, TILES, 512)
        pick_g = area(14336, TILES, 512)
        putT = area(16384, TILES, 4, P)
        gate2_b = area(18432, 2, D)
        hidT = area(20480, KD, 64)
        affT, work, cum = area(20992, 512), area(21504, 512), area(22016, 512)
        aff = area(22528, TILES, E)
        slot_t = area(22592, TILES, E)
        logit = area(22656, TILES, E)
        best = area(22720, 8)
        aff_m, aff_s, aff_i = area(22736, 4), area(22740, 4), area(22744, 4)
        scat = area(23040, 512)
        out_g = area(0, 2, D)
        silu_g = area(2048, 2, 512)
        hid = area(3072, D)
        xgs = area(12288, KD, 4, 64)
        puts = area(14336, TILES, P)
        row_tmp = area(0, 2, D)

        def rows(ap):
            return ap.rearrange("(k p) -> k p", p=P)

        vec_loads = []
        for l in range(DEPTH):
            for at, ap in ((0, A["norm1_g"][l]), (8, A["norm2_g"][l]), (16, A["c"][0]), (24, A["c_ctx"]), (32, A["b_ada"][l])):
                n = ap.shape[0] // P
                vec_loads.append((vec_in[at:at + n, l, :], rows(ap)))
        for at, ap in ((0, A["norm_mix_pre_2"][0]), (8, A["norm_ffn_pre_2"][0]), (16, A["c_2"][0]), (24, A["c_ctx_2"]),
                       (32, A["b_mod_2"][0]), (80, A["conv_b_2"][0]), (86, A["gla_bg_f_2"][0]), (88, A["gla_bg_b_2"][0])):
            vec_loads.append((vec_in[at:at + ap.shape[0] // P, 2, :], rows(ap)))
        vec_loads.append((vec_in[0:54, 3, :], A["conv_w_2"][0].rearrange("y x (k p) -> (y x k) p", p=P)))
        VEC_ROWS = (80, 80, 90, 54)
        small_loads = []
        for l in range(DEPTH):
            small_loads.append((w_router[:, l, :, :], A["w_router"][l].rearrange("(k p) e -> p k e", p=P)))
            small_loads.append((qk_gain[:, l, 0, :], A["q_norm_g"][l].partition_broadcast(P)))
            small_loads.append((qk_gain[:, l, 1, :], A["k_norm_g"][l].partition_broadcast(P)))
            small_loads.append((sinks[:, l, :], A["sink"][l].partition_broadcast(P)))
        N_VEC, N_SMALL = len(vec_loads), len(small_loads)

        block = ctx.enter_context(nc.Block())
        released = []
        expert_start = {}

        def big(w, c0, c1):
            return w[:, c0:c1].rearrange("(k p) n -> p k n", p=P)

        def slot_view(r, width=512):
            return ring[:, r, :].rearrange("p (k n) -> p k n", n=width)

        LAYERS = [
            dict(w_mod=A["w_ada"][0], b_mod=A["b_ada"], row=0),
            dict(w_mod=A["w_ada"][1], b_mod=A["b_ada"], row=1),
            dict(w_mod=A["w_mod_2"][0], b_mod=A["b_mod_2"], row=0),
        ]

        V2 = area(4096, TILES, 512)
        silu_r = area(6144, 2, 512)
        silu_z = area(7168, 2, 512)
        final_gain = area(8192, D)
        qc = area(8192, 2, SEQ)
        kc = area(8704, 2, 512)
        x_raw = area(9728, 6, 512)
        lr_rows = area(12800, 512)
        dt_raw = area(13312, 512)
        gates = area(13824, 4, 512)
        gate_tmp = area(15872, 4, 512)
        xbc = area(17920, 6, 512)
        cum_g = area(20992, 8, 257)
        cum_s = area(0, 514)
        dt_rows = area(520, 512)
        decays = area(1032, 4, SEQ)
        cols = area(2056, 224)
        BT = area(2928, 2, P)
        seg = area(3184, 768)
        a_rows = area(3184, 512)
        lev_tmp = area(3184, 512)
        XS = area(9728, TILES, 512)
        att8 = area(11776, 2, 512)
        att = area(12800, 2, 512)
        lev = area(13824, 2, 1024)
        KDt = area(13824, 2, 512)
        QD = area(15872, 4, SEQ)
        KD_rows = area(16896, 4, SEQ)
        SG = area(17920, 4, 256)
        BC = area(18944, 2, 512)
        XW = area(13824, 4, 512)
        SS = area(20992, 2, 256)
        W = area(21504, 2, 512)
        intra = area(15872, 2, 512)
        O = X[:, 2:4, :]
        oT2 = area(0, KD, SEQ)
        Y = area(4096, 2, D)
        gain_b = area(9216, D)
        gate3_b = area(8192, 1, D)
        xn3 = area(10240, 2, D)
        h3T = area(12288, KD, SEQ)
        ffT = area(14336, FB, SEQ)
        ff_silu = area(19968, 2, SEQ)
        rows2 = sb("gla_ssd_gains", 648)
        gla_gain, ssd_gain, skip_gain = rows2[:, 0:128], rows2[:, 128:640], rows2[:, 640:648]
        wg = vec_in.rearrange("p (d h) n -> p d (h n)", d=2)
        dt_bias, neg_a = small[0:16, 100:101], small[0:16, 101:102]

        def load_block2(sp, load, load_cols, load_modulation, T):
            due = T.step
            load_modulation(2)
            w = A["w_in_2"][0]
            for c0 in (B_Q, B_V, B_R, B_Z, B_X):
                load_cols(w, c0, c0 + 512)
            load((lambda r: slot_view(r)[:, :, 0:272], big(w, B_X + 512, B_END)),
                 (lambda r: slot_view(r)[:, :, 272:304], big(w, B_LR, B_Z)))
            for n in range(2):
                load_cols(A["w_out_2"][0], 512 * n, 512 * n + 512)
            for c0 in range(0, D_FF, 512):
                for name in ("w_gate_2", "w_up_2"):
                    load_cols(A[name][0], c0, min(c0 + 512, D_FF))
            for n in range(2):
                for k0 in range(0, FB, KD):
                    k1 = min(k0 + KD, FB)
                    src = A["w_down_2"][0][k0 * P:k1 * P, n * 512:n * 512 + 512].rearrange("(k p) n -> p k n", p=P)
                    load((lambda r, kk=k1 - k0: slot_view(r)[:, 0:kk, :], src))

        def pe_block2(pe, T, next_slot, release, turn, modulation, turn_streams, dense, broadcast_gate):
            due = T.step
            modulation(2)
            pe.wait_ge(S("xn_ready"), due("xn_ready", 2 + TILES))
            turn_streams(xn, range(TILES))
            pe.wait_ge(S("hT_ready_dve"), due("hT_ready_dve", 4))
            pe.wait_ge(S("hT_ready_act"), due("hT_ready_act", 4))

            def rows_of(pool, r, c0, m, n):
                pe.wait_ge(S("free" + pool), due("free" + pool))
                b = bank_of(pool, T.n["free" + pool])
                for k in range(KD):
                    mm = pe.matmul(b[0:m, 0:n], slot_view(r)[:, k, c0:c0 + m], hT[:, k, 0:n], start=(k == 0), stop=(k == KD - 1))
                mm.then_inc(S("full" + pool), 1)

            r = next_slot()
            pe.wait_ge(S(f"slot_landed{r}"), due(f"slot_landed{r}", 16))
            for blk in range(4):
                rows_of("D" if blk < 2 else "A", r, blk * P, P, SEQ if blk < 2 else 512)
            release("A")
            r = next_slot()
            pe.wait_ge(S(f"slot_landed{r}"), due(f"slot_landed{r}", 16))
            for t in range(TILES):
                dense("DA"[t % 2], t, r, hT)
            release("A")
            for _ in range(2):
                r = next_slot()
                pe.wait_ge(S(f"slot_landed{r}"), due(f"slot_landed{r}", 16))
                for t in range(2):
                    dense("A", t, r, hT)
                release("A")
            r = next_slot()
            pe.wait_ge(S(f"slot_landed{r}"), due(f"slot_landed{r}", 16))
            for blk in range(4):
                rows_of("DA"[blk % 2], r, blk * P, P, 512)
            release("A")
            r = next_slot()
            pe.wait_ge(S(f"slot_landed{r}"), due(f"slot_landed{r}", 2 * 16))
            for blk in range(2):
                rows_of("DA"[blk % 2], r, blk * P, P, 512)
            rows_of("D", r, 256, 16, 512)
            rows_of("D", r, 272, 32, 512)
            release("D")
            pe.wait_ge(S("lr_ready"), due("lr_ready"))
            pe.wait_ge(S("wg_landed"), due("wg_landed", 32))
            for d in range(2):
                for blk in range(2):
                    pe.wait_ge(S("freeD"), due("freeD"))
                    b = bank_of("D", T.n["freeD"])
                    pe.matmul(b[:, :], wg[0:32, d, blk * P:blk * P + P], lr_rows[0:32, :], start=True, stop=True)\
                        .then_inc(S("fullD"), 1)
            pe.wait_ge(S("xbc_ready"), due("xbc_ready"))
            for t in range(TILES):
                pe.wait_ge(S("freeA"), due("freeA"))
                b = bank_of("A", T.n["freeA"])
                for blk in range(4):
                    mm = turn(b[:, blk * P:blk * P + P], xbc[:, blk, t * P:t * P + P])
                    if blk == 3:
                        mm.then_inc(S("fullA"), 1)
            pe.wait_ge(S("freeA"), due("freeA"))
            b = bank_of("A", T.n["freeA"])
            for c in range(2):
                mm = turn(b[:, c * P:c * P + P], xbc[:, 4, (2 + c) * P:(3 + c) * P])
                if c:
                    mm.then_inc(S("fullA"), 1)
            pe.wait_ge(S("ssd_rows_ready"), due("ssd_rows_ready"))
            pe.wait_ge(S("freeD"), due("freeD"))
            b = bank_of("D", T.n["freeD"])
            for t in range(2):
                for n, src in enumerate((dt_rows[:, t * P:t * P + P], cum_s[:, 1 + t * P:1 + t * P + P], cum_s[:, t * P:t * P + P],
                                         decays[:, 0, t * P:t * P + P], decays[:, 1, t * P:t * P + P])):
                    turn(b[:, t * 80 + 16 * n:t * 80 + 16 * n + 16], src[0:16, :])
            for c in range(2):
                for n in range(2):
                    mm = turn(b[:, 160 + 32 * c + 16 * n:176 + 32 * c + 16 * n], decays[0:16, 2 + n, c * P:c * P + P])
                    if c and n:
                        mm.then_inc(S("fullD"), 1)
            for g in range(2):
                pe.wait_ge(S("freeD"), due("freeD"))
                b = bank_of("D", T.n["freeD"])
                for j in range(2):
                    mm = pe.matmul(b[:, j * SEQ:j * SEQ + SEQ], xbc[64 * g:64 * g + 64, 4, j * P:j * P + P],
                                   xbc[64 * g:64 * g + 64, 5, 0:SEQ], start=True, stop=True)
                mm.then_inc(S("fullD"), 1)
            pe.wait_ge(S("qd_kd_ready"), due("qd_kd_ready"))
            for d in range(2):
                pe.wait_ge(S("freeA"), due("freeA"))
                b = bank_of("A", T.n["freeA"])
                for c in range(2):
                    for blk in range(2):
                        mm = turn(b[:, (2 * c + blk) * P:(2 * c + blk + 1) * P], KD_rows[:, 2 * d + blk, c * P:c * P + P])
                        if c and blk:
                            mm.then_inc(S("fullA"), 1)
            pe.wait_ge(S("kdt_ready"), due("kdt_ready"))
            for d in range(2):
                pe.wait_ge(S("freeD"), due("freeD"))
                b = bank_of("D", T.n["freeD"])
                for blk in range(2):
                    for c in range(2):
                        mm = pe.matmul(b[:, blk * 256:blk * 256 + 256], KDt[:, d, (2 * c + blk) * P:(2 * c + blk + 1) * P],
                                       V2[:, 2 + c, blk * 256:blk * 256 + 256], start=(c == 0), stop=(c == 1))
                mm.then_inc(S("fullD"), 1)
            def level(keys, queries, cross):
                for par in range(2):
                    rows_ = slice(64 * par, 64 * par + 64)
                    pe.wait_ge(S("freeD"), due("freeD"))
                    b = bank_of("D", T.n["freeD"])
                    for t in range(2):
                        for blk in range(2):
                            at = (2 * t + blk) * P
                            i = 1 - t if cross else t
                            mm = pe.matmul(b[:, at:at + P], keys[rows_, blk, t * P:t * P + P], queries[rows_, blk, i * P:i * P + P],
                                           start=True, stop=True)
                    mm.then_inc(S("fullD"), 1)

            level(kc, qc, False)
            for l in range(1, 9):
                pe.wait_ge(S("level_ready"), due("level_ready"))
                v = lev[:, l % 2, :].rearrange("p (w b i) -> p w b i", w=2, b=2)
                level(v[:, 1], v[:, 0], l == 8)
            pe.wait_ge(S("states_ready"), due("states_ready"))
            pe.wait_ge(S("att_ready"), due("att_ready"))
            for t in range(2):
                pe.wait_ge(S("freeD"), due("freeD"))
                b = bank_of("D", T.n["freeD"])
                for blk in range(2):
                    for d in range(2):
                        pe.matmul(b[:, blk * 256:blk * 256 + 256], QD[:, 2 * d + blk, t * P:t * P + P], SG[:, 2 * d + blk, :],
                                  start=(d == 0), stop=False)
                    for par in range(2):
                        h = 2 * blk + par
                        pe.matmul(b[:, h * P:h * P + P], att[:, par, (2 * t + blk) * P:(2 * t + blk + 1) * P],
                                  V2[:, t, h * P:h * P + P], start=False, stop=False)
                        mm = pe.matmul(b[:, h * P:h * P + P], att8[:, par, (2 * (1 - t) + blk) * P:(2 * (1 - t) + blk + 1) * P],
                                       V2[:, 1 - t, h * P:h * P + P], start=False, stop=(par == 1))
                mm.then_inc(S("fullD"), 1)
            pe.wait_ge(S("xw_ready"), due("xw_ready"))
            pe.wait_ge(S("freeD"), due("freeD"))
            b = bank_of("D", T.n["freeD"])
            for g in range(2):
                for d in range(2):
                    for c in range(2):
                        mm = pe.matmul(b[64 * g:64 * g + 64, d * 256:d * 256 + 256], BT[:, c, 64 * g:64 * g + 64],
                                       XW[:, 2 * c + d, g * 256:g * 256 + 256], start=(c == 0), stop=(c == 1))
            mm.then_inc(S("fullD"), 1)
            pe.wait_ge(S("ss_ready"), due("ss_ready"))
            for t in range(2):
                for g in range(2):
                    pe.wait_ge(S("freeD"), due("freeD"))
                    b = bank_of("D", T.n["freeD"])
                    for d in range(2):
                        mm = pe.matmul(b[:, d * 256:d * 256 + 256], xbc[64 * g:64 * g + 64, 5, t * P:t * P + P],
                                       SS[64 * g:64 * g + 64, d, :], start=True, stop=True)
                    mm.then_inc(S("fullD"), 1)

            def row_out(h):
                for row in (h, 8 + h):
                    pe.wait_ge(S("freeD"), due("freeD"))
                    b = bank_of("D", T.n["freeD"])
                    pe.matmul(b[:, 0:258], ident[0:16, row:row + 1].to_broadcast([16, P]), cum_s[0:16, 0:258],
                              start=True, stop=True).then_inc(S("fullD"), 1)

            row_out(0)
            for h in range(8):
                if h < 7:
                    row_out(h + 1)
                pe.wait_ge(S("w_ready"), due("w_ready"))
                pe.wait_ge(S("freeA"), due("freeA"))
                b = bank_of("A", T.n["freeA"])
                for t in range(2):
                    for j in range(2):
                        mm = pe.matmul(b[:, t * HD:t * HD + HD], W[:, h % 2, j * SEQ + t * P:j * SEQ + t * P + P],
                                       XS[:, j, h * HD:h * HD + HD], start=(j == 0), stop=(j == 1))
                mm.then_inc(S("fullA"), 1)
            broadcast_gate(0, 1)
            pe.wait_ge(S("o_ready"), due("o_ready"))
            turn_streams(O, range(2))
            pe.wait_ge(S("oT2_ready_dve"), due("oT2_ready_dve", 4))
            pe.wait_ge(S("oT2_ready_act"), due("oT2_ready_act", 4))
            for n in range(2):
                r = next_slot()
                pe.wait_ge(S(f"slot_landed{r}"), due(f"slot_landed{r}", 16))
                for t in range(2):
                    dense("D", t, r, oT2)
                release("D")
            broadcast_gate(1, 1)
            pe.wait_ge(S("xn_ready"), due("xn_ready", 2))
            turn_streams(xn3, range(2))
            pe.wait_ge(S("hT_ready_dve"), due("hT_ready_dve", 4))
            pe.wait_ge(S("hT_ready_act"), due("hT_ready_act", 4))
            for c0 in range(0, D_FF, 512):
                rg = next_slot()
                pe.wait_ge(S(f"slot_landed{rg}"), due(f"slot_landed{rg}", 16))
                ru = next_slot()
                pe.wait_ge(S(f"slot_landed{ru}"), due(f"slot_landed{ru}", 16))
                for blk in range(min(4, (D_FF - c0) // P)):
                    pe.wait_ge(S("freeD"), due("freeD"))
                    b = bank_of("D", T.n["freeD"])
                    for n, r in enumerate((rg, ru)):
                        for k in range(KD):
                            mm = pe.matmul(b[:, n * SEQ:n * SEQ + SEQ], slot_view(r)[:, k, blk * P:blk * P + P], h3T[:, k, :],
                                           start=(k == 0), stop=(k == KD - 1))
                    mm.then_inc(S("fullD"), 1)
                    if c0 == 0 and blk == 0:
                        ff_first.append(T.n["freeD"])
                release("D", 2)
            pe.wait_ge(S("ffT_ready"), due("ffT_ready", FB))
            for n in range(2):
                pe.wait_ge(S("freeD"), due("freeD"))
                b0 = bank_of("D", T.n["freeD"])
                pe.wait_ge(S("freeD"), due("freeD"))
                b1 = bank_of("D", T.n["freeD"])
                bs = (b0, b1)
                for k0 in range(0, FB, KD):
                    r = next_slot()
                    pe.wait_ge(S(f"slot_landed{r}"), due(f"slot_landed{r}", 16))
                    for t in range(2):
                        for k in range(k0, min(k0 + KD, FB)):
                            mm = pe.matmul(bs[t][:, :], ffT[:, k, t * P:t * P + P], slot_view(r)[:, k - k0, :],
                                           start=(k == 0), stop=(k == FB - 1))
                            if k == FB - 1:
                                mm.then_inc(S("fullD"), 1)
                    pieces = 1
                    if k0 + KD >= FB:
                        release("D", 3)

        ff_first = []

        def dve_block2(dve, T, norm, modulation, modulate, add_gated):
            due = T.step
            def bc(v, n):
                return v.unsqueeze(2).to_broadcast([P, v.shape[1], n])

            dve.memset(vec_in[:, :, :], 0.0).then_inc(S("dve_step"), 1)
            dve.wait_ge(S("dve_step"), due("dve_step"))
            dve.memset(flag, 0.0).then_inc(S("block1_done"), 1)
            dve.wait_ge(S("block1_done"), due("block1_done"))
            norm(xn, range(2))
            dve.wait_ge(S("final_gain_landed"), due("final_gain_landed", 16))
            for t in range(2):
                dve.tensor_tensor(X[:, t, :], xn[:, t, :], final_gain, ALU.mult).then_inc(S("dve_step"), 1)
                dve.wait_ge(S("dve_step"), due("dve_step"))
            modulation(2)
            dve.wait_ge(S("ctx2_landed"), due("ctx2_landed", 16))
            norm(xn, range(TILES))
            modulate(hT, 0, 2)
            for blk in range(2):
                dve.wait_ge(S("fullD"), due("fullD"))
                b = bank_of("D", T.n["fullD"])
                dve.tensor_scalar(qc[:, blk, :], b[:, 0:SEQ], SCALE, None, ALU.mult).then_inc(S("freeD"), 1)
                dve.wait_ge(S("freeD"), due("freeD"))
            for t in (0, 2):
                dve.wait_ge(S("fullD"), due("fullD"))
                b = bank_of("D", T.n["fullD"])
                dve.tensor_copy(V2[:, t, :], b[:, :]).then_inc(S("freeD"), 1)
                dve.wait_ge(S("freeD"), due("freeD"))
            for blk in (0, 2, 4):
                dve.wait_ge(S("fullD"), due("fullD"))
                b = bank_of("D", T.n["fullD"])
                dve.tensor_copy(x_raw[:, blk, :], b[:, :]).then_inc(S("freeD"), 1)
                dve.wait_ge(S("freeD"), due("freeD"))
            dve.wait_ge(S("fullD"), due("fullD"))
            b = bank_of("D", T.n["fullD"])
            dve.wait_ge(S("block2_rows_landed"), due("block2_rows_landed", 16 * N_ROWS2))
            dve.tensor_scalar(dt_raw[0:16, :], b[0:16, :], dt_bias, None, ALU.add).then_inc(S("freeD"), 1)
            dve.wait_ge(S("freeD"), due("freeD"))
            dve.wait_ge(S("fullD"), due("fullD"))
            b = bank_of("D", T.n["fullD"])
            dve.tensor_copy(lr_rows[0:32, :], b[0:32, :]).then_inc(S("freeD"), 1)
            dve.wait_ge(S("freeD"), due("freeD"))
            dve.memset(flag, 0.0).then_inc(S("lr_ready"), 1)
            dve.wait_ge(S("lr_ready"), due("lr_ready"))
            dve.memset(flag, 0.0).then_inc(S("dt_raw_ready"), 1)
            dve.wait_ge(S("dt_raw_ready"), due("dt_raw_ready"))
            for n in range(4):
                dve.wait_ge(S("fullD"), due("fullD"))
                b = bank_of("D", T.n["fullD"])
                dve.tensor_scalar(gates[:, n, :], b[:, :], vecs[:, 2, 86 + n:87 + n], None, ALU.add).then_inc(S("freeD"), 1)
                dve.wait_ge(S("freeD"), due("freeD"))
            dve.memset(flag, 0.0).then_inc(S("gates_raw_ready"), 1)
            dve.wait_ge(S("gates_raw_ready"), due("gates_raw_ready"))
            dve.wait_ge(S("x_raw_ready_act"), due("x_raw_ready_act"))
            for blk in range(6):
                def tap(y, x):
                    n = (3 * y + x) * 6 + blk
                    return vecs[:, 3, n:n + 1]

                dve.tensor_scalar(xbc[:, blk, :], x_raw[:, blk, :], tap(1, 1), None, ALU.mult).then_inc(S("dve_step"), 1)
                dve.wait_ge(S("dve_step"), due("dve_step"))
                raw = x_raw[:, blk, 0:SEQ].rearrange("p (y x) -> p y x", x=64)
                acc = xbc[:, blk, 0:SEQ].rearrange("p (y x) -> p y x", x=64)
                for y in (-1, 0, 1):
                    for x in (-1, 0, 1):
                        if not y and not x:
                            continue
                        oy, ox = slice(max(0, -y), 4 - max(0, y)), slice(max(0, -x), 64 - max(0, x))
                        iy, ix = slice(max(0, y), 4 - max(0, -y)), slice(max(0, x), 64 - max(0, -x))
                        dve.scalar_tensor_tensor(out=acc[:, oy, ox], in0=raw[:, iy, ix], scalar=tap(1 + y, 1 + x),
                                                 in1=acc[:, oy, ox], op0=ALU.mult, op1=ALU.add).then_inc(S("dve_step"), 1)
                        dve.wait_ge(S("dve_step"), due("dve_step"))
                for x in (-1, 1):
                    o0, i0 = SEQ + max(0, -x), SEQ + max(0, x)
                    dve.scalar_tensor_tensor(out=xbc[:, blk, o0:o0 + 255], in0=x_raw[:, blk, i0:i0 + 255],
                                             scalar=tap(1, 1 + x), in1=xbc[:, blk, o0:o0 + 255], op0=ALU.mult, op1=ALU.add).then_inc(S("dve_step"), 1)
                    dve.wait_ge(S("dve_step"), due("dve_step"))
                dve.memset(flag, 0.0).then_inc(S("conv_ready"), 1)
                dve.wait_ge(S("conv_ready"), due("conv_ready"))
            dve.wait_ge(S("dt_log_ready"), due("dt_log_ready"))
            dve.scalar_tensor_tensor(out=dt_rows[0:16, :], in0=dt_raw[0:16, :], scalar=0.0, in1=dt_rows[0:16, :],
                                     op0=ALU.max, op1=ALU.add).then_inc(S("dve_step"), 1)
            dve.wait_ge(S("dve_step"), due("dve_step"))
            dve.tensor_scalar(neg_a, neg_a, -1.0, None, ALU.mult).then_inc(S("dve_step"), 1)
            dve.wait_ge(S("dve_step"), due("dve_step"))
            dve.tensor_scalar(a_rows[0:16, :], dt_rows[0:16, :], neg_a, None, ALU.mult).then_inc(S("dve_step"), 1)
            dve.wait_ge(S("dve_step"), due("dve_step"))
            for s in range(2):
                c = cum_s[0:16, 257 * s:257 * s + 257]
                a = a_rows[0:16, s * SEQ:s * SEQ + SEQ]
                dve.memset(c[:, 0:1], 0.0).then_inc(S("dve_step"), 1)
                dve.wait_ge(S("dve_step"), due("dve_step"))
                dve.tensor_tensor_scan(c[:, 1:257], a, a, 0.0, ALU.add, ALU.min).then_inc(S("dve_step"), 1)
                dve.wait_ge(S("dve_step"), due("dve_step"))
            lat, cx = cum_s[0:16, 0:257], cum_s[0:16, 257:514]
            dve.tensor_copy(decays[0:16, 0, :], lat[:, 1:257]).then_inc(S("dve_step"), 1)
            dve.wait_ge(S("dve_step"), due("dve_step"))
            dve.tensor_scalar(decays[0:16, 1, :], lat[:, 0:256], lat[:, 256:257], -1.0, ALU.subtract, ALU.mult).then_inc(S("dve_step"), 1)
            dve.wait_ge(S("dve_step"), due("dve_step"))
            dve.tensor_scalar(decays[0:16, 2, :], cx[:, 1:257], cx[:, 256:257], -1.0, ALU.subtract, ALU.mult).then_inc(S("dve_step"), 1)
            dve.wait_ge(S("dve_step"), due("dve_step"))
            dve.tensor_copy(decays[0:16, 3, :], cx[:, 0:256]).then_inc(S("dve_step"), 1)
            dve.wait_ge(S("dve_step"), due("dve_step"))
            dve.memset(flag, 0.0).then_inc(S("decays_ready"), 1)
            dve.wait_ge(S("decays_ready"), due("decays_ready"))
            dve.wait_ge(S("gates_log_ready"), due("gates_log_ready"))
            dve.scalar_tensor_tensor(out=gates, in0=gates, scalar=0.0, in1=gate_tmp, op0=ALU.min, op1=ALU.subtract).then_inc(S("dve_step"), 1)
            dve.wait_ge(S("dve_step"), due("dve_step"))
            dve.tensor_scalar(gates, gates, 1.0 / 16.0, None, ALU.mult).then_inc(S("dve_step"), 1)
            dve.wait_ge(S("dve_step"), due("dve_step"))
            dve.memset(cum_g[:, :, 0:1], 0.0).then_inc(S("dve_step"), 1)
            dve.wait_ge(S("dve_step"), due("dve_step"))
            for n in range(4):
                for s in range(2):
                    g = gates[:, n, s * SEQ:s * SEQ + SEQ]
                    dve.tensor_tensor_scan(cum_g[:, 2 * n + s, 1:257], g, g, 0.0, ALU.add, ALU.min).then_inc(S("dve_step"), 1)
                    dve.wait_ge(S("dve_step"), due("dve_step"))
            Cg = cum_g.rearrange("p (d b s) t -> p d b s t", d=2, b=2)
            for blk in range(2):
                f, g = Cg[:, 0, blk], Cg[:, 1, blk]
                dve.tensor_copy(QD[:, blk, :], f[:, 0, 1:257]).then_inc(S("dve_step"), 1)
                dve.wait_ge(S("dve_step"), due("dve_step"))
                dve.tensor_scalar(QD[:, 2 + blk, :], g[:, 0, 0:256], g[:, 0, 256:257], -1.0, ALU.subtract, ALU.mult).then_inc(S("dve_step"), 1)
                dve.wait_ge(S("dve_step"), due("dve_step"))
                dve.tensor_scalar(KD_rows[:, blk, :], f[:, 1, 1:257], f[:, 1, 256:257], -1.0, ALU.subtract, ALU.mult).then_inc(S("dve_step"), 1)
                dve.wait_ge(S("dve_step"), due("dve_step"))
                dve.tensor_copy(KD_rows[:, 2 + blk, :], g[:, 1, 0:256]).then_inc(S("dve_step"), 1)
                dve.wait_ge(S("dve_step"), due("dve_step"))
            dve.memset(flag, 0.0).then_inc(S("qd_raw_ready"), 1)
            dve.wait_ge(S("qd_raw_ready"), due("qd_raw_ready"))
            dve.wait_ge(S("decays_exp_ready"), due("decays_exp_ready"))
            for n in (2, 3):
                dve.tensor_tensor(decays[0:16, n, :], decays[0:16, n, :], dt_rows[0:16, SEQ:512], ALU.mult).then_inc(S("dve_step"), 1)
                dve.wait_ge(S("dve_step"), due("dve_step"))
            dve.memset(flag, 0.0).then_inc(S("ssd_rows_ready"), 1)
            dve.wait_ge(S("ssd_rows_ready"), due("ssd_rows_ready"))
            dve.wait_ge(S("fullD"), due("fullD"))
            b = bank_of("D", T.n["fullD"])
            dve.tensor_copy(cols, b[:, 0:224]).then_inc(S("freeD"), 1)
            dve.wait_ge(S("freeD"), due("freeD"))
            dve.wait_ge(S("xs_ready"), due("xs_ready"))
            for g in range(2):
                dve.wait_ge(S("fullD"), due("fullD"))
                b = bank_of("D", T.n["fullD"])
                dve.tensor_copy(BC[:, g, :], b[:, :]).then_inc(S("freeD"), 1)
                dve.wait_ge(S("freeD"), due("freeD"))
            dve.wait_ge(S("qd_exp_ready"), due("qd_exp_ready"))
            for d in range(2):
                dve.tensor_tensor(QD[:, 2 * d:2 * d + 2, :], QD[:, 2 * d:2 * d + 2, :], qc, ALU.mult).then_inc(S("dve_step"), 1)
                dve.wait_ge(S("dve_step"), due("dve_step"))
                dve.tensor_tensor(KD_rows[:, 2 * d:2 * d + 2, :], KD_rows[:, 2 * d:2 * d + 2, :], kc[:, :, SEQ:512], ALU.mult).then_inc(S("dve_step"), 1)
                dve.wait_ge(S("dve_step"), due("dve_step"))
            dve.memset(flag, 0.0).then_inc(S("qd_kd_ready"), 1)
            dve.wait_ge(S("qd_kd_ready"), due("qd_kd_ready"))
            dve.memset(SG, 0.0).then_inc(S("dve_step"), 1)
            dve.wait_ge(S("dve_step"), due("dve_step"))
            for d in range(2):
                dve.wait_ge(S("fullD"), due("fullD"))
                b = bank_of("D", T.n["fullD"])
                for par in range(2):
                    rows_ = slice(64 * par, 64 * par + 64)
                    src = b[rows_, :].rearrange("p (b n) -> p b n", b=2)[:, :, par * P:par * P + P]
                    signal = "freeD" if par else "dve_step"
                    dve.tensor_copy(SG[rows_, 2 * d:2 * d + 2, par * P:par * P + P], src).then_inc(S(signal), 1)
                    dve.wait_ge(S(signal), due(signal))
            dve.memset(flag, 0.0).then_inc(S("states_ready"), 1)
            dve.wait_ge(S("states_ready"), due("states_ready"))

            def level_args(l):
                half = 1 << (l - 1)
                v = lev[:, l % 2, :].rearrange("p (w b n two h) -> p w b n two h", w=2, b=2, two=2, h=half)

                def c(d, off):
                    return Cg[:, d, :, 0, off:off + 256].rearrange("p b (n two h) -> p b n two h", two=2, h=half)

                for blk in range(2):
                    f1, f0, b0 = c(0, 1)[:, blk], c(0, 0)[:, blk], c(1, 0)[:, blk]
                    mf = f0[:, :, 1, 0:1].to_broadcast([P, 128 // half, half])
                    mb = b0[:, :, 1, 0:1].to_broadcast([P, 128 // half, half])
                    dve.tensor_tensor(v[:, 0, blk, :, 1, :], f1[:, :, 1, :], mf, ALU.subtract).then_inc(S("dve_step"), 1)
                    dve.wait_ge(S("dve_step"), due("dve_step"))
                    dve.tensor_tensor(v[:, 0, blk, :, 0, :], mb, b0[:, :, 0, :], ALU.subtract).then_inc(S("dve_step"), 1)
                    dve.wait_ge(S("dve_step"), due("dve_step"))
                    dve.tensor_tensor(v[:, 1, blk, :, 0, :], mf, f1[:, :, 0, :], ALU.subtract).then_inc(S("dve_step"), 1)
                    dve.wait_ge(S("dve_step"), due("dve_step"))
                    dve.tensor_tensor(v[:, 1, blk, :, 1, :], b0[:, :, 1, :], mb, ALU.subtract).then_inc(S("dve_step"), 1)
                    dve.wait_ge(S("dve_step"), due("dve_step"))
                dve.memset(flag, 0.0).then_inc(S("level_args_ready"), 1)
                dve.wait_ge(S("level_args_ready"), due("level_args_ready"))

            def level_ops(l):
                dve.wait_ge(S("level_exp_ready"), due("level_exp_ready"))
                v = lev[:, l % 2, :].rearrange("p (w b i) -> p w b i", w=2, b=2)
                dve.tensor_tensor(v[:, 0], v[:, 0], qc, ALU.mult).then_inc(S("dve_step"), 1)
                dve.wait_ge(S("dve_step"), due("dve_step"))
                dve.tensor_tensor(v[:, 1], v[:, 1], kc[:, :, 0:SEQ], ALU.mult).then_inc(S("level_ready"), 1)
                dve.wait_ge(S("level_ready"), due("level_ready"))

            def take_level(l):
                for par in range(2):
                    dve.wait_ge(S("fullD"), due("fullD"))
                    b = bank_of("D", T.n["fullD"])
                    if l == 8:
                        dve.tensor_copy(att8[:, par, :], b[:, :]).then_inc(S("freeD"), 1)
                        dve.wait_ge(S("freeD"), due("freeD"))
                        continue
                    mask = C("twice") if l == 0 else C("levels", 7, P)[:, l - 1, :]
                    mask = mask.unsqueeze(1).to_broadcast([P, 4, P])
                    src = b[:, :].rearrange("p (n i) -> p n i", n=4)
                    dst = att[:, par, :] if l == 0 else lev_tmp
                    dve.tensor_tensor(dst.rearrange("p (n i) -> p n i", n=4), src, mask, ALU.mult).then_inc(S("freeD"), 1)
                    dve.wait_ge(S("freeD"), due("freeD"))
                    if l:
                        dve.tensor_tensor(att[:, par, :], att[:, par, :], lev_tmp, ALU.add).then_inc(S("dve_step"), 1)
                        dve.wait_ge(S("dve_step"), due("dve_step"))

            level_args(1)
            take_level(0)
            level_ops(1)
            for l in range(1, 9):
                if l < 8:
                    level_args(l + 1)
                take_level(l)
                if l < 8:
                    level_ops(l + 1)
            dve.memset(flag, 0.0).then_inc(S("att_ready"), 1)
            dve.wait_ge(S("att_ready"), due("att_ready"))
            sc = small[:, 110:118]
            iv = small[:, 118:126]
            rs = small[:, 126:134]

            def finish_norm(n, width):
                dve.tensor_scalar(iv[:, 0:n], sc[:, 0:n], 1.0 / width, EPS, ALU.mult, ALU.add).then_inc(S("dve_step"), 1)
                dve.wait_ge(S("dve_step"), due("dve_step"))
                dve.reciprocal(iv[:, 0:n], iv[:, 0:n]).then_inc(S("inv_ready"), 1)
                dve.wait_ge(S("inv_ready"), due("inv_ready"))
                dve.wait_ge(S("rstd_ready"), due("rstd_ready"))

            for t in range(2):
                dve.wait_ge(S("fullD"), due("fullD"))
                b = bank_of("D", T.n["fullD"])
                o = O[:, t, 0:512]
                o3 = o.rearrange("p (h v) -> p h v", h=4)
                dve.tensor_copy(o, b[:, :]).then_inc(S("freeD"), 1)
                dve.wait_ge(S("freeD"), due("freeD"))
                dve.tensor_tensor(lev_tmp, o, o, ALU.mult).then_inc(S("dve_step"), 1)
                dve.wait_ge(S("dve_step"), due("dve_step"))
                dve.tensor_reduce(sc[:, 0:4], lev_tmp.rearrange("p (h v) -> p h v", h=4), AX, ALU.add).then_inc(S("dve_step"), 1)
                dve.wait_ge(S("dve_step"), due("dve_step"))
                finish_norm(4, 128)
                dve.tensor_tensor(o3, o3, bc(rs[:, 0:4], P), ALU.mult).then_inc(S("dve_step"), 1)
                dve.wait_ge(S("dve_step"), due("dve_step"))
                dve.tensor_tensor(o3, o3, gla_gain.unsqueeze(1).to_broadcast([P, 4, P]), ALU.mult).then_inc(S("dve_step"), 1)
                dve.wait_ge(S("dve_step"), due("dve_step"))
                dve.tensor_tensor(o, o, silu_r[:, t, :], ALU.mult).then_inc(S("dve_step"), 1)
                dve.wait_ge(S("dve_step"), due("dve_step"))
            for c in range(2):
                for d in range(2):
                    at = 160 + 32 * c + 24 * d
                    dve.tensor_tensor(XW[:, 2 * c + d, :].rearrange("p (h v) -> p h v", h=8),
                                      XS[:, 2 + c, :].rearrange("p (h v) -> p h v", h=8), bc(cols[:, at:at + 8], HD), ALU.mult).then_inc(S("dve_step"), 1)
                    dve.wait_ge(S("dve_step"), due("dve_step"))
            dve.memset(flag, 0.0).then_inc(S("xw_ready"), 1)
            dve.wait_ge(S("xw_ready"), due("xw_ready"))
            dve.wait_ge(S("fullD"), due("fullD"))
            b = bank_of("D", T.n["fullD"])
            dve.tensor_copy(SS, b[:, :].rearrange("p (d n) -> p d n", d=2)).then_inc(S("freeD"), 1)
            dve.wait_ge(S("freeD"), due("freeD"))
            dve.memset(flag, 0.0).then_inc(S("ss_ready"), 1)
            dve.wait_ge(S("ss_ready"), due("ss_ready"))
            for t in range(2):
                for g in range(2):
                    dve.wait_ge(S("fullD"), due("fullD"))
                    b = bank_of("D", T.n["fullD"])
                    y = O[:, t, 512 + 256 * g:768 + 256 * g].rearrange("p (h v) -> p h v", h=4)
                    tmp = lev_tmp[:, 0:256].rearrange("p (h v) -> p h v", h=4)
                    for d in range(2):
                        at = t * 80 + (48 if d == 0 else 72) + 4 * g
                        signal = "freeD" if d else "dve_step"
                        dve.tensor_tensor(tmp if d else y, b[:, d * 256:d * 256 + 256].rearrange("p (h v) -> p h v", h=4),
                                          bc(cols[:, at:at + 4], HD), ALU.mult).then_inc(S(signal), 1)
                        dve.wait_ge(S(signal), due(signal))
                    dve.tensor_tensor(y, y, tmp, ALU.add).then_inc(S("dve_step"), 1)
                    dve.wait_ge(S("dve_step"), due("dve_step"))
                y = O[:, t, 512:1024]
                dve.tensor_tensor(lev_tmp.rearrange("p (h v) -> p h v", h=8), XS[:, t, :].rearrange("p (h v) -> p h v", h=8),
                                  bc(skip_gain, HD), ALU.mult).then_inc(S("dve_step"), 1)
                dve.wait_ge(S("dve_step"), due("dve_step"))
                dve.tensor_tensor(y, y, lev_tmp, ALU.add).then_inc(S("dve_step"), 1)
                dve.wait_ge(S("dve_step"), due("dve_step"))
            for h in range(8):
                def col(j, n):
                    return cols[:, 80 * j + n + h:80 * j + n + h + 1]

                dve.wait_ge(S("fullD"), due("fullD"))
                b = bank_of("D", T.n["fullD"])
                dve.tensor_scalar(seg[:, 0:256], b[:, 1:257], col(0, 16), 0.0, ALU.subtract, ALU.min).then_inc(S("dve_step"), 1)
                dve.wait_ge(S("dve_step"), due("dve_step"))
                dve.tensor_scalar(seg[:, 256:384], b[:, 129:257], col(1, 16), 0.0, ALU.subtract, ALU.min).then_inc(S("freeD"), 1)
                dve.wait_ge(S("freeD"), due("freeD"))
                dve.wait_ge(S("fullD"), due("fullD"))
                b = bank_of("D", T.n["fullD"])
                dve.tensor_scalar(seg[:, 384:512], b[:, 0:128], col(0, 40), 0.0, ALU.subtract, ALU.max).then_inc(S("dve_step"), 1)
                dve.wait_ge(S("dve_step"), due("dve_step"))
                dve.tensor_scalar(seg[:, 512:768], b[:, 0:256], col(1, 40), 0.0, ALU.subtract, ALU.max).then_inc(S("freeD"), 1)
                dve.wait_ge(S("freeD"), due("freeD"))
                dve.memset(flag, 0.0).then_inc(S("seg_ready"), 1)
                dve.wait_ge(S("seg_ready"), due("seg_ready"))
                dve.wait_ge(S("seg_exp_ready"), due("seg_exp_ready"))
                w = W[:, h % 2, :]

                def masked(c0, c1, scalar, mask):
                    v = seg[:, c0:c1]
                    dve.scalar_tensor_tensor(out=v, in0=v, scalar=scalar, in1=C(mask), op0=ALU.mult, op1=ALU.mult).then_inc(S("dve_step"), 1)
                    dve.wait_ge(S("dve_step"), due("dve_step"))

                masked(0, 128, col(0, 0), "after")
                masked(384, 512, col(0, 8), "before")
                masked(256, 384, col(1, 0), "after")
                masked(640, 768, col(1, 8), "before")
                dve.tensor_tensor(w[:, 0:128], seg[:, 0:128], seg[:, 384:512], ALU.add).then_inc(S("dve_step"), 1)
                dve.wait_ge(S("dve_step"), due("dve_step"))
                dve.tensor_scalar(w[:, 128:256], seg[:, 128:256], col(0, 0), None, ALU.mult).then_inc(S("dve_step"), 1)
                dve.wait_ge(S("dve_step"), due("dve_step"))
                dve.tensor_scalar(w[:, 256:384], seg[:, 512:640], col(1, 8), None, ALU.mult).then_inc(S("dve_step"), 1)
                dve.wait_ge(S("dve_step"), due("dve_step"))
                dve.tensor_tensor(w[:, 384:512], seg[:, 256:384], seg[:, 640:768], ALU.add).then_inc(S("dve_step"), 1)
                dve.wait_ge(S("dve_step"), due("dve_step"))
                dve.tensor_tensor(w, w, BC[:, h // 4, :], ALU.mult).then_inc(S("w_ready"), 1)
                dve.wait_ge(S("w_ready"), due("w_ready"))
            dve.wait_ge(S("intra_ready"), due("intra_ready"))
            for t in range(2):
                y = O[:, t, 512:1024]
                y2 = y.rearrange("p (g v) -> p g v", g=2)
                dve.tensor_tensor(y, y, intra[:, t, :], ALU.add).then_inc(S("dve_step"), 1)
                dve.wait_ge(S("dve_step"), due("dve_step"))
                dve.tensor_tensor(y, y, silu_z[:, t, :], ALU.mult).then_inc(S("dve_step"), 1)
                dve.wait_ge(S("dve_step"), due("dve_step"))
                dve.tensor_tensor(lev_tmp, y, y, ALU.mult).then_inc(S("dve_step"), 1)
                dve.wait_ge(S("dve_step"), due("dve_step"))
                dve.tensor_reduce(sc[:, 0:2], lev_tmp.rearrange("p (g v) -> p g v", g=2), AX, ALU.add).then_inc(S("dve_step"), 1)
                dve.wait_ge(S("dve_step"), due("dve_step"))
                finish_norm(2, 256)
                dve.tensor_tensor(y2, y2, bc(rs[:, 0:2], 256), ALU.mult).then_inc(S("dve_step"), 1)
                dve.wait_ge(S("dve_step"), due("dve_step"))
                dve.tensor_tensor(y, y, ssd_gain, ALU.mult).then_inc(S("dve_step"), 1)
                dve.wait_ge(S("dve_step"), due("dve_step"))

            def gate_and_gain(which):
                for n in range(2):
                    dve.wait_ge(S("fullD"), due("fullD"))
                    b = bank_of("D", T.n["fullD"])
                    dve.tensor_copy(gate3_b[:, 0, n * 512:n * 512 + 512], b[:, :]).then_inc(S("freeD"), 1)
                    dve.wait_ge(S("freeD"), due("freeD"))
                if which == 0:
                    dve.memset(flag, 0.0).then_inc(S("mixer2_done"), 1)
                    dve.wait_ge(S("mixer2_done"), due("mixer2_done"))
                dve.wait_ge(S("gain_landed"), due("gain_landed", 16))
                dve.tensor_tensor(gate3_b[:, 0, :], gate3_b[:, 0, :], gain_b, ALU.mult).then_inc(S("dve_step"), 1)
                dve.wait_ge(S("dve_step"), due("dve_step"))
                dve.memset(flag, 0.0).then_inc(S("gain_used"), 1)
                dve.wait_ge(S("gain_used"), due("gain_used"))

            def post(last):
                for t in range(2):
                    dve.tensor_tensor_reduce(xn3[:, t, :], Y[:, t, :], Y[:, t, :], 1.0, 0.0, ALU.mult, ALU.add, sc[:, t:t + 1]).then_inc(S("dve_step"), 1)
                    dve.wait_ge(S("dve_step"), due("dve_step"))
                finish_norm(2, D)
                for t in range(2):
                    dve.scalar_tensor_tensor(out=Y[:, t, :], in0=Y[:, t, :], scalar=rs[:, t:t + 1], in1=gate3_b[:, 0, :],
                                             op0=ALU.mult, op1=ALU.mult).then_inc(S("dve_step"), 1)
                    dve.wait_ge(S("dve_step"), due("dve_step"))
                    signal = "out_ready_rows" if last else "dve_step"
                    dve.tensor_tensor(X[:, t, :], X[:, t, :], Y[:, t, :], ALU.add).then_inc(S(signal), 1)
                    dve.wait_ge(S(signal), due(signal))

            gate_and_gain(0)
            dve.memset(flag, 0.0).then_inc(S("o_ready"), 1)
            dve.wait_ge(S("o_ready"), due("o_ready"))
            for k in range(0, KD, 2):
                dve.wait_ge(S("fullD"), due("fullD"))
                b = bank_of("D", T.n["fullD"])
                dve.tensor_copy(oT2[:, k, :], b[:, 0:SEQ]).then_inc(S("freeD"), 1)
                dve.wait_ge(S("freeD"), due("freeD"))
                dve.memset(flag, 0.0).then_inc(S("oT2_ready_dve"), 1)
                dve.wait_ge(S("oT2_ready_dve"), due("oT2_ready_dve"))

            def take_y():
                for n in range(2):
                    for t in range(2):
                        dve.wait_ge(S("fullD"), due("fullD"))
                        b = bank_of("D", T.n["fullD"])
                        dve.tensor_copy(Y[:, t, n * 512:n * 512 + 512], b[:, :]).then_inc(S("freeD"), 1)
                        dve.wait_ge(S("freeD"), due("freeD"))

            take_y()
            post(False)
            gate_and_gain(1)
            norm(xn3, range(2))
            modulate(h3T, 1, 1)
            for blk in range(FB):
                dve.wait_ge(S("fullD"), due("fullD"))
                b = bank_of("D", T.n["fullD"])
                dve.wait_ge(S("ff_silu_ready"), due("ff_silu_ready"))
                dve.tensor_tensor(ffT[:, blk, :], b[:, SEQ:512], ff_silu[:, blk % 2, :], ALU.mult).then_inc(S("ffT_ready"), 1)
                dve.wait_ge(S("ffT_ready"), due("ffT_ready"))
                dve.memset(flag, 0.0).then_inc(S("freeD"), 1)
                dve.wait_ge(S("freeD"), due("freeD"))
            take_y()
            post(True)

        def act_block2(act, T, norm, modulate):
            due = T.step
            act.wait_ge(S("block1_done"), due("block1_done"))
            act.dma_start(final_gain, A["final_g"].partition_broadcast(P)).then_inc(S("final_gain_landed"), 16)
            act.dma_start(X[:, 2:4, :], A["ctx_2"][0].rearrange("(t p) n -> p t n", p=P)).then_inc(S("ctx2_landed"), 16)
            act.dma_start(wg[0:16, 0, :], A["gla_wg_f_2"][0]).then_inc(S("wg_landed"), 16)
            act.dma_start(wg[16:32, 1, :], A["gla_wg_b_2"][0]).then_inc(S("wg_landed"), 16)
            for dst, src in rows2_loads:
                act.dma_start(dst, src).then_inc(S("block2_rows_landed"), 16)
            norm(2)
            norm(TILES)
            modulate(hT, 0, 2)
            for blk in range(2):
                act.wait_ge(S("fullA"), due("fullA"))
                b = bank_of("A", T.n["fullA"])
                act.activation(kc[:, blk, :], b[:, :], ACT.Copy).then_inc(S("freeA"), 1)
                act.wait_ge(S("freeA"), due("freeA"))
            for t in (1, 3):
                act.wait_ge(S("fullA"), due("fullA"))
                b = bank_of("A", T.n["fullA"])
                act.activation(V2[:, t, :], b[:, :], ACT.Copy).then_inc(S("freeA"), 1)
                act.wait_ge(S("freeA"), due("freeA"))
            for dst in (silu_r, silu_z):
                for t in range(2):
                    act.wait_ge(S("fullA"), due("fullA"))
                    b = bank_of("A", T.n["fullA"])
                    act.activation(dst[:, t, :], b[:, :], ACT.Silu).then_inc(S("freeA"), 1)
                    act.wait_ge(S("freeA"), due("freeA"))
            for blk in (1, 3, 5):
                act.wait_ge(S("fullA"), due("fullA"))
                b = bank_of("A", T.n["fullA"])
                act.activation(x_raw[:, blk, :], b[:, :], ACT.Copy).then_inc(S("freeA"), 1)
                act.wait_ge(S("freeA"), due("freeA"))
            act.activation(flag_a, zero, ACT.Copy).then_inc(S("x_raw_ready_act"), 1)
            act.wait_ge(S("x_raw_ready_act"), due("x_raw_ready_act"))

            def log1p_exp_neg_abs(dst, src):
                act.activation(dst, src, ACT.Abs).then_inc(S("act_step"), 1)
                act.wait_ge(S("act_step"), due("act_step"))
                act.activation(dst, dst, ACT.Exp, scale=-1.0).then_inc(S("act_step"), 1)
                act.wait_ge(S("act_step"), due("act_step"))
                act.activation(dst, dst, ACT.Ln, bias=ones[0:dst.shape[0], :]).then_inc(S("act_step"), 1)
                act.wait_ge(S("act_step"), due("act_step"))

            act.wait_ge(S("dt_raw_ready"), due("dt_raw_ready"))
            act.wait_ge(S("block2_rows_landed"), 16 * N_ROWS2)
            log1p_exp_neg_abs(dt_rows[0:16, :], dt_raw[0:16, :])
            act.activation(neg_a, neg_a, ACT.Exp).then_inc(S("act_step"), 1)
            act.wait_ge(S("act_step"), due("act_step"))
            act.activation(flag_a, zero, ACT.Copy).then_inc(S("dt_log_ready"), 1)
            act.wait_ge(S("dt_log_ready"), due("dt_log_ready"))
            act.wait_ge(S("gates_raw_ready"), due("gates_raw_ready"))
            log1p_exp_neg_abs(gate_tmp, gates)
            act.activation(flag_a, zero, ACT.Copy).then_inc(S("gates_log_ready"), 1)
            act.wait_ge(S("gates_log_ready"), due("gates_log_ready"))
            for blk in range(6):
                act.wait_ge(S("conv_ready"), due("conv_ready"))
                act.activation(xbc[:, blk, :], xbc[:, blk, :], ACT.Silu, bias=vecs[:, 2, 80 + blk:81 + blk]).then_inc(S("act_step"), 1)
                act.wait_ge(S("act_step"), due("act_step"))
            act.activation(flag_a, zero, ACT.Copy).then_inc(S("xbc_ready"), 1)
            act.wait_ge(S("xbc_ready"), due("xbc_ready"))
            act.wait_ge(S("decays_ready"), due("decays_ready"))
            act.activation(decays[0:16, :, :], decays[0:16, :, :], ACT.Exp).then_inc(S("decays_exp_ready"), 1)
            act.wait_ge(S("decays_exp_ready"), due("decays_exp_ready"))
            for t in range(TILES):
                act.wait_ge(S("fullA"), due("fullA"))
                b = bank_of("A", T.n["fullA"])
                act.activation(XS[:, t, :], b[:, :], ACT.Copy).then_inc(S("freeA"), 1)
                act.wait_ge(S("freeA"), due("freeA"))
            act.wait_ge(S("fullA"), due("fullA"))
            b = bank_of("A", T.n["fullA"])
            act.activation(BT, b[:, 0:256].rearrange("p (c n) -> p c n", c=2), ACT.Copy).then_inc(S("freeA"), 1)
            act.wait_ge(S("freeA"), due("freeA"))
            act.activation(flag_a, zero, ACT.Copy).then_inc(S("xs_ready"), 1)
            act.wait_ge(S("xs_ready"), due("xs_ready"))
            act.wait_ge(S("qd_raw_ready"), due("qd_raw_ready"))
            both = area(15872, 2048)
            act.activation(both, both, ACT.Exp).then_inc(S("qd_exp_ready"), 1)
            act.wait_ge(S("qd_exp_ready"), due("qd_exp_ready"))
            for d in range(2):
                act.wait_ge(S("fullA"), due("fullA"))
                b = bank_of("A", T.n["fullA"])
                act.activation(KDt[:, d, :], b[:, :], ACT.Copy).then_inc(S("freeA"), 1)
                act.wait_ge(S("freeA"), due("freeA"))
            act.activation(flag_a, zero, ACT.Copy).then_inc(S("kdt_ready"), 1)
            act.wait_ge(S("kdt_ready"), due("kdt_ready"))
            for l in range(1, 9):
                act.wait_ge(S("level_args_ready"), due("level_args_ready"))
                act.activation(lev[:, l % 2, :], lev[:, l % 2, :], ACT.Exp).then_inc(S("level_exp_ready"), 1)
                act.wait_ge(S("level_exp_ready"), due("level_exp_ready"))

            def root(n):
                act.wait_ge(S("inv_ready"), due("inv_ready"))
                act.activation(small[:, 126:126 + n], small[:, 118:118 + n], ACT.Sqrt).then_inc(S("rstd_ready"), 1)
                act.wait_ge(S("rstd_ready"), due("rstd_ready"))

            root(4)
            root(4)
            for h in range(9):
                if h < 8:
                    act.wait_ge(S("seg_ready"), due("seg_ready"))
                    act.activation(seg[:, 0:384], seg[:, 0:384], ACT.Exp).then_inc(S("act_step"), 1)
                    act.wait_ge(S("act_step"), due("act_step"))
                    act.activation(seg[:, 384:768], seg[:, 384:768], ACT.Exp, scale=-1.0).then_inc(S("seg_exp_ready"), 1)
                    act.wait_ge(S("seg_exp_ready"), due("seg_exp_ready"))
                if h:
                    act.wait_ge(S("fullA"), due("fullA"))
                    b = bank_of("A", T.n["fullA"])
                    act.activation(intra[:, :, (h - 1) * HD:h * HD], b[:, 0:P].rearrange("p (t v) -> p t v", t=2), ACT.Copy).then_inc(S("freeA"), 1)
                    act.wait_ge(S("freeA"), due("freeA"))
            act.activation(flag_a, zero, ACT.Copy).then_inc(S("intra_ready"), 1)
            act.wait_ge(S("intra_ready"), due("intra_ready"))
            root(2)
            root(2)
            act.wait_ge(S("mixer2_done"), due("mixer2_done"))
            act.dma_start(gain_b, A["norm_mix_post_2"][0].partition_broadcast(P)).then_inc(S("gain_landed"), 16)
            for k in range(1, KD, 2):
                act.wait_ge(S("fullA"), due("fullA"))
                b = bank_of("A", T.n["fullA"])
                act.activation(oT2[:, k, :], b[:, 0:SEQ], ACT.Copy).then_inc(S("freeA"), 1)
                act.wait_ge(S("freeA"), due("freeA"))
                act.activation(flag_a, zero, ACT.Copy).then_inc(S("oT2_ready_act"), 1)
                act.wait_ge(S("oT2_ready_act"), due("oT2_ready_act"))
            root(2)
            act.wait_ge(S("gain_used"), due("gain_used"))
            act.dma_start(gain_b, A["norm_ffn_post_2"][0].partition_broadcast(P)).then_inc(S("gain_landed"), 16)
            norm(2)
            modulate(h3T, 1, 1)
            for blk in range(FB):
                job = ff_first[0] + blk
                if blk > 1:
                    act.wait_ge(S("ffT_ready"), blk - 1)
                act.wait_ge(S("fullD"), job)
                act.activation(ff_silu[:, blk % 2, :], pool_banks["D"][(job - 1) % POOL][:, 0:SEQ], ACT.Silu).then_inc(S("ff_silu_ready"), 1)
                act.wait_ge(S("ff_silu_ready"), due("ff_silu_ready"))
            root(2)
            for t in range(2):
                act.wait_ge(S("out_ready_rows"), t + 1)
                act.dma_start(out[0, t * P:t * P + P, :], X[:, t, :]).then_inc(S("out_stored"), 16)
            act.wait_ge(S("out_stored"), 32)

        rows2_loads = [(gla_gain, A["gla_norm_2"][0].partition_broadcast(P)), (ssd_gain, A["ssd_norm_2"][0].partition_broadcast(P)),
                       (skip_gain, A["d_skip_2"][0].partition_broadcast(P))]
        for at, d in ((0, "f"), (8, "b")):
            rows2_loads.append((small[at:at + 8, 100:101], A[f"dt_bias_{d}_2"][0].rearrange("(h a) -> h a", a=1)))
            rows2_loads.append((small[at:at + 8, 101:102], A[f"a_log_{d}_2"][0].rearrange("(h a) -> h a", a=1)))
        N_ROWS2 = len(rows2_loads)

        @block.tensor
        def _(pe):
            T = Tally()
            due = T.step

            def release(pool, units=1):
                for _ in range(units):
                    released.append((pool, T.n["free" + pool], T.per and T.per["free" + pool]))

            def next_slot():
                T.step("ring")
                return (T.n["ring"] - 1) % RING

            def turn(dst, src):
                return pe.transpose(dst, src, ident[0:src.shape[0], 0:src.shape[0]])

            def modulation(l):
                for seg in range(7):
                    if seg < 6:
                        pe.wait_ge(S("freeD"), due("freeD"))
                        b = bank_of("D", T.n["freeD"])
                        r0 = next_slot()
                        pe.wait_ge(S(f"slot_landed{r0}"), due(f"slot_landed{r0}", 16))
                        r1 = next_slot()
                        pe.wait_ge(S(f"slot_landed{r1}"), due(f"slot_landed{r1}", 16))
                        for k in range(KD):
                            for h, r in ((0, r0), (1, r1)):
                                mm = pe.matmul(b[64 * h:64 * h + 2, :], silu_c[:, l, k, :], slot_view(r)[:, k, :],
                                               start=(k == 0), stop=(k == KD - 1))
                        mm.then_inc(S("fullD"), 1)
                        release("D", 2)
                    if seg and (seg - 1) % 3 != 2:
                        pe.wait_ge(S("seg_row_ready"), due("seg_row_ready"))
                        pe.wait_ge(S("freeD"), due("freeD"))
                        b = bank_of("D", T.n["freeD"])
                        for k in range(KD):
                            mm = turn(b[:, 2 * k:2 * k + 2], row_tmp[0:2, (seg - 1) % 3, k * P:k * P + P])
                            if k == KD - 1:
                                mm.then_inc(S("fullD"), 1)

            def turn_streams(src, tiles):
                for k in range(KD):
                    pool = "DA"[k % 2]
                    pe.wait_ge(S("free" + pool), due("free" + pool))
                    b = bank_of(pool, T.n["free" + pool])
                    for t in tiles:
                        mm = turn(b[:, t * P:t * P + P], src[:, t, k * P:k * P + P])
                        if t == tiles[-1]:
                            mm.then_inc(S("full" + pool), 1)

            def dense(pool, t, r, lhs, c0=0, c1=512, ks=KD, signal=None):
                pe.wait_ge(S("free" + pool), due("free" + pool))
                b = bank_of(pool, T.n["free" + pool])
                for k in range(ks):
                    mm = pe.matmul(b[:, 0:c1 - c0], lhs[:, k, t * P:t * P + P], slot_view(r)[:, k, c0:c1],
                                   start=(k == 0), stop=(k == ks - 1))
                mm.then_inc(S("full" + pool), 1)
                return mm

            def broadcast_gate(g, streams):
                for s in range(streams):
                    for n in range(2):
                        pe.wait_ge(S("freeD"), due("freeD"))
                        b = bank_of("D", T.n["freeD"])
                        pe.matmul(b[:, :], ident[0:2, s:s + 1].to_broadcast([2, P]), gate_rows[0:2, g, n * 512:n * 512 + 512],
                                  start=True, stop=True).then_inc(S("fullD"), 1)

            def mixer(l):
                tiles = range(TILES)
                own = range(TILES) if l == 0 else range(2)
                pe.wait_ge(S("xn_ready"), due("xn_ready", TILES))
                turn_streams(xn, range(TILES))
                pe.wait_ge(S("hT_ready_dve"), due("hT_ready_dve", 4 * 1))
                pe.wait_ge(S("hT_ready_act"), due("hT_ready_act", 4 * 1))
                for u in range(3):
                    r = next_slot()
                    pe.wait_ge(S(f"slot_landed{r}"), due(f"slot_landed{r}", 16))
                    for t in tiles:
                        lone = t not in own
                        if lone and u == 0:
                            continue
                        dense("DA"[t % 2], t, r, hT, 256 if lone else 0, 512)
                    release("A")
                pe.wait_ge(S("z_ready_dve"), due("z_ready_dve"))
                pe.wait_ge(S("z_ready_act"), due("z_ready_act"))
                for s in range(len(own) // 2):
                    for c in range(2):
                        pe.wait_ge(S("freeD"), due("freeD"))
                        b = bank_of("D", T.n["freeD"])
                        for t in range(2):
                            mm = pe.matmul(b[:, :], Z[:, 2 * s + t, c * P:c * P + P], C("dft_pos", 2, 512)[:, t, :],
                                           start=(t == 0), stop=(t == 1))
                        mm.then_inc(S("fullD"), 1)
                    for c in range(2):
                        pe.wait_ge(S("four_ready"), due("four_ready"))
                        pe.wait_ge(S("freeA"), due("freeA"))
                        b = bank_of("A", T.n["freeA"])
                        pe.matmul(b[:, 0:SEQ], C("dft_cos"), four[:, c, 0:SEQ], start=True, stop=False)
                        pe.matmul(b[:, 0:SEQ], C("dft_nsin"), four[:, c, SEQ:512], start=False, stop=True)\
                            .then_inc(S("fullA"), 1)
                pe.wait_ge(S("rope_ready"), due("rope_ready"))
                for t in range(2):
                    turn_q(t)
                for t in tiles:
                    turn_k(t)
                for s in range(len(own) // 2):
                    if s == 1:
                        for t in (2, 3):
                            turn_q(t)
                    attention(s)
                for n in range(2):
                    for br, ks in ((0, 2), (1, 4), (2, 2)):
                        rg = next_slot()
                        pe.wait_ge(S(f"slot_landed{rg}"), due(f"slot_landed{rg}", 16))
                        for t in own:
                            dense("A", t, rg, hT)
                        release("A")
                        rb = next_slot()
                        pe.wait_ge(S(f"slot_landed{rb}"), due(f"slot_landed{rb}", 16))
                        lhs = {0: fT, 1: oT[:, 0:4, :], 2: oT[:, 4:6, :]}[br]
                        if n == 0 and br == 0:
                            pe.wait_ge(S("fT_ready"), due("fT_ready", len(own)))
                        if n == 0 and br == 1:
                            pe.wait_ge(S("oT_ready"), due("oT_ready", 12 * (len(own) // 2)))
                        for t in own:
                            dense("D", t, rb, lhs, ks=ks)
                        release("D")
                broadcast_gate(0, len(own) // 2)
                pe.wait_ge(S("m_ready"), due("m_ready"))
                turn_streams(m_sum, list(own))
                pe.wait_ge(S("mT_ready_dve"), due("mT_ready_dve", 4))
                pe.wait_ge(S("mT_ready_act"), due("mT_ready_act", 4))
                for n in range(2):
                    r = next_slot()
                    pe.wait_ge(S(f"slot_landed{r}"), due(f"slot_landed{r}", 16))
                    for t in own:
                        dense("D", t, r, mT)
                    release("D")

            def turn_q(t):
                pe.wait_ge(S("freeD"), due("freeD"))
                b = bank_of("D", T.n["freeD"])
                for h in range(4):
                    mm = turn(b[:, h * P:h * P + P], Z[:, t, GQ + h * P:GQ + h * P + P])
                    if h == 3:
                        mm.then_inc(S("fullD"), 1)
                pe.wait_ge(S("freeD"), due("freeD"))
                b = bank_of("D", T.n["freeD"])
                for h in range(2):
                    mm = turn(b[:, h * P:h * P + P], Z[:, t, WQ + h * P:WQ + h * P + P])
                    if h == 1:
                        mm.then_inc(S("fullD"), 1)

            def turn_k(t):
                pe.wait_ge(S("freeD"), due("freeD"))
                b = bank_of("D", T.n["freeD"])
                turn(b[:, 0:P], Z[:, t, GK:GK + P])
                turn(b[:, P:2 * P], Z[:, t, WK:WK + P]).then_inc(S("fullD"), 1)

            def attention(s):
                pe.wait_ge(S("qT_ready"), due("qT_ready", 8))
                if s == 0:
                    pe.wait_ge(S("kT_ready"), due("kT_ready", 8))
                keys = range(TILES) if s == 0 else range(2, TILES)
                k0 = keys[0] * P
                for t in (2 * s, 2 * s + 1):
                    for grp in range(3):
                        for h in range(4):
                            kv = grp if grp < 2 else 2 + h // 2
                            pe.wait_ge(S("freeD"), due("freeD"))
                            b = bank_of("D", T.n["freeD"])
                            pe.matmul(b[:, 0:512 - k0], qT[0:HD, 4 * grp + h, (t % 2) * P:(t % 2) * P + P],
                                      kT[0:HD, kv, k0:512], start=True, stop=True).then_inc(S("fullD"), 1)
                        pe.wait_ge(S("probs_ready"), due("probs_ready", 4))
                        for kt in keys:
                            pe.wait_ge(S("freeA"), due("freeA"))
                            b = bank_of("A", T.n["freeA"])
                            for h in range(4):
                                mm = turn(b[:, h * P:h * P + P], probs[:, h, kt * P - k0:kt * P - k0 + P])
                                if h == 3:
                                    mm.then_inc(S("fullA"), 1)
                        pe.wait_ge(S("probsT_ready"), due("probsT_ready", len(keys)))
                        pe.wait_ge(S("freeA"), due("freeA"))
                        b = bank_of("A", T.n["freeA"])
                        for kt in keys:
                            if grp < 2:
                                mm = pe.matmul(b[0:HD, :], Z[:, kt, GV + HD * grp:GV + HD * grp + HD], probsT[:, kt, :],
                                               start=(kt == keys[0]), stop=(kt == keys[-1]))
                        if grp == 2:
                            for v in range(2):
                                for kt in keys:
                                    mm = pe.matmul(b[0:HD, v * 256:v * 256 + 256], Z[:, kt, WV + HD * v:WV + HD * v + HD],
                                                   probsT[:, kt, v * 256:v * 256 + 256],
                                                   start=(kt == keys[0]), stop=(kt == keys[-1]))
                        mm.then_inc(S("fullA"), 1)

            def experts(l):
                ns = 2 if l == 0 else 1
                tiles = range(2 * ns)
                R = CAP * ns
                pe.wait_ge(S("xn_ready"), due("xn_ready", 2 * ns))
                turn_streams(xn2, list(tiles))
                pe.wait_ge(S("hT_ready_dve"), due("hT_ready_dve", 4))
                pe.wait_ge(S("hT_ready_act"), due("hT_ready_act", 4))
                pe.wait_ge(S("freeD"), due("freeD"))
                b = bank_of("D", T.n["freeD"])
                for t in tiles:
                    for k in range(KD):
                        mm = pe.matmul(b[:, t * E:t * E + E], h2T[:, k, t * P:t * P + P], w_router[:, l, k, :],
                                       start=(k == 0), stop=(k == KD - 1))
                mm.then_inc(S("fullD"), 1)
                broadcast_gate(1, ns)
                pe.wait_ge(S("aff_ready"), due("aff_ready"))
                pe.wait_ge(S("freeD"), due("freeD"))
                b = bank_of("D", T.n["freeD"])
                for t in tiles:
                    mm = turn(b[0:E, t * P:t * P + P], aff[:, t, :])
                    if t == tiles[-1]:
                        mm.then_inc(S("fullD"), 1)
                pe.wait_ge(S("slots_ready"), due("slots_ready"))
                pe.wait_ge(S("freeD"), due("freeD"))
                b = bank_of("D", T.n["freeD"])
                for t in tiles:
                    mm = turn(b[:, t * E:t * E + E], cum[0:E, t * P:t * P + P])
                    if t == tiles[-1]:
                        mm.then_inc(S("fullD"), 1)
                pe.wait_ge(S("pick_ready"), due("pick_ready"))
                for k in range(KD):
                    for s in range(ns):
                        pool = "DA"[s] if ns == 2 else "DA"[k % 2]
                        pe.wait_ge(S("free" + pool), due("free" + pool))
                        b = bank_of(pool, T.n["free" + pool])
                        for t in (2 * s, 2 * s + 1):
                            mm = pe.matmul(b[:, :], xn2[:, t, k * P:k * P + P], pick[:, t, :],
                                           start=(t == 2 * s), stop=(t == 2 * s + 1))
                        mm.then_inc(S("full" + pool), 1)
                for t in tiles:
                    pe.wait_ge(S("freeD"), due("freeD"))
                    b = bank_of("D", T.n["freeD"])
                    for g in range(4):
                        mm = turn(b[:, g * P:g * P + P], pick_g[:, t, g * P:g * P + P])
                        if g == 3:
                            mm.then_inc(S("fullD"), 1)
                per = {"ring": 24, "freeD": 12 + 4 * ns, "freeA": 4, "xgs_ready": 1, "hid_ready": 4 * 2,
                       "hidT_ready": 4, "out_ready": 4, "puts_ready": 1, **{f"slot_landed{r}": 96 for r in range(RING)}}
                expert_start[l] = T.n["freeD"]
                with pe.Fori(0, 4) as i:
                    T.enter(i, per)
                    pe.wait_ge(S("xgs_ready"), due("xgs_ready"))
                    for j in range(4):
                        for n in range(2):
                            rg = next_slot()
                            pe.wait_ge(S(f"slot_landed{rg}"), due(f"slot_landed{rg}", 16))
                            ru = next_slot()
                            pe.wait_ge(S(f"slot_landed{ru}"), due(f"slot_landed{ru}", 16))
                            pe.wait_ge(S("freeD"), due("freeD"))
                            b = bank_of("D", T.n["freeD"])
                            for k in range(KD):
                                for c, r in ((0, rg), (64, ru)):
                                    mm = pe.matmul(b[c:c + R, :], xgs[:, k, j, 0:R], slot_view(r)[:, k, :],
                                                   start=(k == 0), stop=(k == KD - 1))
                            mm.then_inc(S("fullD"), 1)
                            release("D", 2)
                        pe.wait_ge(S("hid_ready"), due("hid_ready", 2))
                        pe.wait_ge(S("freeD"), due("freeD"))
                        b = bank_of("D", T.n["freeD"])
                        pe.nop(nofuse=True)
                        for k in range(KD):
                            mm = turn(b[:, k * 64:k * 64 + R], hid[0:R, k * P:k * P + P])
                            if k == KD - 1:
                                mm.then_inc(S("fullD"), 1)
                        pe.wait_ge(S("hidT_ready"), due("hidT_ready"))
                        r0 = next_slot()
                        pe.wait_ge(S(f"slot_landed{r0}"), due(f"slot_landed{r0}", 16))
                        r1 = next_slot()
                        pe.wait_ge(S(f"slot_landed{r1}"), due(f"slot_landed{r1}", 16))
                        pe.wait_ge(S("freeA"), due("freeA"))
                        b = bank_of("A", T.n["freeA"])
                        for k in range(KD):
                            for n, r in ((0, r0), (1, r1)):
                                mm = pe.matmul(b[64 * n:64 * n + R, :], hidT[:, k, 0:R], slot_view(r)[:, k, :],
                                               start=(k == 0), stop=(k == KD - 1))
                        mm.then_inc(S("fullA"), 1)
                        release("A", 2)
                    pe.wait_ge(S("out_ready"), due("out_ready", 4))
                    pe.wait_ge(S("puts_ready"), due("puts_ready"))
                    for t in tiles:
                        for n in range(2):
                            pe.wait_ge(S("freeD"), due("freeD"))
                            b = bank_of("D", T.n["freeD"])
                            pe.matmul(b[:, :], puts[:, t, :], out_g[:, stream_of(t), n * 512:n * 512 + 512],
                                      start=True, stop=True).then_inc(S("fullD"), 1)
                T.leave(4)

            pe.wait_ge(S("const_landed"), 16)
            pe.wait_ge(S("vecs_landed"), due("vecs_landed", 16 * N_VEC))
            pe.wait_ge(S("small_ready"), due("small_ready"))
            pe.wait_ge(S("freeD"), due("freeD"))
            b = bank_of("D", T.n["freeD"])
            for v in range(4):
                mm = turn(b[:, v * P:v * P + VEC_ROWS[v]], vec_in[0:VEC_ROWS[v], v, :])
                if v == 3:
                    mm.then_inc(S("fullD"), 1)
            pe.wait_ge(S("silu_c_ready"), due("silu_c_ready", 6))
            for l in range(DEPTH):
                modulation(l)
                mixer(l)
                experts(l)
            pe_block2(pe, T, next_slot, release, turn, modulation, turn_streams, dense, broadcast_gate)

        @block.sync
        def _(sp):
            T = Tally()
            due = T.step

            def load(*pieces, in_loop=False, turn=None):
                n = T.step("ring")
                n = T.n["ring"]
                if n > RING:
                    pool, jobs, per = released[n - RING - 1]
                    sp.wait_ge(S("full" + pool), jobs + (per or 0) * (turn if in_loop else 3 if per else 0))
                r = (T.n["ring"] - 1) % RING
                for dst, src in pieces:
                    sp.dma_start(dst(r), src).then_inc(S(f"slot_landed{r}"), 16)

            def load_cols(w, c0, c1):
                wd = c1 - c0
                load((lambda r: slot_view(r)[:, :, 0:wd], big(w, c0, c1)))

            def load_modulation(l):
                L = LAYERS[l]
                if l:
                    sp.wait_ge(S("gate_rows_used"), l)
                for g in range(2):
                    src = L["b_mod"][L["row"], (2 + 3 * g) * D:(3 + 3 * g) * D]
                    sp.dma_start(gate_rows[0:2, g, :], src.partition_broadcast(2)).then_inc(S("gate_bias_landed"), 16)
                for u in range(12):
                    load_cols(L["w_mod"], 512 * u, 512 * u + 512)

            sp.dma_start(const[:, :], A["const"]).then_inc(S("const_landed"), 16)
            for l in range(DEPTH):
                load_modulation(l)
                w = A["w_in"][l]
                for u in range(3):
                    load_cols(w, 512 * u, 512 * u + 512)
                wb = {"w_br_fourier": 2, "w_br_global": 4, "w_br_window": 2}
                for n in range(2):
                    for b, (name, k) in enumerate(wb.items()):
                        load_cols(w, Z_W + b * D + n * 512, Z_W + b * D + n * 512 + 512)
                        load((lambda r, k=k: slot_view(r)[:, 0:k, :],
                              A[name][l][:, n * 512:n * 512 + 512].rearrange("(k p) n -> p k n", p=P)))
                for n in range(2):
                    load_cols(A["w_out"][l], 512 * n, 512 * n + 512)
                def expert_unit(g, q, turn=None):
                    j, name, n = q // 6, ("w_gate_e", "w_up_e", "w_gate_e", "w_up_e", "w_down_e", "w_down_e")[q % 6], (0, 0, 1, 1, 0, 1)[q % 6]
                    src = A[name][l].rearrange("(g j) (k p) n -> g j p k n", j=4, p=P)
                    load((lambda r: slot_view(r), src[g, j, :, :, n * 512:n * 512 + 512]), in_loop=turn is not None, turn=turn)

                for q in range(RING):
                    expert_unit(0, q)
                with sp.Fori(0, 3) as i:
                    for q in range(RING, 24):
                        expert_unit(i, q, turn=i)
                    for q in range(RING):
                        expert_unit(i + 1, q, turn=i)
                T.n["ring"] -= 24
                for q in range(RING, 24):
                    expert_unit(3, q)
            load_block2(sp, load, load_cols, load_modulation, T)

        @block.vector
        def _(dve):
            T = Tally()
            due = T.step

            def norm(dst, tiles):
                for t in tiles:
                    dve.tensor_tensor_reduce(dst[:, t, :], X[:, t, :], X[:, t, :], 1.0, 0.0, ALU.mult, ALU.add,
                                             ss[:, t:t + 1]).then_inc(S("dve_step"), 1)
                    dve.wait_ge(S("dve_step"), due("dve_step"))
                n = len(tiles)
                dve.tensor_scalar(inv[:, 0:n], ss[:, 0:n], 1.0 / D, EPS, ALU.mult, ALU.add).then_inc(S("dve_step"), 1)
                dve.wait_ge(S("dve_step"), due("dve_step"))
                dve.reciprocal(inv[:, 0:n], inv[:, 0:n]).then_inc(S("inv_ready"), 1)
                dve.wait_ge(S("inv_ready"), due("inv_ready"))
                dve.wait_ge(S("rstd_ready"), due("rstd_ready"))
                for t in tiles:
                    dve.tensor_scalar(dst[:, t, :], X[:, t, :], rstd[:, t:t + 1], None, ALU.mult).then_inc(S("xn_ready"), 1)
                    dve.wait_ge(S("xn_ready"), due("xn_ready"))

            def modulation(l):
                for seg in range(7):
                    if seg < 6:
                        dve.wait_ge(S("fullD"), due("fullD"))
                        b = bank_of("D", T.n["fullD"])
                        for h in range(2):
                            last = h == 1
                            if seg % 3 == 2:
                                if h == 0 and seg == 2:
                                    dve.wait_ge(S("gate_bias_landed"), due("gate_bias_landed", 32))
                                g = gate_rows[0:2, seg // 3, h * 512:h * 512 + 512]
                                signal = "freeD" if last else "dve_step"
                                dve.tensor_tensor(g, b[64 * h:64 * h + 2, :], g, ALU.add).then_inc(S(signal), 1)
                                dve.wait_ge(S(signal), due(signal))
                            else:
                                signal = "freeD" if last else "dve_step"
                                dve.tensor_copy(row_tmp[0:2, seg % 3, h * 512:h * 512 + 512], b[64 * h:64 * h + 2, :]).then_inc(S(signal), 1)
                                dve.wait_ge(S(signal), due(signal))
                        if seg % 3 != 2:
                            dve.memset(flag, 0.0).then_inc(S("seg_row_ready"), 1)
                            dve.wait_ge(S("seg_row_ready"), due("seg_row_ready"))
                    if seg and (seg - 1) % 3 != 2:
                        done = seg - 1
                        dve.wait_ge(S("fullD"), due("fullD"))
                        b = bank_of("D", T.n["fullD"])
                        col = mod_cols[:, done // 3, 1 - done % 3, :, :]
                        bias = vecs[:, l, 32 + 8 * done:40 + 8 * done].unsqueeze(2).to_broadcast([P, KD, 2])
                        dve.tensor_tensor(col, b[:, 0:16].rearrange("p (k s) -> p k s", s=2), bias, ALU.add).then_inc(S("freeD"), 1)
                        dve.wait_ge(S("freeD"), due("freeD"))
                        if done % 3 == 1:
                            gain = vecs[:, l, 8 * (done // 3):8 * (done // 3) + 8].unsqueeze(2).to_broadcast([P, KD, 2])
                            dve.scalar_tensor_tensor(out=col, in0=col, scalar=1.0, in1=gain, op0=ALU.add, op1=ALU.mult).then_inc(S("dve_step"), 1)
                            dve.wait_ge(S("dve_step"), due("dve_step"))
                dve.memset(flag, 0.0).then_inc(S("mod_ready"), 1)
                dve.wait_ge(S("mod_ready"), due("mod_ready"))

            def modulate(dst, which, streams):
                for k in range(0, KD, 2):
                    dve.wait_ge(S("fullD"), due("fullD"))
                    b = bank_of("D", T.n["fullD"])
                    for s in range(streams):
                        signal = "freeD" if s == streams - 1 else "dve_step"
                        dve.tensor_scalar(dst[:, k, s * SEQ:s * SEQ + SEQ], b[:, s * SEQ:s * SEQ + SEQ],
                                          mod_cols[:, which, 0, k, s:s + 1], mod_cols[:, which, 1, k, s:s + 1],
                                          ALU.mult, ALU.add).then_inc(S(signal), 1)
                        dve.wait_ge(S(signal), due(signal))
                    dve.memset(flag, 0.0).then_inc(S("hT_ready_dve"), 1)
                    dve.wait_ge(S("hT_ready_dve"), due("hT_ready_dve"))

            def heads_norm(t, c0, n, l, which):
                z = Z[:, t, c0:c0 + n * HD]
                z3 = z.rearrange("p (h d) -> p h d", d=HD)
                sq = head_sq[:, 0:n * HD]
                dve.tensor_tensor(sq, z, z, ALU.mult).then_inc(S("dve_step"), 1)
                dve.wait_ge(S("dve_step"), due("dve_step"))
                dve.tensor_reduce(head_ss[:, 0:n], sq.rearrange("p (h d) -> p h d", d=HD), AX, ALU.add).then_inc(S("dve_step"), 1)
                dve.wait_ge(S("dve_step"), due("dve_step"))
                dve.tensor_scalar(head_inv[:, 0:n], head_ss[:, 0:n], 1.0 / HD, EPS, ALU.mult, ALU.add).then_inc(S("dve_step"), 1)
                dve.wait_ge(S("dve_step"), due("dve_step"))
                dve.reciprocal(head_inv[:, 0:n], head_inv[:, 0:n]).then_inc(S("inv_ready"), 1)
                dve.wait_ge(S("inv_ready"), due("inv_ready"))
                dve.wait_ge(S("rstd_ready"), due("rstd_ready"))
                dve.tensor_tensor(z3, z3, head_rstd[:, 0:n].unsqueeze(2).to_broadcast([P, n, HD]), ALU.mult).then_inc(S("dve_step"), 1)
                dve.wait_ge(S("dve_step"), due("dve_step"))
                dve.tensor_tensor(z3, z3, qk_gain[:, l, which, :].unsqueeze(1).to_broadcast([P, n, HD]), ALU.mult).then_inc(S("dve_step"), 1)
                dve.wait_ge(S("dve_step"), due("dve_step"))

            def rope(t, c0, n):
                z = Z[:, t, c0:c0 + n * HD].rearrange("p (h i two) -> p h i two", two=2, i=32)
                x0, x1 = z[:, :, :, 0], z[:, :, :, 1]
                cos = C("rope_cos", 2, 32)[:, t, :].unsqueeze(1).to_broadcast([P, n, 32])
                sin = C("rope_sin", 2, 32)[:, t, :].unsqueeze(1).to_broadcast([P, n, 32])
                tmp = [rope_tmp[:, i, 0:n * 32].rearrange("p (h i) -> p h i", i=32) for i in range(4)]
                for d, (x, c) in zip(tmp, ((x0, cos), (x1, sin), (x0, sin), (x1, cos))):
                    dve.tensor_tensor(d, x, c, ALU.mult).then_inc(S("dve_step"), 1)
                    dve.wait_ge(S("dve_step"), due("dve_step"))
                dve.tensor_tensor(x0, tmp[0], tmp[1], ALU.subtract).then_inc(S("dve_step"), 1)
                dve.wait_ge(S("dve_step"), due("dve_step"))
                dve.tensor_tensor(x1, tmp[2], tmp[3], ALU.add).then_inc(S("dve_step"), 1)
                dve.wait_ge(S("dve_step"), due("dve_step"))

            def split_heads(b, pairs, dst, h0, cols):
                for odd in range(2):
                    src = b[64 * odd:64 * odd + 64, 0:pairs * P].rearrange("p (h i) -> p h i", i=P)
                    yield dst[0:HD, h0 + odd:h0 + 2 * pairs:2, cols:cols + P], src

            def take_q(t):
                for pairs, h0 in ((4, 0), (2, 8)):
                    dve.wait_ge(S("fullD"), due("fullD"))
                    b = bank_of("D", T.n["fullD"])
                    for n, (d, s) in enumerate(split_heads(b, pairs, qT, h0, (t % 2) * P)):
                        signal = "freeD" if n else "dve_step"
                        dve.tensor_copy(d, s).then_inc(S(signal), 1)
                        dve.wait_ge(S(signal), due(signal))
                        dve.memset(flag, 0.0).then_inc(S("qT_ready"), 1)
                        dve.wait_ge(S("qT_ready"), due("qT_ready"))

            def take_k(t):
                dve.wait_ge(S("fullD"), due("fullD"))
                b = bank_of("D", T.n["fullD"])
                for n, (d, s) in enumerate(split_heads(b, 2, kT, 0, t * P)):
                    signal = "freeD" if n else "dve_step"
                    dve.tensor_copy(d, s).then_inc(S(signal), 1)
                    dve.wait_ge(S(signal), due(signal))
                    dve.memset(flag, 0.0).then_inc(S("kT_ready"), 1)
                    dve.wait_ge(S("kT_ready"), due("kT_ready"))

            def attention(s, l):
                nk = 512 if s == 0 else 256
                for t in (2 * s, 2 * s + 1):
                    for grp in range(3):
                        for h in range(4):
                            dve.wait_ge(S("fullD"), due("fullD"))
                            b = bank_of("D", T.n["fullD"])
                            if grp == 2 and s == 0:
                                mask = C("band", 2, 512)[:, t, :]
                            else:
                                mask = zero.to_broadcast([P, nk])
                            low = sinks[:, l, h:h + 1] if grp == 2 else -3.0e38
                            dve.tensor_tensor_reduce(probs[:, h, 0:nk], b[:, 0:nk], mask, SCALE, low, ALU.add, ALU.max,
                                                     row_max[:, h:h + 1]).then_inc(S("freeD"), 1)
                            dve.wait_ge(S("freeD"), due("freeD"))
                        dve.tensor_scalar(row_neg, row_max, -1.0, None, ALU.mult).then_inc(S("scores_ready"), 1)
                        dve.wait_ge(S("scores_ready"), due("scores_ready"))
                        dve.wait_ge(S("exp_ready"), due("exp_ready"))
                        if grp == 2:
                            dve.tensor_tensor(row_sum, row_sum, sink_e, ALU.add).then_inc(S("dve_step"), 1)
                            dve.wait_ge(S("dve_step"), due("dve_step"))
                        dve.reciprocal(row_inv, row_sum).then_inc(S("dve_step"), 1)
                        dve.wait_ge(S("dve_step"), due("dve_step"))
                        for h in range(4):
                            dve.tensor_scalar(probs[:, h, 0:nk], probs[:, h, 0:nk], row_inv[:, h:h + 1], None, ALU.mult).then_inc(S("probs_ready"), 1)
                            dve.wait_ge(S("probs_ready"), due("probs_ready"))
                        dve.wait_ge(S("probs_turned"), due("probs_turned"))

            def mixer(l):
                own = range(TILES) if l == 0 else range(2)
                norm(xn, range(TILES))
                modulate(hT, 0, 2)
                for u in range(3):
                    for t in range(0, TILES, 2):
                        if t in own:
                            dve.wait_ge(S("fullD"), due("fullD"))
                            b = bank_of("D", T.n["fullD"])
                            dve.tensor_copy(Z[:, t, u * 512:u * 512 + 512], b[:, :]).then_inc(S("freeD"), 1)
                            dve.wait_ge(S("freeD"), due("freeD"))
                        elif u:
                            dve.wait_ge(S("fullD"), due("fullD"))
                            b = bank_of("D", T.n["fullD"])
                            dve.tensor_copy(Z[:, t, u * 512 + 256:u * 512 + 512], b[:, 0:256]).then_inc(S("freeD"), 1)
                            dve.wait_ge(S("freeD"), due("freeD"))
                dve.memset(flag, 0.0).then_inc(S("z_ready_dve"), 1)
                dve.wait_ge(S("z_ready_dve"), due("z_ready_dve"))
                dve.wait_ge(S("z_ready_act_v"), due("z_ready_act_v"))
                for s in range(len(own) // 2):
                    for c in range(2):
                        dve.wait_ge(S("fullD"), due("fullD"))
                        b = bank_of("D", T.n["fullD"])
                        dve.tensor_copy(four[:, c, :], b[:, :]).then_inc(S("freeD"), 1)
                        dve.wait_ge(S("freeD"), due("freeD"))
                        dve.memset(flag, 0.0).then_inc(S("four_ready"), 1)
                        dve.wait_ge(S("four_ready"), due("four_ready"))
                    dve.wait_ge(S("fT_done"), due("fT_done", 2))
                for t in range(TILES):
                    if t in own:
                        heads_norm(t, GQ, 8, l, 0)
                    heads_norm(t, GK, 2, l, 1)
                    if t < 2:
                        rope(t, GQ, 10)
                        rope(t, WQ, 6)
                dve.memset(flag, 0.0).then_inc(S("rope_ready"), 1)
                dve.wait_ge(S("rope_ready"), due("rope_ready"))
                for t in range(2):
                    take_q(t)
                for t in range(TILES):
                    take_k(t)
                for s in range(len(own) // 2):
                    if s == 1:
                        for t in (2, 3):
                            take_q(t)
                    attention(s, l)
                for n in range(2):
                    for br in range(3):
                        for t in own:
                            dve.wait_ge(S("sig_ready"), due("sig_ready"))
                            dve.wait_ge(S("fullD"), due("fullD"))
                            b = bank_of("D", T.n["fullD"])
                            dst = m_sum[:, t, n * 512:n * 512 + 512]
                            if br == 0:
                                dve.tensor_tensor(dst, b[:, :], sig[:, t, :], ALU.mult).then_inc(S("freeD"), 1)
                                dve.wait_ge(S("freeD"), due("freeD"))
                            else:
                                dve.tensor_tensor(prod[:, t, :], b[:, :], sig[:, t, :], ALU.mult).then_inc(S("freeD"), 1)
                                dve.wait_ge(S("freeD"), due("freeD"))
                                dve.tensor_tensor(dst, dst, prod[:, t, :], ALU.add).then_inc(S("dve_step"), 1)
                                dve.wait_ge(S("dve_step"), due("dve_step"))
                            dve.memset(flag, 0.0).then_inc(S("sig_used"), 1)
                            dve.wait_ge(S("sig_used"), due("sig_used"))
                for s in range(len(own) // 2):
                    for n in range(2):
                        dve.wait_ge(S("fullD"), due("fullD"))
                        b = bank_of("D", T.n["fullD"])
                        dve.tensor_copy(gate_b[:, s, n * 512:n * 512 + 512], b[:, :]).then_inc(S("freeD"), 1)
                        dve.wait_ge(S("freeD"), due("freeD"))
                dve.memset(flag, 0.0).then_inc(S("m_ready"), 1)
                dve.wait_ge(S("m_ready"), due("m_ready"))
                for k in range(0, KD, 2):
                    dve.wait_ge(S("fullD"), due("fullD"))
                    b = bank_of("D", T.n["fullD"])
                    dve.tensor_copy(mT[:, k, 0:P * len(own)], b[:, 0:P * len(own)]).then_inc(S("freeD"), 1)
                    dve.wait_ge(S("freeD"), due("freeD"))
                    dve.memset(flag, 0.0).then_inc(S("mT_ready_dve"), 1)
                    dve.wait_ge(S("mT_ready_dve"), due("mT_ready_dve"))
                for n in range(2):
                    for t in own:
                        dve.wait_ge(S("fullD"), due("fullD"))
                        b = bank_of("D", T.n["fullD"])
                        add_gated(b, gate_b, prod[:, t, :], t, n)

            def add_gated(b, gate, tmp, t, n):
                x = X[:, t, n * 512:n * 512 + 512]
                dve.tensor_tensor(tmp, b[:, :], gate[:, stream_of(t), n * 512:n * 512 + 512], ALU.mult).then_inc(S("freeD"), 1)
                dve.wait_ge(S("freeD"), due("freeD"))
                dve.tensor_tensor(x, x, tmp, ALU.add).then_inc(S("dve_step"), 1)
                dve.wait_ge(S("dve_step"), due("dve_step"))

            def experts(l):
                ns = 2 if l == 0 else 1
                nt = 2 * ns
                norm(xn2, range(nt))
                modulate(h2T, 1, ns)
                dve.wait_ge(S("fullD"), due("fullD"))
                b = bank_of("D", T.n["fullD"])
                lg = b[:, 0:nt * E].rearrange("p (t e) -> p t e", e=E)
                dve.tensor_reduce(aff_m[:, 0:nt], lg, AX, ALU.max).then_inc(S("dve_step"), 1)
                dve.wait_ge(S("dve_step"), due("dve_step"))
                dve.tensor_tensor(logit[:, 0:nt, :], lg, aff_m[:, 0:nt].unsqueeze(2).to_broadcast([P, nt, E]),
                                  ALU.subtract).then_inc(S("freeD"), 1)
                dve.wait_ge(S("freeD"), due("freeD"))
                dve.memset(flag, 0.0).then_inc(S("logits_ready"), 1)
                dve.wait_ge(S("logits_ready"), due("logits_ready"))
                for s in range(ns):
                    for n in range(2):
                        dve.wait_ge(S("fullD"), due("fullD"))
                        b = bank_of("D", T.n["fullD"])
                        dve.tensor_copy(gate2_b[:, s, n * 512:n * 512 + 512], b[:, :]).then_inc(S("freeD"), 1)
                        dve.wait_ge(S("freeD"), due("freeD"))
                dve.memset(flag, 0.0).then_inc(S("gate_rows_used"), 1)
                dve.wait_ge(S("gate_rows_used"), due("gate_rows_used"))
                dve.wait_ge(S("aff_exp_ready"), due("aff_exp_ready"))
                dve.tensor_reduce(aff_s[:, 0:nt], logit[:, 0:nt, :], AX, ALU.add).then_inc(S("dve_step"), 1)
                dve.wait_ge(S("dve_step"), due("dve_step"))
                dve.reciprocal(aff_i[:, 0:nt], aff_s[:, 0:nt]).then_inc(S("dve_step"), 1)
                dve.wait_ge(S("dve_step"), due("dve_step"))
                dve.tensor_tensor(aff[:, 0:nt, :], logit[:, 0:nt, :],
                                  aff_i[:, 0:nt].unsqueeze(2).to_broadcast([P, nt, E]), ALU.mult).then_inc(S("aff_ready"), 1)
                dve.wait_ge(S("aff_ready"), due("aff_ready"))
                dve.wait_ge(S("fullD"), due("fullD"))
                b = bank_of("D", T.n["fullD"])
                dve.tensor_copy(work[0:E, 0:nt * P], b[0:E, 0:nt * P]).then_inc(S("freeD"), 1)
                dve.wait_ge(S("freeD"), due("freeD"))
                for s in range(ns):
                    w = work[0:E, s * SEQ:s * SEQ + SEQ]
                    for _ in range(CAP // 8):
                        dve.max(best[0:E, :], w).then_inc(S("dve_step"), 1)
                        dve.wait_ge(S("dve_step"), due("dve_step"))
                        dve.match_replace(w, best[0:E, :], w, -1.0).then_inc(S("dve_step"), 1)
                        dve.wait_ge(S("dve_step"), due("dve_step"))
                    dve.tensor_scalar(w, w, 0.0, None, ALU.is_lt).then_inc(S("dve_step"), 1)
                    dve.wait_ge(S("dve_step"), due("dve_step"))
                    c = cum[0:E, s * SEQ:s * SEQ + SEQ]
                    dve.tensor_tensor_scan(affT[0:E, s * SEQ:s * SEQ + SEQ], w, w, 0.0, ALU.add, ALU.max).then_inc(S("dve_step"), 1)
                    dve.wait_ge(S("dve_step"), due("dve_step"))
                    dve.tensor_tensor(c, affT[0:E, s * SEQ:s * SEQ + SEQ], w, ALU.mult).then_inc(S("dve_step"), 1)
                    dve.wait_ge(S("dve_step"), due("dve_step"))
                    dve.tensor_scalar(c, c, -1.0, None, ALU.add).then_inc(S("dve_step"), 1)
                    dve.wait_ge(S("dve_step"), due("dve_step"))
                dve.memset(flag, 0.0).then_inc(S("slots_ready"), 1)
                dve.wait_ge(S("slots_ready"), due("slots_ready"))
                dve.wait_ge(S("fullD"), due("fullD"))
                b = bank_of("D", T.n["fullD"])
                dve.tensor_copy(slot_t[:, 0:nt, :], b[:, 0:nt * E].rearrange("p (t e) -> p t e", e=E)).then_inc(S("freeD"), 1)
                dve.wait_ge(S("freeD"), due("freeD"))
                for t in range(nt):
                    pk = pick[:, t, :].rearrange("p (e c) -> p e c", c=CAP)
                    dve.tensor_tensor(pk, slot_t[:, t, :].unsqueeze(2).to_broadcast([P, E, CAP]),
                                      C("iota").unsqueeze(1).to_broadcast([P, E, CAP]), ALU.is_equal).then_inc(S("dve_step"), 1)
                    dve.wait_ge(S("dve_step"), due("dve_step"))
                    dve.tensor_tensor(pick_g[:, t, :].rearrange("p (e c) -> p e c", c=CAP), pk,
                                      aff[:, t, :].unsqueeze(2).to_broadcast([P, E, CAP]), ALU.mult).then_inc(S("dve_step"), 1)
                    dve.wait_ge(S("dve_step"), due("dve_step"))
                dve.memset(flag, 0.0).then_inc(S("pick_ready"), 1)
                dve.wait_ge(S("pick_ready"), due("pick_ready"))
                for k in range(KD):
                    if ns == 1 and k % 2:
                        continue
                    dve.wait_ge(S("fullD"), due("fullD"))
                    b = bank_of("D", T.n["fullD"])
                    dve.tensor_scalar(xgT[:, k, :, 0:CAP], b[:, :].rearrange("p (e c) -> p e c", c=CAP),
                                      mod_cols[:, 1, 0, k, 0:1], mod_cols[:, 1, 1, k, 0:1], ALU.mult, ALU.add).then_inc(S("freeD"), 1)
                    dve.wait_ge(S("freeD"), due("freeD"))
                dve.wait_ge(S("xgT_done"), due("xgT_done"))
                for t in range(nt):
                    dve.wait_ge(S("fullD"), due("fullD"))
                    b = bank_of("D", T.n["fullD"])
                    dve.tensor_copy(putT[:, t, :, :], b[:, :].rearrange("p (g i) -> p g i", g=4)).then_inc(S("freeD"), 1)
                    dve.wait_ge(S("freeD"), due("freeD"))
                R = CAP * ns
                per = {"fullD": 12 + 4 * ns, "silu_ready": 8, "dve_step": None, "freeD": 12 + 4 * ns, "xgs_ready": 1,
                       "puts_ready": 1, "hid_ready": 8, "hidT_ready": 4}
                per["dve_step"] = 4 * ns
                with dve.Fori(0, 4) as i:
                    T.enter(i, per)
                    src = xgT.rearrange("p k (g j) r -> p k g j r", j=4)
                    dve.tensor_copy(xgs[:, :, :, 0:R], src[:, :, i, :, 0:R]).then_inc(S("xgs_ready"), 1)
                    dve.wait_ge(S("xgs_ready"), due("xgs_ready"))
                    dve.tensor_copy(puts[:, 0:nt, :], putT[:, 0:nt, i, :]).then_inc(S("puts_ready"), 1)
                    dve.wait_ge(S("puts_ready"), due("puts_ready"))
                    for j in range(4):
                        for n in range(2):
                            dve.wait_ge(S("silu_ready"), due("silu_ready"))
                            dve.wait_ge(S("fullD"), due("fullD"))
                            b = bank_of("D", T.n["fullD"])
                            dve.tensor_tensor(hid[0:R, n * 512:n * 512 + 512], b[64:64 + R, :], silu_g[0:R, n, :], ALU.mult).then_inc(S("hid_ready"), 1)
                            dve.wait_ge(S("hid_ready"), due("hid_ready"))
                            dve.memset(flag, 0.0).then_inc(S("freeD"), 1)
                            dve.wait_ge(S("freeD"), due("freeD"))
                        dve.wait_ge(S("fullD"), due("fullD"))
                        b = bank_of("D", T.n["fullD"])
                        dve.tensor_copy(hidT[:, :, 0:R], b[:, :].rearrange("p (k r) -> p k r", r=64)[:, :, 0:R]).then_inc(S("hidT_ready"), 1)
                        dve.wait_ge(S("hidT_ready"), due("hidT_ready"))
                        dve.memset(flag, 0.0).then_inc(S("freeD"), 1)
                        dve.wait_ge(S("freeD"), due("freeD"))
                    for t in range(nt):
                        for n in range(2):
                            dve.wait_ge(S("fullD"), due("fullD"))
                            b = bank_of("D", T.n["fullD"])
                            add_gated(b, gate2_b, scat, t, n)
                T.leave(4)

            dve.memset(small[:, :], 0.0).then_inc(S("dve_step"), 1)
            dve.wait_ge(S("dve_step"), due("dve_step"))
            for _ in range(POOL):
                dve.memset(flag, 0.0).then_inc(S("freeD"), 1)
                dve.wait_ge(S("freeD"), due("freeD"))
            dve.memset(ones, 1.0).then_inc(S("small_ready"), 1)
            dve.wait_ge(S("small_ready"), due("small_ready"))
            dve.memset(flag, 0.0).then_inc(S("small_ready_a"), 1)
            dve.wait_ge(S("small_ready_a"), due("small_ready_a"))
            dve.wait_ge(S("const_landed"), 16)
            dve.wait_ge(S("fullD"), due("fullD"))
            b = bank_of("D", T.n["fullD"])
            for v in range(4):
                dve.tensor_copy(vecs[:, v, 0:VEC_ROWS[v]], b[:, v * P:v * P + VEC_ROWS[v]]).then_inc(S("dve_step"), 1)
                dve.wait_ge(S("dve_step"), due("dve_step"))
            dve.memset(flag, 0.0).then_inc(S("vecs_ready"), 1)
            dve.wait_ge(S("vecs_ready"), due("vecs_ready"))
            dve.wait_ge(S("smalls_landed"), 16 * N_SMALL)
            dve.wait_ge(S("x_landed"), 16 * 2)
            dve.memset(flag, 0.0).then_inc(S("freeD"), 1)
            dve.wait_ge(S("freeD"), due("freeD"))
            for l in range(DEPTH):
                modulation(l)
                mixer(l)
                experts(l)
            dve_block2(dve, T, norm, modulation, modulate, add_gated)

        @block.scalar
        def _(act):
            T = Tally()
            due = T.step

            def norm(n):
                act.wait_ge(S("inv_ready"), due("inv_ready"))
                act.activation(rstd[:, 0:n], inv[:, 0:n], ACT.Sqrt).then_inc(S("rstd_ready"), 1)
                act.wait_ge(S("rstd_ready"), due("rstd_ready"))

            def heads_norm(n):
                act.wait_ge(S("inv_ready"), due("inv_ready"))
                act.activation(head_rstd[:, 0:n], head_inv[:, 0:n], ACT.Sqrt).then_inc(S("rstd_ready"), 1)
                act.wait_ge(S("rstd_ready"), due("rstd_ready"))

            def modulate(dst, which, streams):
                for k in range(1, KD, 2):
                    act.wait_ge(S("fullA"), due("fullA"))
                    b = bank_of("A", T.n["fullA"])
                    for s in range(streams):
                        signal = "freeA" if s == streams - 1 else "act_step"
                        act.activation(dst[:, k, s * SEQ:s * SEQ + SEQ], b[:, s * SEQ:s * SEQ + SEQ], ACT.Identity,
                                       scale=mod_cols[:, which, 0, k, s:s + 1], bias=mod_cols[:, which, 1, k, s:s + 1]).then_inc(S(signal), 1)
                        act.wait_ge(S(signal), due(signal))
                    act.activation(flag_a, zero, ACT.Copy).then_inc(S("hT_ready_act"), 1)
                    act.wait_ge(S("hT_ready_act"), due("hT_ready_act"))

            def attention(s, l):
                nk = 512 if s == 0 else 256
                keys = range(TILES) if s == 0 else range(2, TILES)
                for t in (2 * s, 2 * s + 1):
                    for grp in range(3):
                        act.wait_ge(S("scores_ready"), due("scores_ready"))
                        for h in range(4):
                            act.activation(probs[:, h, 0:nk], probs[:, h, 0:nk], ACT.Exp, bias=row_neg[:, h:h + 1],
                                           accum_out=row_sum[:, h:h + 1]).then_inc(S("act_step"), 1)
                            act.wait_ge(S("act_step"), due("act_step"))
                            if grp == 2:
                                act.activation(sink_e[:, h:h + 1], sinks[:, l, h:h + 1], ACT.Exp, bias=row_neg[:, h:h + 1]).then_inc(S("act_step"), 1)
                                act.wait_ge(S("act_step"), due("act_step"))
                        act.activation(flag_a, zero, ACT.Copy).then_inc(S("exp_ready"), 1)
                        act.wait_ge(S("exp_ready"), due("exp_ready"))
                        for kt in keys:
                            act.wait_ge(S("fullA"), due("fullA"))
                            b = bank_of("A", T.n["fullA"])
                            act.activation(probsT[:, kt, :], b[:, :], ACT.Copy).then_inc(S("freeA"), 1)
                            act.wait_ge(S("freeA"), due("freeA"))
                            if kt == keys[-1]:
                                act.activation(flag_a, zero, ACT.Copy).then_inc(S("probs_turned"), 1)
                                act.wait_ge(S("probs_turned"), due("probs_turned"))
                            act.activation(flag_a, zero, ACT.Copy).then_inc(S("probsT_ready"), 1)
                            act.wait_ge(S("probsT_ready"), due("probsT_ready"))
                        act.wait_ge(S("fullA"), due("fullA"))
                        b = bank_of("A", T.n["fullA"])
                        for odd in range(2):
                            src = b[0:HD, :].rearrange("p (a two i) -> p a two i", two=2, i=P)[:, :, odd, :]
                            signal = "freeA" if odd else "act_step"
                            act.activation(oT[64 * odd:64 * odd + 64, 2 * grp:2 * grp + 2, t * P:t * P + P], src, ACT.Copy).then_inc(S(signal), 1)
                            act.wait_ge(S(signal), due(signal))
                            act.activation(flag_a, zero, ACT.Copy).then_inc(S("oT_ready"), 1)
                            act.wait_ge(S("oT_ready"), due("oT_ready"))

            def mixer(l):
                own = range(TILES) if l == 0 else range(2)
                norm(TILES)
                modulate(hT, 0, 2)
                for u in range(3):
                    for t in range(1, TILES, 2):
                        if t in own:
                            act.wait_ge(S("fullA"), due("fullA"))
                            b = bank_of("A", T.n["fullA"])
                            act.activation(Z[:, t, u * 512:u * 512 + 512], b[:, :], ACT.Copy).then_inc(S("freeA"), 1)
                            act.wait_ge(S("freeA"), due("freeA"))
                        elif u:
                            act.wait_ge(S("fullA"), due("fullA"))
                            b = bank_of("A", T.n["fullA"])
                            act.activation(Z[:, t, u * 512 + 256:u * 512 + 512], b[:, 0:256], ACT.Copy).then_inc(S("freeA"), 1)
                            act.wait_ge(S("freeA"), due("freeA"))
                act.activation(flag_a, zero, ACT.Copy).then_inc(S("z_ready_act"), 1)
                act.wait_ge(S("z_ready_act"), due("z_ready_act"))
                act.activation(flag_a, zero, ACT.Copy).then_inc(S("z_ready_act_v"), 1)
                act.wait_ge(S("z_ready_act_v"), due("z_ready_act_v"))
                for s in range(len(own) // 2):
                    for c in range(2):
                        act.wait_ge(S("fullA"), due("fullA"))
                        b = bank_of("A", T.n["fullA"])
                        act.activation(fT[:, c, s * SEQ:s * SEQ + SEQ], b[:, 0:SEQ], ACT.Copy).then_inc(S("freeA"), 1)
                        act.wait_ge(S("freeA"), due("freeA"))
                        act.activation(flag_a, zero, ACT.Copy).then_inc(S("fT_done"), 1)
                        act.wait_ge(S("fT_done"), due("fT_done"))
                        act.activation(flag_a, zero, ACT.Copy).then_inc(S("fT_ready"), 1)
                        act.wait_ge(S("fT_ready"), due("fT_ready"))
                for t in range(TILES):
                    if t in own:
                        heads_norm(8)
                    heads_norm(2)
                for s in range(len(own) // 2):
                    attention(s, l)
                for n in range(2):
                    for br in range(3):
                        for t in own:
                            if n or br:
                                act.wait_ge(S("sig_used"), due("sig_used"))
                            act.wait_ge(S("fullA"), due("fullA"))
                            b = bank_of("A", T.n["fullA"])
                            act.activation(sig[:, t, :], b[:, :], ACT.Sigmoid).then_inc(S("freeA"), 1)
                            act.wait_ge(S("freeA"), due("freeA"))
                            act.activation(flag_a, zero, ACT.Copy).then_inc(S("sig_ready"), 1)
                            act.wait_ge(S("sig_ready"), due("sig_ready"))
                act.wait_ge(S("sig_used"), due("sig_used", len(own)))
                for k in range(1, KD, 2):
                    act.wait_ge(S("fullA"), due("fullA"))
                    b = bank_of("A", T.n["fullA"])
                    act.activation(mT[:, k, 0:P * len(own)], b[:, 0:P * len(own)], ACT.Copy).then_inc(S("freeA"), 1)
                    act.wait_ge(S("freeA"), due("freeA"))
                    act.activation(flag_a, zero, ACT.Copy).then_inc(S("mT_ready_act"), 1)
                    act.wait_ge(S("mT_ready_act"), due("mT_ready_act"))

            def experts(l):
                ns = 2 if l == 0 else 1
                nt = 2 * ns
                norm(nt)
                modulate(h2T, 1, ns)
                act.wait_ge(S("logits_ready"), due("logits_ready"))
                act.activation(logit[:, 0:nt, :], logit[:, 0:nt, :], ACT.Exp).then_inc(S("aff_exp_ready"), 1)
                act.wait_ge(S("aff_exp_ready"), due("aff_exp_ready"))
                for k in range(KD):
                    if ns == 1 and k % 2 == 0:
                        continue
                    s = ns - 1
                    act.wait_ge(S("fullA"), due("fullA"))
                    b = bank_of("A", T.n["fullA"])
                    act.activation(xgT[:, k, :, CAP * s:CAP * s + CAP], b[:, :].rearrange("p (e c) -> p e c", c=CAP),
                                   ACT.Identity, scale=mod_cols[:, 1, 0, k, s:s + 1], bias=mod_cols[:, 1, 1, k, s:s + 1]).then_inc(S("freeA"), 1)
                    act.wait_ge(S("freeA"), due("freeA"))
                act.activation(flag_a, zero, ACT.Copy).then_inc(S("xgT_done"), 1)
                act.wait_ge(S("xgT_done"), due("xgT_done"))
                R = CAP * ns
                per = {"fullA": 4, "silu_ready": 8, "act_step": 4 * (2 * ns - 1), "freeA": 4, "out_ready": 4}
                with act.Fori(0, 4) as i:
                    T.enter(i, per)
                    for j in range(4):
                        for n in range(2):
                            job = expert_start[l] + 3 * j + n
                            act.wait_ge(S("fullD"), i * (12 + 4 * ns) + job + 1)
                            bD = pool_banks["D"][job % POOL]
                            act.activation(silu_g[0:R, n, :], bD[0:R, :], ACT.Silu).then_inc(S("silu_ready"), 1)
                            act.wait_ge(S("silu_ready"), due("silu_ready"))
                        act.wait_ge(S("fullA"), due("fullA"))
                        b = bank_of("A", T.n["fullA"])
                        for n in range(2):
                            for s in range(ns):
                                last = n == 1 and s == ns - 1
                                signal = "freeA" if last else "act_step"
                                act.activation(out_g[CAP * j:CAP * j + CAP, s, n * 512:n * 512 + 512],
                                               b[64 * n + CAP * s:64 * n + CAP * s + CAP, :], ACT.Copy).then_inc(S(signal), 1)
                                act.wait_ge(S(signal), due(signal))
                        act.activation(flag_a, zero, ACT.Copy).then_inc(S("out_ready"), 1)
                        act.wait_ge(S("out_ready"), due("out_ready"))
                T.leave(4)

            act.dma_start(X[:, 0:2, :], A["x"][0].rearrange("(t p) n -> p t n", p=P)).then_inc(S("x_landed"), 16)
            act.dma_start(X[:, 2:4, :], A["ctx"][0].rearrange("(t p) n -> p t n", p=P)).then_inc(S("x_landed"), 16)
            for dst, src in vec_loads:
                act.dma_start(dst, src).then_inc(S("vecs_landed"), 16)
            for dst, src in small_loads:
                act.dma_start(dst, src).then_inc(S("smalls_landed"), 16)
            act.wait_ge(S("small_ready_a"), due("small_ready_a"))
            for _ in range(POOL):
                act.activation(flag_a, zero, ACT.Copy).then_inc(S("freeA"), 1)
                act.wait_ge(S("freeA"), due("freeA"))
            act.wait_ge(S("vecs_ready"), due("vecs_ready"))
            for l in range(3):
                for s in range(2):
                    act.activation(silu_c[:, l, :, s], vecs[:, l, 16 + 8 * s:24 + 8 * s], ACT.Silu).then_inc(S("silu_c_ready"), 1)
                    act.wait_ge(S("silu_c_ready"), due("silu_c_ready"))
            for l in range(DEPTH):
                mixer(l)
                experts(l)
            act_block2(act, T, norm, modulate)


_INS = ("x c ctx c_ctx w_ada b_ada norm1_g w_in q_norm_g k_norm_g sink w_br_fourier w_br_global w_br_window w_out "
        "norm2_g w_router w_gate_e w_up_e w_down_e final_g c_2 ctx_2 c_ctx_2 w_mod_2 b_mod_2 norm_mix_pre_2 "
        "norm_mix_post_2 norm_ffn_pre_2 norm_ffn_post_2 w_in_2 conv_w_2 conv_b_2 gla_wg_f_2 gla_bg_f_2 gla_wg_b_2 "
        "gla_bg_b_2 gla_norm_2 a_log_f_2 a_log_b_2 dt_bias_f_2 dt_bias_b_2 d_skip_2 ssd_norm_2 w_out_2 w_gate_2 "
        "w_up_2 w_down_2").split()


def kernel(**inputs):
    import concourse.bacc as _bacc
    from concourse.bass_utils import run_bass_kernel_spmd as _run

    nc = _bacc.Bacc("TRN2", target_bir_lowering=False, num_devices=1)
    arrays, A = {}, {}
    for name, a in [("const", constants())] + [(n, inputs[n]) for n in _INS]:
        a = np.ascontiguousarray(a)
        arrays[f"in_{name}"] = a
        A[name] = nc.dram_tensor(f"in_{name}", a.shape, mybir.dt.from_np(a.dtype), kind="ExternalInput").ap()
    out = nc.dram_tensor("out", (1, SEQ, D), F32, kind="ExternalOutput").ap()
    build(nc, A, out)
    r = _run(nc, [arrays], core_ids=[0])
    return r.results[0]["out"]
```

```python
from contextlib import ExitStack

import numpy as np

import concourse.bass as bass
from concourse import mybir

F32 = mybir.dt.float32
ACT = mybir.ActivationFunctionType
ALU = mybir.AluOpType
AX = mybir.AxisListType.X

P = 128
D = 1024
KD = D // P
SEQ = 256
TILES = 4
DEPTH = 2
E = 16
CAP = 2 * SEQ // E
HD = 64
EPS = 1e-6
RING = 4
POOL = 4
SLOT = KD * 512
SCALE = HD ** -0.5

Z_W = 1536
GQ, GK, GV, WQ, WK, WV = 256, 768, 896, 1024, 1280, 1408
B_Q, B_K, B_V, B_R, B_LR, B_Z, B_X, B_DT, B_END = 0, 256, 512, 1024, 1536, 1568, 2080, 2848, 2864
D_FF = 2816
FB = D_FF // P


CONST = {}


def constants():
    parts, at = [], 0

    def put(name, a):
        nonlocal at
        a = np.asarray(a, np.float64).reshape(a.shape[0], -1)
        full = np.zeros((P, a.shape[1]))
        full[: a.shape[0]] = a
        CONST[name] = (at, a.shape[1])
        at += a.shape[1]
        parts.append(full)

    put("ident", np.eye(P))
    n = np.arange(SEQ)
    ang = 2 * np.pi * ((n[:, None] * n[None]) % SEQ) / SEQ
    norm = 1 / np.sqrt(SEQ * HD)
    cs = np.concatenate([np.cos(ang), np.sin(ang)], 1) * norm
    put("dft_pos", cs.reshape(2, P, 512).transpose(1, 0, 2))
    c = np.arange(HD)
    ang = 2 * np.pi * ((c[:, None] * c[None]) % HD) / HD
    put("dft_cos", np.kron(np.eye(2), np.cos(ang)))
    put("dft_nsin", -np.kron(np.eye(2), np.sin(ang)))
    mask = np.zeros((2, P, 512))
    q, k = np.arange(SEQ)[:, None], np.arange(SEQ)[None]
    mask[:, :, :SEQ] = np.where(abs(q - k) <= 128, 0, -1e30 / SCALE).reshape(2, P, SEQ)
    put("band", mask.transpose(1, 0, 2))
    t = np.arange(SEQ)
    inv = np.float32(10000.0) ** (-np.arange(0, 32, 2, dtype=np.float32) / np.float32(32))
    ang = np.concatenate([(t // 64).astype(np.float32)[:, None] * inv, (t % 64).astype(np.float32)[:, None] * inv], 1)
    put("rope_cos", np.cos(ang).reshape(2, P, 32).transpose(1, 0, 2))
    put("rope_sin", np.sin(ang).reshape(2, P, 32).transpose(1, 0, 2))
    put("iota", np.tile(np.arange(CAP), (P, 1)))
    j, i = np.arange(P)[:, None], np.arange(P)[None]
    put("after", j <= i)
    put("before", j >= i)
    put("twice", 2.0 * np.eye(P))
    lev = []
    for l in range(1, 8):
        half = 1 << (l - 1)
        lev.append(((j >> l) == (i >> l)) & (((j // half) & 1) != ((i // half) & 1)))
    put("levels", np.stack(lev, 1))
    return np.concatenate(parts, 1).astype(np.float32)


def mod_steps():
    order = [(l, seg) for l in range(3) for seg in range(6)]
    early = [(order[0], None), (order[1], order[0]), (None, order[1])]
    late = []
    for n, (l, seg) in enumerate(order[2:], 2):
        last = order[n - 1]
        late.append(((l, seg), last if n > 2 and last[1] % 3 != 2 else None))
    return early, {0: late[:12], 1: late[12:]}


class Tally:

    def __init__(self):
        self.n, self.per, self.i = {}, None, None

    def step(self, name, k=1):
        self.n[name] = self.n.get(name, 0) + k
        return self.value(name)

    def value(self, name, less=0):
        v = self.n.get(name, 0) - less
        return v if self.per is None else v + self.i * self.per[name]

    def enter(self, i, per):
        self.i, self.per, self.start = i, per, dict(self.n)

    def leave(self, turns):
        for name, k in self.per.items():
            got = self.n.get(name, 0) - self.start.get(name, 0)
            assert got == k, (name, got, k)
            self.n[name] = self.start.get(name, 0) + k * turns
        self.per = None


def stream_of(t):
    return t // 2


def build(nc: bass.Bass, A, out):
    with ExitStack() as ctx:
        def sb(name, *shape):
            return ctx.enter_context(nc.sbuf_tensor(name, [P, *shape], F32))

        class Sems:
            def __init__(self):
                self.made = {}

            def __call__(self, name):
                if name not in self.made:
                    self.made[name] = ctx.enter_context(nc.semaphore(name))
                return self.made[name]

        S = Sems()

        X = sb("x_tokens", TILES, D)
        ring = sb("weight_ring", RING, SLOT)
        const = sb("const", sum(n for _, n in CONST.values()))
        gate_rows = sb("gate_rows", 2, D)
        row_tmp = gate_rows[96:98]
        arena = sb("arena", 23552)
        vec_in = sb("vec_in", 4, P)
        vecs = sb("vecs", 4, P)
        silu_c = sb("silu_c", 3, KD, 2)
        mod_cols = sb("mod_cols", 3 * 2, 2, KD, 2)
        w_router = sb("w_router", 2, KD, E)
        qk_gain = sb("qk_gain", 2, 2, HD)
        sinks = sb("sinks", 2, 4)
        small = sb("small", 256)
        banks = [ctx.enter_context(nc.psum_tensor(f"bank{i}", [P, 512], F32)) for i in range(2 * POOL)]
        pool_banks = {"D": banks[:POOL], "A": banks[POOL:]}

        def bank_of(pool, n):
            return pool_banks[pool][(n - 1) % POOL]

        def C(name, *dims):
            at, n = CONST[name]
            v = const[:, at:at + n]
            if len(dims) == 2:
                v = v.rearrange("p (a b) -> p a b", a=dims[0])
            return v

        def area(at, *dims):
            n = int(np.prod(dims))
            v = arena[:, at:at + n]
            if len(dims) == 2:
                v = v.rearrange("p (a b) -> p a b", a=dims[0])
            if len(dims) == 3:
                v = v.rearrange("p (a b c) -> p a b c", a=dims[0], b=dims[1])
            return v

        ident = C("ident")
        zero = small[:, 0:1]
        flag, flag_a = small[:, 2:3], small[:, 3:4]
        ones = small[:, 1:2]
        ss, inv, rstd = small[:, 4:8], small[:, 8:12], small[:, 12:16]

        hT = area(0, KD, 512)
        xn = area(4096, TILES, D)
        Z = area(4096, TILES, Z_W)
        qT = area(10240, 12, SEQ)
        kT = area(13312, 4, 512)
        probs_buf = (area(15360, 4, 512), Z[:, :, 0:512])
        probsT = area(17408, 4, 512)
        oT = area(19456, 6, 512)
        fT = area(22528, 2, 512)
        head_sq = area(15360, 640)
        rope_tmp = area(17408, 4, 320)
        four = area(15360, 2, 512)
        m_sum = area(4096, TILES, D)
        mT = area(0, KD, 512)
        sig = area(15360, 4, 512)
        prod = area(10240, 4, 512)
        sq = area(12288, D)
        gate_b = area(17408, 2, D)
        head_ss = small[:, 16:26]
        head_inv = small[:, 26:36]
        head_rstd = small[:, 36:46]
        row_max, row_sum, sink_e, row_inv = (small[:, 48 + 4 * i:52 + 4 * i] for i in range(4))
        row_neg = (small[:, 64:68], small[:, 68:72])
        xn2 = area(0, TILES, D)
        h2T = area(4096, KD, 512)
        xgT = area(4096, KD, E, 64)
        pick = area(12288, TILES, 512)
        pick_g = area(14336, TILES, 512)
        putT = area(16384, TILES, 4, P)
        gate2_b = area(18432, 2, D)
        hidT = area(20480, KD, 64)
        affT, work, cum = area(20992, 512), area(21504, 512), area(22016, 512)
        aff = area(22528, TILES, E)
        slot_t = area(22592, TILES, E)
        logit = area(22656, TILES, E)
        best = area(22720, 8)
        aff_m, aff_s, aff_i = area(22736, 4), area(22740, 4), area(22744, 4)
        scat = area(23040, 512)
        out_g = area(0, 2, D)
        silu_g = area(2048, 2, 512)
        hid = area(3072, D)
        xgs = area(12288, KD, 4, 64)
        puts = area(14336, TILES, P)

        def rows(ap):
            return ap.rearrange("(k p) -> k p", p=P)

        vec_loads = []
        for l in range(DEPTH):
            for at, ap in ((0, A["norm1_g"][l]), (8, A["norm2_g"][l]), (16, A["c"][0]), (24, A["c_ctx"]), (32, A["b_ada"][l])):
                n = ap.shape[0] // P
                vec_loads.append((vec_in[at:at + n, l, :], rows(ap)))
        for at, ap in ((0, A["norm_mix_pre_2"][0]), (8, A["norm_ffn_pre_2"][0]), (16, A["c_2"][0]), (24, A["c_ctx_2"]),
                       (32, A["b_mod_2"][0]), (80, A["conv_b_2"][0]), (86, A["gla_bg_f_2"][0]), (88, A["gla_bg_b_2"][0])):
            vec_loads.append((vec_in[at:at + ap.shape[0] // P, 2, :], rows(ap)))
        vec_loads.append((vec_in[0:54, 3, :], A["conv_w_2"][0].rearrange("y x (k p) -> (y x k) p", p=P)))
        VEC_ROWS = (80, 80, 90, 54)
        small_loads = []
        for l in range(DEPTH):
            small_loads.append((w_router[:, l, :, :], A["w_router"][l].rearrange("(k p) e -> p k e", p=P)))
            small_loads.append((qk_gain[:, l, 0, :], A["q_norm_g"][l].partition_broadcast(P)))
            small_loads.append((qk_gain[:, l, 1, :], A["k_norm_g"][l].partition_broadcast(P)))
            small_loads.append((sinks[:, l, :], A["sink"][l].partition_broadcast(P)))
        N_VEC, N_SMALL = len(vec_loads), len(small_loads)

        block = ctx.enter_context(nc.Block())
        released = []
        expert_start = {}

        def big(w, c0, c1):
            return w[:, c0:c1].rearrange("(k p) n -> p k n", p=P)

        def slot_view(r, width=512):
            return ring[:, r, :].rearrange("p (k n) -> p k n", n=width)

        EARLY_STEPS, LATE_STEPS = mod_steps()
        LAYERS = [
            dict(w_mod=A["w_ada"][0], b_mod=A["b_ada"], row=0),
            dict(w_mod=A["w_ada"][1], b_mod=A["b_ada"], row=1),
            dict(w_mod=A["w_mod_2"][0], b_mod=A["b_mod_2"], row=0),
        ]

        V2 = area(4096, TILES, 512)
        silu_r = area(6144, 2, 512)
        silu_z = area(7168, 2, 512)
        final_gain = area(8192, D)
        qc = area(8192, 2, SEQ)
        kc = area(8704, 2, 512)
        x_raw = area(9728, 6, 512)
        lr_rows = area(12800, 512)
        dt_raw = area(13312, 512)
        gates = area(13824, 4, 512)
        gate_tmp = area(15872, 4, 512)
        xbc = area(17920, 6, 512)
        cum_g = area(20992, 8, 257)
        cum_s = sb("ssd_prefix_sums", 514)
        spare = X[:, 2:4, :].rearrange("p t n -> p (t n)")
        dt_rows, a_rows = spare[:, 0:512], spare[:, 512:1024]
        decays = spare[:, 1024:2048].rearrange("p (n t) -> p n t", n=4)
        cols = area(23048, 224)
        BT = area(23272, 2, P)
        BC_back = area(0, 2, SEQ)
        seg = area(2560, 2, 768)
        lev_tmp = area(2560, 512)
        XS = area(9728, TILES, 512)
        att8 = area(11776, 2, 512)
        att = area(12800, 2, 512)
        lev = area(13824, 2, 1024)
        KDt = area(13824, 2, 512)
        QD = area(15872, 4, SEQ)
        KD_rows = area(16896, 4, SEQ)
        SG = area(17920, 4, 256)
        BC = area(18944, 2, 512)
        XW = area(512, 4, 512)
        SS = area(3072, 2, 256)
        W = area(21504, 3, 512)
        intra = area(15872, 2, 512)
        prod2 = area(13824, 512)
        O = X[:, 2:4, :]
        oT2 = area(0, KD, SEQ)
        Y = area(4096, 2, D)
        gain_b = area(9216, D)
        gate3_b = area(8192, 1, D)
        xn3 = area(10240, 2, D)
        h3T = area(12288, KD, SEQ)
        ffT = area(14336, FB, SEQ)
        ff_silu = area(19968, 2, SEQ)
        rows2 = sb("gla_ssd_gains", 648)
        gla_gain, ssd_gain, skip_gain = rows2[:, 0:128], rows2[:, 128:640], rows2[:, 640:648]
        wg = vec_in.rearrange("p (d h) n -> p d (h n)", d=2)
        dt_bias, neg_a = small[0:16, 100:101], small[0:16, 101:102]

        def load_block2(sp, load, load_cols, T):
            due = T.step
            w = A["w_in_2"][0]
            load_cols(w, B_X, B_X + 512)
            load((lambda r: slot_view(r)[:, :, 0:272], big(w, B_X + 512, B_END)),
                 (lambda r: slot_view(r)[:, :, 272:304], big(w, B_LR, B_Z)))
            for c0 in (B_Q, B_V, B_R, B_Z):
                load_cols(w, c0, c0 + 512)
            for n in range(2):
                load_cols(A["w_out_2"][0], 512 * n, 512 * n + 512)
            for c0 in range(0, D_FF, 512):
                for name in ("w_gate_2", "w_up_2"):
                    load_cols(A[name][0], c0, min(c0 + 512, D_FF))
            for n in range(2):
                for k0 in range(0, FB, KD):
                    k1 = min(k0 + KD, FB)
                    src = A["w_down_2"][0][k0 * P:k1 * P, n * 512:n * 512 + 512].rearrange("(k p) n -> p k n", p=P)
                    load((lambda r, kk=k1 - k0: slot_view(r)[:, 0:kk, :], src))

        def pe_block2(pe, T, next_slot, release, turn, turn_streams, dense, broadcast_gate):
            due = T.step
            pe.wait_ge(S("xn_ready"), due("xn_ready", 2 + TILES))
            turn_streams(xn, range(TILES))
            pe.wait_ge(S("hT_ready_dve"), due("hT_ready_dve", 4))
            pe.wait_ge(S("hT_ready_act"), due("hT_ready_act", 4))

            def rows_of(pool, r, c0, m, n):
                pe.wait_ge(S("free" + pool), due("free" + pool))
                b = bank_of(pool, T.n["free" + pool])
                for k in range(KD):
                    mm = pe.matmul(b[0:m, 0:n], slot_view(r)[:, k, c0:c0 + m], hT[:, k, 0:n], start=(k == 0), stop=(k == KD - 1))
                mm.then_inc(S("full" + pool), 1)

            def level(keys, queries, cross):
                for par in range(2):
                    rows_ = slice(64 * par, 64 * par + 64)
                    pe.wait_ge(S("freeD"), due("freeD"))
                    b = bank_of("D", T.n["freeD"])
                    for t in range(2):
                        for blk in range(2):
                            at = (2 * t + blk) * P
                            i = 1 - t if cross else t
                            mm = pe.matmul(b[:, at:at + P], keys[rows_, blk, t * P:t * P + P], queries[rows_, blk, i * P:i * P + P],
                                           start=True, stop=True)
                    mm.then_inc(S("fullD"), 1)

            r = next_slot()
            pe.wait_ge(S(f"slot_landed{r}"), due(f"slot_landed{r}", 16))
            for blk in range(4):
                rows_of("DA"[blk % 2], r, blk * P, P, 512)
            release("A")
            r = next_slot()
            pe.wait_ge(S(f"slot_landed{r}"), due(f"slot_landed{r}", 2 * 16))
            for blk in range(2):
                rows_of("DA"[blk % 2], r, blk * P, P, 512)
            rows_of("D", r, 256, 16, 512)
            rows_of("D", r, 272, 32, 512)
            release("D")
            r = next_slot()
            pe.wait_ge(S(f"slot_landed{r}"), due(f"slot_landed{r}", 16))
            for blk in range(4):
                rows_of("D" if blk < 2 else "A", r, blk * P, P, SEQ if blk < 2 else 512)
            release("A")
            pe.wait_ge(S("lr_ready"), due("lr_ready"))
            pe.wait_ge(S("wg_landed"), due("wg_landed", 32))
            for d in range(2):
                for blk in range(2):
                    pe.wait_ge(S("freeD"), due("freeD"))
                    b = bank_of("D", T.n["freeD"])
                    pe.matmul(b[:, :], wg[0:32, d, blk * P:blk * P + P], lr_rows[0:32, :], start=True, stop=True)\
                        .then_inc(S("fullD"), 1)
            r = next_slot()
            pe.wait_ge(S(f"slot_landed{r}"), due(f"slot_landed{r}", 16))
            for t in range(TILES):
                dense("DA"[t % 2], t, r, hT)
            release("A")
            r = next_slot()
            pe.wait_ge(S(f"slot_landed{r}"), due(f"slot_landed{r}", 16))
            for t in range(2):
                dense("A", t, r, hT)
            release("A")
            pe.wait_ge(S("xbc_ready"), due("xbc_ready"))
            for t in range(TILES):
                pe.wait_ge(S("freeA"), due("freeA"))
                b = bank_of("A", T.n["freeA"])
                for blk in range(4):
                    mm = turn(b[:, blk * P:blk * P + P], xbc[:, blk, t * P:t * P + P])
                    if blk == 3:
                        mm.then_inc(S("fullA"), 1)
            pe.wait_ge(S("freeA"), due("freeA"))
            b = bank_of("A", T.n["freeA"])
            for c in range(2):
                mm = turn(b[:, c * P:c * P + P], xbc[:, 4, (2 + c) * P:(3 + c) * P])
                if c:
                    mm.then_inc(S("fullA"), 1)
            pe.wait_ge(S("ssd_rows_ready"), due("ssd_rows_ready"))
            pe.wait_ge(S("freeD"), due("freeD"))
            b = bank_of("D", T.n["freeD"])
            for t in range(2):
                for n, src in enumerate((dt_rows[:, t * P:t * P + P], cum_s[:, 1 + t * P:1 + t * P + P], cum_s[:, t * P:t * P + P],
                                         decays[:, 0, t * P:t * P + P], decays[:, 1, t * P:t * P + P])):
                    turn(b[:, t * 80 + 16 * n:t * 80 + 16 * n + 16], src[0:16, :])
            for c in range(2):
                for n in range(2):
                    mm = turn(b[:, 160 + 32 * c + 16 * n:176 + 32 * c + 16 * n], decays[0:16, 2 + n, c * P:c * P + P])
                    if c and n:
                        mm.then_inc(S("fullD"), 1)
            pe.wait_ge(S("qd_kd_ready"), due("qd_kd_ready"))
            for d in range(2):
                pe.wait_ge(S("freeA"), due("freeA"))
                b = bank_of("A", T.n["freeA"])
                for c in range(2):
                    for blk in range(2):
                        mm = turn(b[:, (2 * c + blk) * P:(2 * c + blk + 1) * P], KD_rows[:, 2 * d + blk, c * P:c * P + P])
                        if c and blk:
                            mm.then_inc(S("fullA"), 1)
            r = next_slot()
            pe.wait_ge(S(f"slot_landed{r}"), due(f"slot_landed{r}", 16))
            for t in range(2):
                dense("A", t, r, hT)
            release("A")
            pe.wait_ge(S("kdt_ready"), due("kdt_ready"))
            for d in range(2):
                pe.wait_ge(S("freeD"), due("freeD"))
                b = bank_of("D", T.n["freeD"])
                for blk in range(2):
                    for c in range(2):
                        mm = pe.matmul(b[:, blk * 256:blk * 256 + 256], KDt[:, d, (2 * c + blk) * P:(2 * c + blk + 1) * P],
                                       V2[:, 2 + c, blk * 256:blk * 256 + 256], start=(c == 0), stop=(c == 1))
                mm.then_inc(S("fullD"), 1)
            for g in range(2):
                pe.wait_ge(S("freeD"), due("freeD"))
                b = bank_of("D", T.n["freeD"])
                for j in range(2):
                    mm = pe.matmul(b[:, j * SEQ:j * SEQ + SEQ], xbc[64 * g:64 * g + 64, 4, j * P:j * P + P],
                                   xbc[64 * g:64 * g + 64, 5, 0:SEQ], start=True, stop=True)
                mm.then_inc(S("fullD"), 1)
            level(kc, qc, False)
            pe.wait_ge(S("xw_ready"), due("xw_ready"))
            pe.wait_ge(S("freeD"), due("freeD"))
            b = bank_of("D", T.n["freeD"])
            for g in range(2):
                for d in range(2):
                    for c in range(2):
                        mm = pe.matmul(b[64 * g:64 * g + 64, d * 256:d * 256 + 256], BT[:, c, 64 * g:64 * g + 64],
                                       XW[:, 2 * c + d, g * 256:g * 256 + 256], start=(c == 0), stop=(c == 1))
            mm.then_inc(S("fullD"), 1)
            for l in range(1, 9):
                pe.wait_ge(S("level_ready"), due("level_ready"))
                v = lev[:, l % 2, :].rearrange("p (w b i) -> p w b i", w=2, b=2)
                level(v[:, 1], v[:, 0], l == 8)
                if l > 1:
                    continue
                pe.wait_ge(S("ss_ready"), due("ss_ready"))
                for t in range(2):
                    for g in range(2):
                        pe.wait_ge(S("freeD"), due("freeD"))
                        b = bank_of("D", T.n["freeD"])
                        for d in range(2):
                            mm = pe.matmul(b[:, d * 256:d * 256 + 256], xbc[64 * g:64 * g + 64, 5, t * P:t * P + P],
                                           SS[64 * g:64 * g + 64, d, :], start=True, stop=True)
                        mm.then_inc(S("fullD"), 1)

            def row_out(h):
                for row in (h, 8 + h):
                    pe.wait_ge(S("freeD"), due("freeD"))
                    b = bank_of("D", T.n["freeD"])
                    pe.matmul(b[:, 0:258], ident[0:16, row:row + 1].to_broadcast([16, P]), cum_s[0:16, 0:258],
                              start=True, stop=True).then_inc(S("fullD"), 1)

            row_out(0)
            row_out(1)
            pe.wait_ge(S("states_ready"), due("states_ready"))
            pe.wait_ge(S("att_ready"), due("att_ready"))
            for t in range(2):
                pe.wait_ge(S("freeD"), due("freeD"))
                b = bank_of("D", T.n["freeD"])
                for blk in range(2):
                    for d in range(2):
                        pe.matmul(b[:, blk * 256:blk * 256 + 256], QD[:, 2 * d + blk, t * P:t * P + P], SG[:, 2 * d + blk, :],
                                  start=(d == 0), stop=False)
                    for par in range(2):
                        h = 2 * blk + par
                        pe.matmul(b[:, h * P:h * P + P], att[:, par, (2 * t + blk) * P:(2 * t + blk + 1) * P],
                                  V2[:, t, h * P:h * P + P], start=False, stop=False)
                        mm = pe.matmul(b[:, h * P:h * P + P], att8[:, par, (2 * (1 - t) + blk) * P:(2 * (1 - t) + blk + 1) * P],
                                       V2[:, 1 - t, h * P:h * P + P], start=False, stop=(par == 1))
                mm.then_inc(S("fullD"), 1)
            for h in range(8):
                if h < 6:
                    row_out(h + 2)
                pe.wait_ge(S("w_ready"), due("w_ready"))
                pe.wait_ge(S("freeA"), due("freeA"))
                b = bank_of("A", T.n["freeA"])
                for t in range(2):
                    for j in range(2):
                        mm = pe.matmul(b[:, t * HD:t * HD + HD], W[:, h % 3, j * SEQ + t * P:j * SEQ + t * P + P],
                                       XS[:, j, h * HD:h * HD + HD], start=(j == 0), stop=(j == 1))
                mm.then_inc(S("fullA"), 1)
            broadcast_gate(2, 0, 1)
            pe.wait_ge(S("o_ready"), due("o_ready"))
            turn_streams(O, range(2))
            pe.wait_ge(S("oT2_ready_dve"), due("oT2_ready_dve", 4))
            pe.wait_ge(S("oT2_ready_act"), due("oT2_ready_act", 4))
            for n in range(2):
                r = next_slot()
                pe.wait_ge(S(f"slot_landed{r}"), due(f"slot_landed{r}", 16))
                for t in range(2):
                    dense("D", t, r, oT2)
                release("D")
            broadcast_gate(2, 1, 1)
            pe.wait_ge(S("xn_ready"), due("xn_ready", 2))
            turn_streams(xn3, range(2))
            pe.wait_ge(S("hT_ready_dve"), due("hT_ready_dve", 4))
            pe.wait_ge(S("hT_ready_act"), due("hT_ready_act", 4))
            for c0 in range(0, D_FF, 512):
                rg = next_slot()
                pe.wait_ge(S(f"slot_landed{rg}"), due(f"slot_landed{rg}", 16))
                ru = next_slot()
                pe.wait_ge(S(f"slot_landed{ru}"), due(f"slot_landed{ru}", 16))
                for blk in range(min(4, (D_FF - c0) // P)):
                    pe.wait_ge(S("freeD"), due("freeD"))
                    b = bank_of("D", T.n["freeD"])
                    for n, r in enumerate((rg, ru)):
                        for k in range(KD):
                            mm = pe.matmul(b[:, n * SEQ:n * SEQ + SEQ], slot_view(r)[:, k, blk * P:blk * P + P], h3T[:, k, :],
                                           start=(k == 0), stop=(k == KD - 1))
                    mm.then_inc(S("fullD"), 1)
                    if c0 == 0 and blk == 0:
                        ff_first.append(T.n["freeD"])
                release("D", 2)
            pe.wait_ge(S("ffT_ready"), due("ffT_ready", FB))
            for n in range(2):
                pe.wait_ge(S("freeD"), due("freeD"))
                b0 = bank_of("D", T.n["freeD"])
                pe.wait_ge(S("freeD"), due("freeD"))
                b1 = bank_of("D", T.n["freeD"])
                bs = (b0, b1)
                for k0 in range(0, FB, KD):
                    r = next_slot()
                    pe.wait_ge(S(f"slot_landed{r}"), due(f"slot_landed{r}", 16))
                    for t in range(2):
                        for k in range(k0, min(k0 + KD, FB)):
                            mm = pe.matmul(bs[t][:, :], ffT[:, k, t * P:t * P + P], slot_view(r)[:, k - k0, :],
                                           start=(k == 0), stop=(k == FB - 1))
                            if k == FB - 1:
                                mm.then_inc(S("fullD"), 1)
                    pieces = 1
                    if k0 + KD >= FB:
                        release("D", 3)

        ff_first = []

        def dve_block2(dve, T, norm, modulate, add_gated):
            due = T.step
            def bc(v, n):
                return v.unsqueeze(2).to_broadcast([P, v.shape[1], n])

            dve.memset(vec_in[:, :, :], 0.0).then_inc(S("dve_step"), 1)
            dve.wait_ge(S("dve_step"), due("dve_step"))
            dve.memset(flag, 0.0).then_inc(S("block1_done"), 1)
            dve.wait_ge(S("block1_done"), due("block1_done"))
            norm(xn, range(2))
            dve.wait_ge(S("final_gain_landed"), due("final_gain_landed", 16))
            for t in range(2):
                dve.tensor_tensor(X[:, t, :], xn[:, t, :], final_gain, ALU.mult).then_inc(S("dve_step"), 1)
                dve.wait_ge(S("dve_step"), due("dve_step"))
            dve.wait_ge(S("ctx2_landed"), due("ctx2_landed", 16))
            norm(xn, range(TILES))
            modulate(hT, 4, 2)
            def take_x(blk):
                dve.wait_ge(S("fullD"), due("fullD"))
                b = bank_of("D", T.n["fullD"])
                dve.tensor_copy(x_raw[:, blk, :], b[:, :]).then_inc(S("freeD"), 1)
                dve.wait_ge(S("freeD"), due("freeD"))

            def conv(blk):
                def tap(y, x):
                    n = (3 * y + x) * 6 + blk
                    return vecs[:, 3, n:n + 1]

                if blk % 2:
                    dve.wait_ge(S("x_raw_ready_act"), due("x_raw_ready_act"))
                dve.tensor_scalar(xbc[:, blk, :], x_raw[:, blk, :], tap(1, 1), None, ALU.mult).then_inc(S("dve_step"), 1)
                dve.wait_ge(S("dve_step"), due("dve_step"))
                raw = x_raw[:, blk, 0:SEQ].rearrange("p (y x) -> p y x", x=64)
                acc = xbc[:, blk, 0:SEQ].rearrange("p (y x) -> p y x", x=64)
                for y in (-1, 0, 1):
                    for x in (-1, 0, 1):
                        if not y and not x:
                            continue
                        oy, ox = slice(max(0, -y), 4 - max(0, y)), slice(max(0, -x), 64 - max(0, x))
                        iy, ix = slice(max(0, y), 4 - max(0, -y)), slice(max(0, x), 64 - max(0, -x))
                        dve.scalar_tensor_tensor(out=acc[:, oy, ox], in0=raw[:, iy, ix], scalar=tap(1 + y, 1 + x),
                                                 in1=acc[:, oy, ox], op0=ALU.mult, op1=ALU.add).then_inc(S("dve_step"), 1)
                        dve.wait_ge(S("dve_step"), due("dve_step"))
                for x in (-1, 1):
                    o0, i0 = SEQ + max(0, -x), SEQ + max(0, x)
                    dve.scalar_tensor_tensor(out=xbc[:, blk, o0:o0 + 255], in0=x_raw[:, blk, i0:i0 + 255],
                                             scalar=tap(1, 1 + x), in1=xbc[:, blk, o0:o0 + 255], op0=ALU.mult, op1=ALU.add).then_inc(S("dve_step"), 1)
                    dve.wait_ge(S("dve_step"), due("dve_step"))
                dve.memset(flag, 0.0).then_inc(S("conv_ready"), 1)
                dve.wait_ge(S("conv_ready"), due("conv_ready"))

            take_x(0)
            conv(0)
            take_x(2)
            conv(2)
            conv(1)
            take_x(4)
            conv(4)
            conv(3)
            dve.wait_ge(S("fullD"), due("fullD"))
            b = bank_of("D", T.n["fullD"])
            dve.wait_ge(S("block2_rows_landed"), due("block2_rows_landed", 16 * N_ROWS2))
            dve.tensor_scalar(dt_raw[0:16, :], b[0:16, :], dt_bias, None, ALU.add).then_inc(S("freeD"), 1)
            dve.wait_ge(S("freeD"), due("freeD"))
            dve.memset(flag, 0.0).then_inc(S("dt_raw_ready"), 1)
            dve.wait_ge(S("dt_raw_ready"), due("dt_raw_ready"))
            dve.wait_ge(S("fullD"), due("fullD"))
            b = bank_of("D", T.n["fullD"])
            dve.tensor_copy(lr_rows[0:32, :], b[0:32, :]).then_inc(S("freeD"), 1)
            dve.wait_ge(S("freeD"), due("freeD"))
            dve.memset(flag, 0.0).then_inc(S("lr_ready"), 1)
            dve.wait_ge(S("lr_ready"), due("lr_ready"))
            conv(5)
            for blk in range(2):
                dve.wait_ge(S("fullD"), due("fullD"))
                b = bank_of("D", T.n["fullD"])
                dve.tensor_scalar(qc[:, blk, :], b[:, 0:SEQ], SCALE, None, ALU.mult).then_inc(S("freeD"), 1)
                dve.wait_ge(S("freeD"), due("freeD"))
            for n in range(4):
                dve.wait_ge(S("fullD"), due("fullD"))
                b = bank_of("D", T.n["fullD"])
                dve.tensor_scalar(gates[:, n, :], b[:, :], vecs[:, 2, 86 + n:87 + n], None, ALU.add).then_inc(S("freeD"), 1)
                dve.wait_ge(S("freeD"), due("freeD"))
            dve.memset(flag, 0.0).then_inc(S("gates_raw_ready"), 1)
            dve.wait_ge(S("gates_raw_ready"), due("gates_raw_ready"))
            dve.wait_ge(S("dt_log_ready"), due("dt_log_ready"))
            dve.scalar_tensor_tensor(out=dt_rows[0:16, :], in0=dt_raw[0:16, :], scalar=0.0, in1=dt_rows[0:16, :],
                                     op0=ALU.max, op1=ALU.add).then_inc(S("dve_step"), 1)
            dve.wait_ge(S("dve_step"), due("dve_step"))
            dve.tensor_scalar(neg_a, neg_a, -1.0, None, ALU.mult).then_inc(S("dve_step"), 1)
            dve.wait_ge(S("dve_step"), due("dve_step"))
            dve.tensor_scalar(a_rows[0:16, :], dt_rows[0:16, :], neg_a, None, ALU.mult).then_inc(S("dve_step"), 1)
            dve.wait_ge(S("dve_step"), due("dve_step"))
            for s in range(2):
                c = cum_s[0:16, 257 * s:257 * s + 257]
                a = a_rows[0:16, s * SEQ:s * SEQ + SEQ]
                dve.memset(c[:, 0:1], 0.0).then_inc(S("dve_step"), 1)
                dve.wait_ge(S("dve_step"), due("dve_step"))
                dve.tensor_tensor_scan(c[:, 1:257], a, a, 0.0, ALU.add, ALU.min).then_inc(S("dve_step"), 1)
                dve.wait_ge(S("dve_step"), due("dve_step"))
            lat, cx = cum_s[0:16, 0:257], cum_s[0:16, 257:514]
            dve.tensor_copy(decays[0:16, 0, :], lat[:, 1:257]).then_inc(S("dve_step"), 1)
            dve.wait_ge(S("dve_step"), due("dve_step"))
            dve.tensor_scalar(decays[0:16, 1, :], lat[:, 0:256], lat[:, 256:257], -1.0, ALU.subtract, ALU.mult).then_inc(S("dve_step"), 1)
            dve.wait_ge(S("dve_step"), due("dve_step"))
            dve.tensor_scalar(decays[0:16, 2, :], cx[:, 1:257], cx[:, 256:257], -1.0, ALU.subtract, ALU.mult).then_inc(S("dve_step"), 1)
            dve.wait_ge(S("dve_step"), due("dve_step"))
            dve.tensor_copy(decays[0:16, 3, :], cx[:, 0:256]).then_inc(S("dve_step"), 1)
            dve.wait_ge(S("dve_step"), due("dve_step"))
            dve.memset(flag, 0.0).then_inc(S("decays_ready"), 1)
            dve.wait_ge(S("decays_ready"), due("decays_ready"))
            dve.wait_ge(S("fullD"), due("fullD"))
            b = bank_of("D", T.n["fullD"])
            dve.tensor_copy(V2[:, 0, :], b[:, :]).then_inc(S("freeD"), 1)
            dve.wait_ge(S("freeD"), due("freeD"))
            dve.wait_ge(S("gates_log_ready"), due("gates_log_ready"))
            dve.scalar_tensor_tensor(out=gates, in0=gates, scalar=0.0, in1=gate_tmp, op0=ALU.min, op1=ALU.subtract).then_inc(S("dve_step"), 1)
            dve.wait_ge(S("dve_step"), due("dve_step"))
            dve.tensor_scalar(gates, gates, 1.0 / 16.0, None, ALU.mult).then_inc(S("dve_step"), 1)
            dve.wait_ge(S("dve_step"), due("dve_step"))
            dve.memset(cum_g[:, :, 0:1], 0.0).then_inc(S("dve_step"), 1)
            dve.wait_ge(S("dve_step"), due("dve_step"))
            for n in range(4):
                for s in range(2):
                    g = gates[:, n, s * SEQ:s * SEQ + SEQ]
                    dve.tensor_tensor_scan(cum_g[:, 2 * n + s, 1:257], g, g, 0.0, ALU.add, ALU.min).then_inc(S("dve_step"), 1)
                    dve.wait_ge(S("dve_step"), due("dve_step"))
            Cg = cum_g.rearrange("p (d b s) t -> p d b s t", d=2, b=2)
            for blk in range(2):
                f, g = Cg[:, 0, blk], Cg[:, 1, blk]
                dve.tensor_copy(QD[:, blk, :], f[:, 0, 1:257]).then_inc(S("dve_step"), 1)
                dve.wait_ge(S("dve_step"), due("dve_step"))
                dve.tensor_scalar(QD[:, 2 + blk, :], g[:, 0, 0:256], g[:, 0, 256:257], -1.0, ALU.subtract, ALU.mult).then_inc(S("dve_step"), 1)
                dve.wait_ge(S("dve_step"), due("dve_step"))
                dve.tensor_scalar(KD_rows[:, blk, :], f[:, 1, 1:257], f[:, 1, 256:257], -1.0, ALU.subtract, ALU.mult).then_inc(S("dve_step"), 1)
                dve.wait_ge(S("dve_step"), due("dve_step"))
                dve.tensor_copy(KD_rows[:, 2 + blk, :], g[:, 1, 0:256]).then_inc(S("dve_step"), 1)
                dve.wait_ge(S("dve_step"), due("dve_step"))
            dve.memset(flag, 0.0).then_inc(S("qd_raw_ready"), 1)
            dve.wait_ge(S("qd_raw_ready"), due("qd_raw_ready"))
            dve.wait_ge(S("fullD"), due("fullD"))
            b = bank_of("D", T.n["fullD"])
            dve.tensor_copy(V2[:, 2, :], b[:, :]).then_inc(S("freeD"), 1)
            dve.wait_ge(S("freeD"), due("freeD"))
            dve.wait_ge(S("decays_exp_ready"), due("decays_exp_ready"))
            for n in (2, 3):
                dve.tensor_tensor(decays[0:16, n, :], decays[0:16, n, :], dt_rows[0:16, SEQ:512], ALU.mult).then_inc(S("dve_step"), 1)
                dve.wait_ge(S("dve_step"), due("dve_step"))
            dve.memset(flag, 0.0).then_inc(S("ssd_rows_ready"), 1)
            dve.wait_ge(S("ssd_rows_ready"), due("ssd_rows_ready"))
            dve.wait_ge(S("qd_exp_ready"), due("qd_exp_ready"))
            for d in range(2):
                dve.tensor_tensor(QD[:, 2 * d:2 * d + 2, :], QD[:, 2 * d:2 * d + 2, :], qc, ALU.mult).then_inc(S("dve_step"), 1)
                dve.wait_ge(S("dve_step"), due("dve_step"))
                dve.tensor_tensor(KD_rows[:, 2 * d:2 * d + 2, :], KD_rows[:, 2 * d:2 * d + 2, :], kc[:, :, SEQ:512], ALU.mult).then_inc(S("dve_step"), 1)
                dve.wait_ge(S("dve_step"), due("dve_step"))
            dve.memset(flag, 0.0).then_inc(S("qd_kd_ready"), 1)
            dve.wait_ge(S("qd_kd_ready"), due("qd_kd_ready"))

            def level_args(l):
                half = 1 << (l - 1)
                v = lev[:, l % 2, :].rearrange("p (w b n two h) -> p w b n two h", w=2, b=2, two=2, h=half)

                def c(d, off):
                    return Cg[:, d, :, 0, off:off + 256].rearrange("p b (n two h) -> p b n two h", two=2, h=half)

                f1, f0, b0 = c(0, 1), c(0, 0), c(1, 0)
                mf = f0[:, :, :, 1, 0:1].to_broadcast([P, 2, 128 // half, half])
                mb = b0[:, :, :, 1, 0:1].to_broadcast([P, 2, 128 // half, half])
                dve.tensor_tensor(v[:, 0, :, :, 1, :], f1[:, :, :, 1, :], mf, ALU.subtract).then_inc(S("dve_step"), 1)
                dve.wait_ge(S("dve_step"), due("dve_step"))
                dve.tensor_tensor(v[:, 0, :, :, 0, :], mb, b0[:, :, :, 0, :], ALU.subtract).then_inc(S("dve_step"), 1)
                dve.wait_ge(S("dve_step"), due("dve_step"))
                dve.tensor_tensor(v[:, 1, :, :, 0, :], mf, f1[:, :, :, 0, :], ALU.subtract).then_inc(S("dve_step"), 1)
                dve.wait_ge(S("dve_step"), due("dve_step"))
                dve.tensor_tensor(v[:, 1, :, :, 1, :], b0[:, :, :, 1, :], mb, ALU.subtract).then_inc(S("level_args_ready"), 1)
                dve.wait_ge(S("level_args_ready"), due("level_args_ready"))

            def level_ops(l):
                dve.wait_ge(S("level_exp_ready"), due("level_exp_ready"))
                v = lev[:, l % 2, :].rearrange("p (w b i) -> p w b i", w=2, b=2)
                dve.tensor_tensor(v[:, 0], v[:, 0], qc, ALU.mult).then_inc(S("dve_step"), 1)
                dve.wait_ge(S("dve_step"), due("dve_step"))
                dve.tensor_tensor(v[:, 1], v[:, 1], kc[:, :, 0:SEQ], ALU.mult).then_inc(S("level_ready"), 1)
                dve.wait_ge(S("level_ready"), due("level_ready"))

            def take_level(l):
                for par in range(2):
                    dve.wait_ge(S("fullD"), due("fullD"))
                    b = bank_of("D", T.n["fullD"])
                    if par and 0 < l < 7:
                        level_args(l + 2)
                    if l == 8:
                        dve.tensor_copy(att8[:, par, :], b[:, :]).then_inc(S("freeD"), 1)
                        dve.wait_ge(S("freeD"), due("freeD"))
                        continue
                    mask = C("twice") if l == 0 else C("levels", 7, P)[:, l - 1, :]
                    mask = mask.unsqueeze(1).to_broadcast([P, 4, P])
                    src = b[:, :].rearrange("p (n i) -> p n i", n=4)
                    dst = att[:, par, :] if l == 0 else lev_tmp
                    dve.tensor_tensor(dst.rearrange("p (n i) -> p n i", n=4), src, mask, ALU.mult).then_inc(S("freeD"), 1)
                    dve.wait_ge(S("freeD"), due("freeD"))
                    if l:
                        dve.tensor_tensor(att[:, par, :], att[:, par, :], lev_tmp, ALU.add).then_inc(S("dve_step"), 1)
                        dve.wait_ge(S("dve_step"), due("dve_step"))

            level_args(1)
            dve.wait_ge(S("fullD"), due("fullD"))
            b = bank_of("D", T.n["fullD"])
            dve.tensor_copy(cols, b[:, 0:224]).then_inc(S("freeD"), 1)
            dve.wait_ge(S("freeD"), due("freeD"))
            dve.wait_ge(S("xs_ready"), due("xs_ready"))
            dve.memset(SG, 0.0).then_inc(S("dve_step"), 1)
            dve.wait_ge(S("dve_step"), due("dve_step"))
            for d in range(2):
                dve.wait_ge(S("fullD"), due("fullD"))
                b = bank_of("D", T.n["fullD"])
                for par in range(2):
                    rows_ = slice(64 * par, 64 * par + 64)
                    src = b[rows_, :].rearrange("p (b n) -> p b n", b=2)[:, :, par * P:par * P + P]
                    signal = "freeD" if par else "dve_step"
                    dve.tensor_copy(SG[rows_, 2 * d:2 * d + 2, par * P:par * P + P], src).then_inc(S(signal), 1)
                    dve.wait_ge(S(signal), due(signal))
            dve.memset(flag, 0.0).then_inc(S("states_ready"), 1)
            dve.wait_ge(S("states_ready"), due("states_ready"))
            level_args(2)
            for g in range(2):
                dve.wait_ge(S("fullD"), due("fullD"))
                b = bank_of("D", T.n["fullD"])
                tiles_ = b[:, :].rearrange("p (n i) -> p n i", n=4)
                bc_g = BC[:, g, :].rearrange("p (n i) -> p n i", n=4)
                dve.tensor_tensor(bc_g[:, 0:4:3, :], tiles_[:, 0:4:3, :], C("after").unsqueeze(1).to_broadcast([P, 2, P]), ALU.mult).then_inc(S("dve_step"), 1)
                dve.wait_ge(S("dve_step"), due("dve_step"))
                dve.tensor_tensor(BC_back[:, g, :].rearrange("p (n i) -> p n i", n=2), tiles_[:, 0:4:3, :],
                                  C("before").unsqueeze(1).to_broadcast([P, 2, P]), ALU.mult).then_inc(S("dve_step"), 1)
                dve.wait_ge(S("dve_step"), due("dve_step"))
                dve.tensor_copy(bc_g[:, 1:3, :], tiles_[:, 1:3, :]).then_inc(S("freeD"), 1)
                dve.wait_ge(S("freeD"), due("freeD"))
            for c in range(2):
                for d in range(2):
                    at = 160 + 32 * c + 24 * d
                    dve.tensor_tensor(XW[:, 2 * c + d, :].rearrange("p (h v) -> p h v", h=8),
                                      XS[:, 2 + c, :].rearrange("p (h v) -> p h v", h=8), bc(cols[:, at:at + 8], HD), ALU.mult).then_inc(S("dve_step"), 1)
                    dve.wait_ge(S("dve_step"), due("dve_step"))
            dve.memset(flag, 0.0).then_inc(S("xw_ready"), 1)
            dve.wait_ge(S("xw_ready"), due("xw_ready"))
            level_ops(1)
            take_level(0)
            dve.wait_ge(S("fullD"), due("fullD"))
            b = bank_of("D", T.n["fullD"])
            dve.tensor_copy(SS, b[:, :].rearrange("p (d n) -> p d n", d=2)).then_inc(S("freeD"), 1)
            dve.wait_ge(S("freeD"), due("freeD"))
            dve.memset(flag, 0.0).then_inc(S("ss_ready"), 1)
            dve.wait_ge(S("ss_ready"), due("ss_ready"))
            level_ops(2)
            take_level(1)
            for t in range(2):
                for g in range(2):
                    dve.wait_ge(S("fullD"), due("fullD"))
                    b = bank_of("D", T.n["fullD"])
                    y = O[:, t, 512 + 256 * g:768 + 256 * g].rearrange("p (h v) -> p h v", h=4)
                    tmp = lev_tmp[:, 0:256].rearrange("p (h v) -> p h v", h=4)
                    for d in range(2):
                        at = t * 80 + (48 if d == 0 else 72) + 4 * g
                        signal = "freeD" if d else "dve_step"
                        dve.tensor_tensor(tmp if d else y, b[:, d * 256:d * 256 + 256].rearrange("p (h v) -> p h v", h=4),
                                          bc(cols[:, at:at + 4], HD), ALU.mult).then_inc(S(signal), 1)
                        dve.wait_ge(S(signal), due(signal))
                    dve.tensor_tensor(y, y, tmp, ALU.add).then_inc(S("dve_step"), 1)
                    dve.wait_ge(S("dve_step"), due("dve_step"))
                y = O[:, t, 512:1024]
                dve.tensor_tensor(lev_tmp.rearrange("p (h v) -> p h v", h=8), XS[:, t, :].rearrange("p (h v) -> p h v", h=8),
                                  bc(skip_gain, HD), ALU.mult).then_inc(S("dve_step"), 1)
                dve.wait_ge(S("dve_step"), due("dve_step"))
                dve.tensor_tensor(y, y, lev_tmp, ALU.add).then_inc(S("dve_step"), 1)
                dve.wait_ge(S("dve_step"), due("dve_step"))
            for l in range(2, 9):
                if l < 8:
                    level_ops(l + 1)
                take_level(l)
            dve.memset(flag, 0.0).then_inc(S("att_ready"), 1)
            dve.wait_ge(S("att_ready"), due("att_ready"))
            sc = small[:, 110:118]
            iv = small[:, 118:126]
            rs = small[:, 126:134]

            def start_norm(n, width):
                dve.tensor_scalar(iv[:, 0:n], sc[:, 0:n], 1.0 / width, EPS, ALU.mult, ALU.add).then_inc(S("dve_step"), 1)
                dve.wait_ge(S("dve_step"), due("dve_step"))
                dve.reciprocal(iv[:, 0:n], iv[:, 0:n]).then_inc(S("inv_ready"), 1)
                dve.wait_ge(S("inv_ready"), due("inv_ready"))

            def col(j, n):
                return cols[:, 80 * j + n:80 * j + n + 1]

            def head_args(h):
                s = seg[:, h % 2, :]
                dve.wait_ge(S("fullD"), due("fullD"))
                b = bank_of("D", T.n["fullD"])
                dve.tensor_scalar(s[:, 0:256], b[:, 1:257], col(0, 16 + h), 0.0, ALU.subtract, ALU.min).then_inc(S("dve_step"), 1)
                dve.wait_ge(S("dve_step"), due("dve_step"))
                dve.tensor_scalar(s[:, 256:384], b[:, 129:257], col(1, 16 + h), 0.0, ALU.subtract, ALU.min).then_inc(S("freeD"), 1)
                dve.wait_ge(S("freeD"), due("freeD"))
                dve.wait_ge(S("fullD"), due("fullD"))
                b = bank_of("D", T.n["fullD"])
                dve.tensor_scalar(s[:, 384:512], b[:, 0:128], col(0, 40 + h), 0.0, ALU.subtract, ALU.max).then_inc(S("dve_step"), 1)
                dve.wait_ge(S("dve_step"), due("dve_step"))
                dve.tensor_scalar(s[:, 512:768], b[:, 0:256], col(1, 40 + h), 0.0, ALU.subtract, ALU.max).then_inc(S("freeD"), 1)
                dve.wait_ge(S("freeD"), due("freeD"))
                dve.memset(flag, 0.0).then_inc(S("seg_ready"), 1)
                dve.wait_ge(S("seg_ready"), due("seg_ready"))

            def head_weights(h):
                dve.wait_ge(S("seg_exp_ready"), due("seg_exp_ready"))
                w = W[:, h % 3, :]
                s = seg[:, h % 2, :]
                products = BC[:, h // 4, :]
                for out_, at, scalar, by in ((w[:, 0:128], 0, col(0, h), products[:, 0:128]),
                                             (s[:, 384:512], 384, col(0, 8 + h), BC_back[:, h // 4, 0:128]),
                                             (w[:, 128:256], 128, col(0, h), products[:, 128:256]),
                                             (w[:, 256:384], 512, col(1, 8 + h), products[:, 256:384]),
                                             (w[:, 384:512], 256, col(1, h), products[:, 384:512]),
                                             (s[:, 640:768], 640, col(1, 8 + h), BC_back[:, h // 4, 128:256])):
                    dve.scalar_tensor_tensor(out=out_, in0=s[:, at:at + 128], scalar=scalar, in1=by, op0=ALU.mult, op1=ALU.mult).then_inc(S("dve_step"), 1)
                    dve.wait_ge(S("dve_step"), due("dve_step"))
                w2 = w.rearrange("p (n i) -> p n i", n=4)[:, 0:4:3, :]
                s2 = s[:, 384:896 - 128].rearrange("p (n i) -> p n i", n=3)[:, 0:3:2, :]
                dve.tensor_tensor(w2, w2, s2, ALU.add).then_inc(S("w_ready"), 1)
                dve.wait_ge(S("w_ready"), due("w_ready"))

            head_args(0)
            head_args(1)
            for t in range(2):
                dve.wait_ge(S("fullD"), due("fullD"))
                b = bank_of("D", T.n["fullD"])
                o = O[:, t, 0:512]
                dve.tensor_copy(o, b[:, :]).then_inc(S("freeD"), 1)
                dve.wait_ge(S("freeD"), due("freeD"))
                dve.tensor_tensor(prod2, o, o, ALU.mult).then_inc(S("dve_step"), 1)
                dve.wait_ge(S("dve_step"), due("dve_step"))
                dve.tensor_reduce(sc[:, 4 * t:4 * t + 4], prod2.rearrange("p (h v) -> p h v", h=4), AX, ALU.add).then_inc(S("dve_step"), 1)
                dve.wait_ge(S("dve_step"), due("dve_step"))
            start_norm(8, 128)
            for h in range(8):
                head_weights(h)
                if h < 6:
                    head_args(h + 2)
                if h:
                    continue
                dve.wait_ge(S("rstd_ready"), due("rstd_ready"))
                for t in range(2):
                    o = O[:, t, 0:512]
                    o3 = o.rearrange("p (h v) -> p h v", h=4)
                    dve.tensor_tensor(o3, o3, bc(rs[:, 4 * t:4 * t + 4], P), ALU.mult).then_inc(S("dve_step"), 1)
                    dve.wait_ge(S("dve_step"), due("dve_step"))
                    dve.tensor_tensor(o3, o3, gla_gain.unsqueeze(1).to_broadcast([P, 4, P]), ALU.mult).then_inc(S("dve_step"), 1)
                    dve.wait_ge(S("dve_step"), due("dve_step"))
                    dve.tensor_tensor(o, o, silu_r[:, t, :], ALU.mult).then_inc(S("dve_step"), 1)
                    dve.wait_ge(S("dve_step"), due("dve_step"))
            dve.wait_ge(S("intra_ready"), due("intra_ready"))
            for t in range(2):
                y = O[:, t, 512:1024]
                dve.tensor_tensor(y, y, intra[:, t, :], ALU.add).then_inc(S("dve_step"), 1)
                dve.wait_ge(S("dve_step"), due("dve_step"))
                dve.tensor_tensor(y, y, silu_z[:, t, :], ALU.mult).then_inc(S("dve_step"), 1)
                dve.wait_ge(S("dve_step"), due("dve_step"))
                dve.tensor_tensor(lev_tmp, y, y, ALU.mult).then_inc(S("dve_step"), 1)
                dve.wait_ge(S("dve_step"), due("dve_step"))
                dve.tensor_reduce(sc[:, 2 * t:2 * t + 2], lev_tmp.rearrange("p (g v) -> p g v", g=2), AX, ALU.add).then_inc(S("dve_step"), 1)
                dve.wait_ge(S("dve_step"), due("dve_step"))
            start_norm(4, 256)
            dve.wait_ge(S("rstd_ready"), due("rstd_ready"))
            for t in range(2):
                y = O[:, t, 512:1024]
                y2 = y.rearrange("p (g v) -> p g v", g=2)
                dve.tensor_tensor(y2, y2, bc(rs[:, 2 * t:2 * t + 2], 256), ALU.mult).then_inc(S("dve_step"), 1)
                dve.wait_ge(S("dve_step"), due("dve_step"))
                dve.tensor_tensor(y, y, ssd_gain, ALU.mult).then_inc(S("dve_step"), 1)
                dve.wait_ge(S("dve_step"), due("dve_step"))

            def gate_and_gain(which):
                for n in range(2):
                    dve.wait_ge(S("fullD"), due("fullD"))
                    b = bank_of("D", T.n["fullD"])
                    dve.tensor_copy(gate3_b[:, 0, n * 512:n * 512 + 512], b[:, :]).then_inc(S("freeD"), 1)
                    dve.wait_ge(S("freeD"), due("freeD"))
                if which == 0:
                    dve.memset(flag, 0.0).then_inc(S("mixer2_done"), 1)
                    dve.wait_ge(S("mixer2_done"), due("mixer2_done"))
                dve.wait_ge(S("gain_landed"), due("gain_landed", 16))
                dve.tensor_tensor(gate3_b[:, 0, :], gate3_b[:, 0, :], gain_b, ALU.mult).then_inc(S("dve_step"), 1)
                dve.wait_ge(S("dve_step"), due("dve_step"))
                dve.memset(flag, 0.0).then_inc(S("gain_used"), 1)
                dve.wait_ge(S("gain_used"), due("gain_used"))

            def post(last):
                for t in range(2):
                    dve.tensor_tensor_reduce(xn3[:, t, :], Y[:, t, :], Y[:, t, :], 1.0, 0.0, ALU.mult, ALU.add, sc[:, t:t + 1]).then_inc(S("dve_step"), 1)
                    dve.wait_ge(S("dve_step"), due("dve_step"))
                start_norm(2, D)
                dve.wait_ge(S("rstd_ready"), due("rstd_ready"))
                for t in range(2):
                    dve.scalar_tensor_tensor(out=Y[:, t, :], in0=Y[:, t, :], scalar=rs[:, t:t + 1], in1=gate3_b[:, 0, :],
                                             op0=ALU.mult, op1=ALU.mult).then_inc(S("dve_step"), 1)
                    dve.wait_ge(S("dve_step"), due("dve_step"))
                    signal = "out_ready_rows" if last else "dve_step"
                    dve.tensor_tensor(X[:, t, :], X[:, t, :], Y[:, t, :], ALU.add).then_inc(S(signal), 1)
                    dve.wait_ge(S(signal), due(signal))

            gate_and_gain(0)
            dve.memset(flag, 0.0).then_inc(S("o_ready"), 1)
            dve.wait_ge(S("o_ready"), due("o_ready"))
            for k in range(0, KD, 2):
                dve.wait_ge(S("fullD"), due("fullD"))
                b = bank_of("D", T.n["fullD"])
                dve.tensor_copy(oT2[:, k, :], b[:, 0:SEQ]).then_inc(S("freeD"), 1)
                dve.wait_ge(S("freeD"), due("freeD"))
                dve.memset(flag, 0.0).then_inc(S("oT2_ready_dve"), 1)
                dve.wait_ge(S("oT2_ready_dve"), due("oT2_ready_dve"))

            def take_y():
                for n in range(2):
                    for t in range(2):
                        dve.wait_ge(S("fullD"), due("fullD"))
                        b = bank_of("D", T.n["fullD"])
                        dve.tensor_copy(Y[:, t, n * 512:n * 512 + 512], b[:, :]).then_inc(S("freeD"), 1)
                        dve.wait_ge(S("freeD"), due("freeD"))

            take_y()
            post(False)
            gate_and_gain(1)
            norm(xn3, range(2))
            modulate(h3T, 5, 1)
            for blk in range(FB):
                dve.wait_ge(S("fullD"), due("fullD"))
                b = bank_of("D", T.n["fullD"])
                dve.wait_ge(S("ff_silu_ready"), due("ff_silu_ready"))
                dve.tensor_tensor(ffT[:, blk, :], b[:, SEQ:512], ff_silu[:, blk % 2, :], ALU.mult).then_inc(S("ffT_ready"), 1)
                dve.wait_ge(S("ffT_ready"), due("ffT_ready"))
                dve.memset(flag, 0.0).then_inc(S("freeD"), 1)
                dve.wait_ge(S("freeD"), due("freeD"))
            take_y()
            post(True)

        def act_block2(act, T, norm, modulate):
            due = T.step
            act.wait_ge(S("block1_done"), due("block1_done"))
            act.dma_start(final_gain, A["final_g"].partition_broadcast(P)).then_inc(S("final_gain_landed"), 16)
            act.dma_start(X[:, 2:4, :], A["ctx_2"][0].rearrange("(t p) n -> p t n", p=P)).then_inc(S("ctx2_landed"), 16)
            act.dma_start(wg[0:16, 0, :], A["gla_wg_f_2"][0]).then_inc(S("wg_landed"), 16)
            act.dma_start(wg[16:32, 1, :], A["gla_wg_b_2"][0]).then_inc(S("wg_landed"), 16)
            for dst, src in rows2_loads:
                act.dma_start(dst, src).then_inc(S("block2_rows_landed"), 16)
            norm(2)
            norm(TILES)
            modulate(hT, 4, 2)
            for blk in (1, 3, 5):
                act.wait_ge(S("fullA"), due("fullA"))
                b = bank_of("A", T.n["fullA"])
                act.activation(x_raw[:, blk, :], b[:, :], ACT.Copy).then_inc(S("freeA"), 1)
                act.wait_ge(S("freeA"), due("freeA"))
                act.activation(flag_a, zero, ACT.Copy).then_inc(S("x_raw_ready_act"), 1)
                act.wait_ge(S("x_raw_ready_act"), due("x_raw_ready_act"))

            def log1p_exp_neg_abs(dst, src):
                act.activation(dst, src, ACT.Abs).then_inc(S("act_step"), 1)
                act.wait_ge(S("act_step"), due("act_step"))
                act.activation(dst, dst, ACT.Exp, scale=-1.0).then_inc(S("act_step"), 1)
                act.wait_ge(S("act_step"), due("act_step"))
                act.activation(dst, dst, ACT.Ln, bias=ones[0:dst.shape[0], :]).then_inc(S("act_step"), 1)
                act.wait_ge(S("act_step"), due("act_step"))

            act.wait_ge(S("dt_raw_ready"), due("dt_raw_ready"))
            act.wait_ge(S("block2_rows_landed"), 16 * N_ROWS2)
            log1p_exp_neg_abs(dt_rows[0:16, :], dt_raw[0:16, :])
            act.activation(neg_a, neg_a, ACT.Exp).then_inc(S("act_step"), 1)
            act.wait_ge(S("act_step"), due("act_step"))
            act.activation(flag_a, zero, ACT.Copy).then_inc(S("dt_log_ready"), 1)
            act.wait_ge(S("dt_log_ready"), due("dt_log_ready"))
            for blk in range(2):
                act.wait_ge(S("fullA"), due("fullA"))
                b = bank_of("A", T.n["fullA"])
                act.activation(kc[:, blk, :], b[:, :], ACT.Copy).then_inc(S("freeA"), 1)
                act.wait_ge(S("freeA"), due("freeA"))
            act.wait_ge(S("gates_raw_ready"), due("gates_raw_ready"))
            log1p_exp_neg_abs(gate_tmp, gates)
            act.activation(flag_a, zero, ACT.Copy).then_inc(S("gates_log_ready"), 1)
            act.wait_ge(S("gates_log_ready"), due("gates_log_ready"))
            act.wait_ge(S("conv_ready"), due("conv_ready", 6))
            for blk in range(6):
                act.activation(xbc[:, blk, :], xbc[:, blk, :], ACT.Silu, bias=vecs[:, 2, 80 + blk:81 + blk]).then_inc(S("act_step"), 1)
                act.wait_ge(S("act_step"), due("act_step"))
            act.activation(flag_a, zero, ACT.Copy).then_inc(S("xbc_ready"), 1)
            act.wait_ge(S("xbc_ready"), due("xbc_ready"))
            act.wait_ge(S("fullA"), due("fullA"))
            b = bank_of("A", T.n["fullA"])
            act.activation(V2[:, 1, :], b[:, :], ACT.Copy).then_inc(S("freeA"), 1)
            act.wait_ge(S("freeA"), due("freeA"))
            act.wait_ge(S("decays_ready"), due("decays_ready"))
            act.activation(decays[0:16, :, :], decays[0:16, :, :], ACT.Exp).then_inc(S("decays_exp_ready"), 1)
            act.wait_ge(S("decays_exp_ready"), due("decays_exp_ready"))
            act.wait_ge(S("fullA"), due("fullA"))
            b = bank_of("A", T.n["fullA"])
            act.activation(V2[:, 3, :], b[:, :], ACT.Copy).then_inc(S("freeA"), 1)
            act.wait_ge(S("freeA"), due("freeA"))
            for t in range(2):
                act.wait_ge(S("fullA"), due("fullA"))
                b = bank_of("A", T.n["fullA"])
                act.activation(silu_r[:, t, :], b[:, :], ACT.Silu).then_inc(S("freeA"), 1)
                act.wait_ge(S("freeA"), due("freeA"))
            act.wait_ge(S("qd_raw_ready"), due("qd_raw_ready"))
            both = area(15872, 2048)
            act.activation(both, both, ACT.Exp).then_inc(S("qd_exp_ready"), 1)
            act.wait_ge(S("qd_exp_ready"), due("qd_exp_ready"))
            for t in range(TILES):
                act.wait_ge(S("fullA"), due("fullA"))
                b = bank_of("A", T.n["fullA"])
                act.activation(XS[:, t, :], b[:, :], ACT.Copy).then_inc(S("freeA"), 1)
                act.wait_ge(S("freeA"), due("freeA"))
            act.wait_ge(S("fullA"), due("fullA"))
            b = bank_of("A", T.n["fullA"])
            act.activation(BT, b[:, 0:256].rearrange("p (c n) -> p c n", c=2), ACT.Copy).then_inc(S("freeA"), 1)
            act.wait_ge(S("freeA"), due("freeA"))
            act.activation(flag_a, zero, ACT.Copy).then_inc(S("xs_ready"), 1)
            act.wait_ge(S("xs_ready"), due("xs_ready"))
            for d in range(2):
                act.wait_ge(S("fullA"), due("fullA"))
                b = bank_of("A", T.n["fullA"])
                act.activation(KDt[:, d, :], b[:, :], ACT.Copy).then_inc(S("freeA"), 1)
                act.wait_ge(S("freeA"), due("freeA"))
            act.activation(flag_a, zero, ACT.Copy).then_inc(S("kdt_ready"), 1)
            act.wait_ge(S("kdt_ready"), due("kdt_ready"))

            def level_exp(l):
                act.wait_ge(S("level_args_ready"), due("level_args_ready"))
                act.activation(lev[:, l % 2, :], lev[:, l % 2, :], ACT.Exp).then_inc(S("level_exp_ready"), 1)
                act.wait_ge(S("level_exp_ready"), due("level_exp_ready"))

            level_exp(1)
            for t in range(2):
                act.wait_ge(S("fullA"), due("fullA"))
                b = bank_of("A", T.n["fullA"])
                act.activation(silu_z[:, t, :], b[:, :], ACT.Silu).then_inc(S("freeA"), 1)
                act.wait_ge(S("freeA"), due("freeA"))
            for l in range(2, 9):
                level_exp(l)

            def root(n):
                act.wait_ge(S("inv_ready"), due("inv_ready"))
                act.activation(small[:, 126:126 + n], small[:, 118:118 + n], ACT.Sqrt).then_inc(S("rstd_ready"), 1)
                act.wait_ge(S("rstd_ready"), due("rstd_ready"))

            def head_exp(h):
                act.wait_ge(S("seg_ready"), due("seg_ready"))
                s = seg[:, h % 2, :]
                act.activation(s[:, 0:384], s[:, 0:384], ACT.Exp).then_inc(S("act_step"), 1)
                act.wait_ge(S("act_step"), due("act_step"))
                act.activation(s[:, 384:768], s[:, 384:768], ACT.Exp, scale=-1.0).then_inc(S("seg_exp_ready"), 1)
                act.wait_ge(S("seg_exp_ready"), due("seg_exp_ready"))

            head_exp(0)
            head_exp(1)
            root(8)
            for h in range(8):
                if h < 6:
                    head_exp(h + 2)
                act.wait_ge(S("fullA"), due("fullA"))
                b = bank_of("A", T.n["fullA"])
                act.activation(intra[:, :, h * HD:h * HD + HD], b[:, 0:P].rearrange("p (t v) -> p t v", t=2), ACT.Copy).then_inc(S("freeA"), 1)
                act.wait_ge(S("freeA"), due("freeA"))
            act.activation(flag_a, zero, ACT.Copy).then_inc(S("intra_ready"), 1)
            act.wait_ge(S("intra_ready"), due("intra_ready"))
            root(4)
            act.wait_ge(S("mixer2_done"), due("mixer2_done"))
            act.dma_start(gain_b, A["norm_mix_post_2"][0].partition_broadcast(P)).then_inc(S("gain_landed"), 16)
            for k in range(1, KD, 2):
                act.wait_ge(S("fullA"), due("fullA"))
                b = bank_of("A", T.n["fullA"])
                act.activation(oT2[:, k, :], b[:, 0:SEQ], ACT.Copy).then_inc(S("freeA"), 1)
                act.wait_ge(S("freeA"), due("freeA"))
                act.activation(flag_a, zero, ACT.Copy).then_inc(S("oT2_ready_act"), 1)
                act.wait_ge(S("oT2_ready_act"), due("oT2_ready_act"))
            root(2)
            act.wait_ge(S("gain_used"), due("gain_used"))
            act.dma_start(gain_b, A["norm_ffn_post_2"][0].partition_broadcast(P)).then_inc(S("gain_landed"), 16)
            norm(2)
            modulate(h3T, 5, 1)
            for blk in range(FB):
                job = ff_first[0] + blk
                if blk > 1:
                    act.wait_ge(S("ffT_ready"), blk - 1)
                act.wait_ge(S("fullD"), job)
                act.activation(ff_silu[:, blk % 2, :], pool_banks["D"][(job - 1) % POOL][:, 0:SEQ], ACT.Silu).then_inc(S("ff_silu_ready"), 1)
                act.wait_ge(S("ff_silu_ready"), due("ff_silu_ready"))
            root(2)
            for t in range(2):
                act.wait_ge(S("out_ready_rows"), t + 1)
                act.dma_start(out[0, t * P:t * P + P, :], X[:, t, :]).then_inc(S("out_stored"), 16)
            act.wait_ge(S("out_stored"), 32)

        rows2_loads = [(gla_gain, A["gla_norm_2"][0].partition_broadcast(P)), (ssd_gain, A["ssd_norm_2"][0].partition_broadcast(P)),
                       (skip_gain, A["d_skip_2"][0].partition_broadcast(P))]
        for at, d in ((0, "f"), (8, "b")):
            rows2_loads.append((small[at:at + 8, 100:101], A[f"dt_bias_{d}_2"][0].rearrange("(h a) -> h a", a=1)))
            rows2_loads.append((small[at:at + 8, 101:102], A[f"a_log_{d}_2"][0].rearrange("(h a) -> h a", a=1)))
        N_ROWS2 = len(rows2_loads)

        @block.tensor
        def _(pe):
            T = Tally()
            due = T.step

            def release(pool, units=1):
                for _ in range(units):
                    released.append((pool, T.n["free" + pool], T.per and T.per["free" + pool]))

            def next_slot():
                T.step("ring")
                return (T.n["ring"] - 1) % RING

            def turn(dst, src):
                return pe.transpose(dst, src, ident[0:src.shape[0], 0:src.shape[0]])

            def mod_step(cur, turned):
                if cur:
                    l, seg = cur
                    pe.wait_ge(S("freeD"), due("freeD"))
                    b = bank_of("D", T.n["freeD"])
                    r0 = next_slot()
                    pe.wait_ge(S(f"slot_landed{r0}"), due(f"slot_landed{r0}", 16))
                    r1 = next_slot()
                    pe.wait_ge(S(f"slot_landed{r1}"), due(f"slot_landed{r1}", 16))
                    for k in range(KD):
                        for h, r in ((0, r0), (1, r1)):
                            mm = pe.matmul(b[64 * h:64 * h + 2, :], silu_c[:, l, k, :], slot_view(r)[:, k, :],
                                           start=(k == 0), stop=(k == KD - 1))
                    mm.then_inc(S("fullD"), 1)
                    release("D", 2)
                if turned:
                    pe.wait_ge(S("seg_row_ready"), due("seg_row_ready"))
                    pe.wait_ge(S("freeD"), due("freeD"))
                    b = bank_of("D", T.n["freeD"])
                    for k in range(KD):
                        mm = pe.transpose(b[:, 2 * k:2 * k + 2], row_tmp[:, turned[1] % 3, k * P:k * P + P], ident[96:98, 96:98])
                    mm.then_inc(S("fullD"), 1)

            def turn_streams(src, tiles):
                for k in range(KD):
                    pool = "DA"[k % 2]
                    pe.wait_ge(S("free" + pool), due("free" + pool))
                    b = bank_of(pool, T.n["free" + pool])
                    for t in tiles:
                        mm = turn(b[:, t * P:t * P + P], src[:, t, k * P:k * P + P])
                        if t == tiles[-1]:
                            mm.then_inc(S("full" + pool), 1)

            def dense(pool, t, r, lhs, c0=0, c1=512, ks=KD, signal=None):
                pe.wait_ge(S("free" + pool), due("free" + pool))
                b = bank_of(pool, T.n["free" + pool])
                for k in range(ks):
                    mm = pe.matmul(b[:, 0:c1 - c0], lhs[:, k, t * P:t * P + P], slot_view(r)[:, k, c0:c1],
                                   start=(k == 0), stop=(k == ks - 1))
                mm.then_inc(S("full" + pool), 1)
                return mm

            def broadcast_gate(l, g, streams):
                rows_ = slice(32 * l, 32 * l + 2)
                for s in range(streams):
                    for n in range(2):
                        pe.wait_ge(S("freeD"), due("freeD"))
                        b = bank_of("D", T.n["freeD"])
                        pe.matmul(b[:, :], ident[rows_, 32 * l + s:32 * l + s + 1].to_broadcast([2, P]),
                                  gate_rows[rows_, g, n * 512:n * 512 + 512],
                                  start=True, stop=True).then_inc(S("fullD"), 1)

            def mixer(l):
                tiles = range(TILES)
                own = range(TILES) if l == 0 else range(2)
                pe.wait_ge(S("xn_ready"), due("xn_ready", TILES))
                turn_streams(xn, range(TILES))
                pe.wait_ge(S("hT_ready_dve"), due("hT_ready_dve", 4 * 1))
                pe.wait_ge(S("hT_ready_act"), due("hT_ready_act", 4 * 1))
                for u in range(3):
                    r = next_slot()
                    pe.wait_ge(S(f"slot_landed{r}"), due(f"slot_landed{r}", 16))
                    for t in tiles:
                        lone = t not in own
                        if lone and u == 0:
                            continue
                        dense("DA"[t % 2], t, r, hT, 256 if lone else 0, 512)
                    release("A")
                pe.wait_ge(S("z_ready_dve"), due("z_ready_dve"))
                pe.wait_ge(S("z_ready_act"), due("z_ready_act"))
                for s in range(len(own) // 2):
                    for c in range(2):
                        pe.wait_ge(S("freeD"), due("freeD"))
                        b = bank_of("D", T.n["freeD"])
                        for t in range(2):
                            mm = pe.matmul(b[:, :], Z[:, 2 * s + t, c * P:c * P + P], C("dft_pos", 2, 512)[:, t, :],
                                           start=(t == 0), stop=(t == 1))
                        mm.then_inc(S("fullD"), 1)
                    for c in range(2):
                        pe.wait_ge(S("four_ready"), due("four_ready"))
                        pe.wait_ge(S("freeA"), due("freeA"))
                        b = bank_of("A", T.n["freeA"])
                        pe.matmul(b[:, 0:SEQ], C("dft_cos"), four[:, c, 0:SEQ], start=True, stop=False)
                        pe.matmul(b[:, 0:SEQ], C("dft_nsin"), four[:, c, SEQ:512], start=False, stop=True)\
                            .then_inc(S("fullA"), 1)
                pe.wait_ge(S("rope_ready"), due("rope_ready"))
                for t in own:
                    turn_q(t)
                for t in tiles:
                    turn_k(t)
                attention(l, len(own) // 2)
                for n in range(2):
                    for br, ks in ((0, 2), (1, 4), (2, 2)):
                        rg = next_slot()
                        pe.wait_ge(S(f"slot_landed{rg}"), due(f"slot_landed{rg}", 16))
                        for t in own:
                            dense("A", t, rg, hT)
                        release("A")
                        rb = next_slot()
                        pe.wait_ge(S(f"slot_landed{rb}"), due(f"slot_landed{rb}", 16))
                        lhs = {0: fT, 1: oT[:, 0:4, :], 2: oT[:, 4:6, :]}[br]
                        if n == 0 and br == 0:
                            pe.wait_ge(S("fT_ready"), due("fT_ready", len(own)))
                        if n == 0 and br == 1:
                            pe.wait_ge(S("oT_ready"), due("oT_ready", 6 * (len(own) // 2)))
                        for t in own:
                            dense("D", t, rb, lhs, ks=ks)
                        release("D")
                broadcast_gate(l, 0, len(own) // 2)
                pe.wait_ge(S("m_ready"), due("m_ready"))
                turn_streams(m_sum, list(own))
                pe.wait_ge(S("mT_ready_dve"), due("mT_ready_dve", 4))
                pe.wait_ge(S("mT_ready_act"), due("mT_ready_act", 4))
                r0 = next_slot()
                pe.wait_ge(S(f"slot_landed{r0}"), due(f"slot_landed{r0}", 16))
                r1 = next_slot()
                pe.wait_ge(S(f"slot_landed{r1}"), due(f"slot_landed{r1}", 16))
                for t in own:
                    dense("D", t, r0, mT)
                    dense("D", t, r1, mT)
                release("D", 2)

            def turn_q(t):
                pe.wait_ge(S("freeD"), due("freeD"))
                b = bank_of("D", T.n["freeD"])
                for h in range(4):
                    mm = turn(b[:, h * P:h * P + P], Z[:, t, GQ + h * P:GQ + h * P + P])
                    if h == 3:
                        mm.then_inc(S("fullD"), 1)
                pe.wait_ge(S("freeD"), due("freeD"))
                b = bank_of("D", T.n["freeD"])
                for h in range(2):
                    mm = turn(b[:, h * P:h * P + P], Z[:, t, WQ + h * P:WQ + h * P + P])
                    if h == 1:
                        mm.then_inc(S("fullD"), 1)

            def turn_k(t):
                pe.wait_ge(S("freeD"), due("freeD"))
                b = bank_of("D", T.n["freeD"])
                turn(b[:, 0:P], Z[:, t, GK:GK + P])
                turn(b[:, P:2 * P], Z[:, t, WK:WK + P]).then_inc(S("fullD"), 1)

            def attention(l, streams):
                pe.wait_ge(S("qT_ready"), due("qT_ready", 8 * streams))
                pe.wait_ge(S("kT_ready"), due("kT_ready", 4 + 2 * 4))
                groups = [(t // 2, t, grp) for t in range(2 * streams) for grp in range(3)]

                def scores(s, t, grp):
                    k0 = 2 * s * P
                    at = slice(64 * s, 64 * s + 64)
                    for h in range(4):
                        kv = grp if grp < 2 else 2 + h // 2
                        pe.wait_ge(S("freeD"), due("freeD"))
                        b = bank_of("D", T.n["freeD"])
                        pe.matmul(b[:, 0:512 - k0], qT[at, 4 * grp + h, (t % 2) * P:(t % 2) * P + P],
                                  kT[at, kv, k0:512], start=True, stop=True).then_inc(S("fullD"), 1)

                scores(*groups[0])
                for step, (s, t, grp) in enumerate(groups):
                    if step + 1 < len(groups):
                        scores(*groups[step + 1])
                    if step < len(LATE_STEPS[l]):
                        mod_step(*LATE_STEPS[l][step])
                    probs = probs_buf[step % 2]
                    keys = range(2 * s, TILES)
                    pe.wait_ge(S("probs_ready"), due("probs_ready", 4))
                    for kt in keys:
                        pe.wait_ge(S("freeA"), due("freeA"))
                        b = bank_of("A", T.n["freeA"])
                        for h in range(4):
                            mm = turn(b[:, h * P:h * P + P], probs[:, h, (kt - keys[0]) * P:(kt - keys[0] + 1) * P])
                            if h == 3:
                                mm.then_inc(S("fullA"), 1)
                    pe.wait_ge(S("probsT_ready"), due("probsT_ready", len(keys)))
                    pe.wait_ge(S("freeA"), due("freeA"))
                    b = bank_of("A", T.n["freeA"])
                    pT = probsT.rearrange("p k (a two i) -> p k a two i", two=2, i=P)
                    for part in ((slice(0, 2),) if grp < 2 else (slice(0, 1), slice(1, 2))):
                        v0 = GV + HD * grp if grp < 2 else WV + HD * part.start
                        for kt in keys:
                            for odd in range(2):
                                mm = pe.matmul(b[64 * odd:64 * odd + 64, part.start * P:part.stop * P], Z[:, kt, v0:v0 + HD],
                                               pT[:, kt, part, odd, :], start=(kt == keys[0]), stop=(kt == keys[-1]))
                    mm.then_inc(S("fullA"), 1)

            def experts(l):
                ns = 2 if l == 0 else 1
                tiles = range(2 * ns)
                R = CAP * ns
                pe.wait_ge(S("xn_ready"), due("xn_ready", 2 * ns))
                turn_streams(xn2, list(tiles))
                pe.wait_ge(S("hT_ready_dve"), due("hT_ready_dve", 4))
                pe.wait_ge(S("hT_ready_act"), due("hT_ready_act", 4))
                pe.wait_ge(S("freeD"), due("freeD"))
                b = bank_of("D", T.n["freeD"])
                for t in tiles:
                    for k in range(KD):
                        mm = pe.matmul(b[:, t * E:t * E + E], h2T[:, k, t * P:t * P + P], w_router[:, l, k, :],
                                       start=(k == 0), stop=(k == KD - 1))
                mm.then_inc(S("fullD"), 1)
                broadcast_gate(l, 1, ns)
                pe.wait_ge(S("aff_ready"), due("aff_ready"))
                pe.wait_ge(S("freeD"), due("freeD"))
                b = bank_of("D", T.n["freeD"])
                for t in tiles:
                    mm = turn(b[0:E, t * P:t * P + P], aff[:, t, :])
                    if t == tiles[-1]:
                        mm.then_inc(S("fullD"), 1)
                pe.wait_ge(S("slots_ready"), due("slots_ready"))
                pe.wait_ge(S("freeD"), due("freeD"))
                b = bank_of("D", T.n["freeD"])
                for t in tiles:
                    mm = turn(b[:, t * E:t * E + E], cum[0:E, t * P:t * P + P])
                    if t == tiles[-1]:
                        mm.then_inc(S("fullD"), 1)
                pe.wait_ge(S("pick_ready"), due("pick_ready"))
                for k in range(KD):
                    for s in range(ns):
                        pool = "DA"[s] if ns == 2 else "DA"[k % 2]
                        pe.wait_ge(S("free" + pool), due("free" + pool))
                        b = bank_of(pool, T.n["free" + pool])
                        for t in (2 * s, 2 * s + 1):
                            mm = pe.matmul(b[:, :], xn2[:, t, k * P:k * P + P], pick[:, t, :],
                                           start=(t == 2 * s), stop=(t == 2 * s + 1))
                        mm.then_inc(S("full" + pool), 1)
                for t in tiles:
                    pe.wait_ge(S("freeD"), due("freeD"))
                    b = bank_of("D", T.n["freeD"])
                    for g in range(4):
                        mm = turn(b[:, g * P:g * P + P], pick_g[:, t, g * P:g * P + P])
                        if g == 3:
                            mm.then_inc(S("fullD"), 1)
                def scatter():
                    for t in tiles:
                        for n in range(2):
                            pe.wait_ge(S("freeD"), due("freeD"))
                            b = bank_of("D", T.n["freeD"])
                            pe.matmul(b[:, :], puts[:, t, :], out_g[:, stream_of(t), n * 512:n * 512 + 512],
                                      start=True, stop=True).then_inc(S("fullD"), 1)

                per = {"ring": 24, "freeD": 16 + 4 * ns, "xgs_ready": 1, "hid_ready": 4 * 2,
                       "hidT_ready": 4, "out_ready": 4, "puts_ready": 1, **{f"slot_landed{r}": 96 for r in range(RING)}}
                expert_start[l] = T.n["freeD"]
                with pe.Fori(0, 4) as i:
                    T.enter(i, per)
                    pe.wait_ge(S("xgs_ready"), due("xgs_ready"))
                    for j in range(4):
                        for n in range(2):
                            rg = next_slot()
                            pe.wait_ge(S(f"slot_landed{rg}"), due(f"slot_landed{rg}", 16))
                            ru = next_slot()
                            pe.wait_ge(S(f"slot_landed{ru}"), due(f"slot_landed{ru}", 16))
                            pe.wait_ge(S("freeD"), due("freeD"))
                            b = bank_of("D", T.n["freeD"])
                            for k in range(KD):
                                for c, r in ((0, rg), (64, ru)):
                                    mm = pe.matmul(b[c:c + R, :], xgs[:, k, j, 0:R], slot_view(r)[:, k, :],
                                                   start=(k == 0), stop=(k == KD - 1))
                            mm.then_inc(S("fullD"), 1)
                            release("D", 2)
                        if j == 0:
                            pe.wait_ge(S("puts_ready"), due("puts_ready"))
                            scatter()
                        pe.wait_ge(S("hid_ready"), due("hid_ready", 2))
                        pe.wait_ge(S("freeD"), due("freeD"))
                        b = bank_of("D", T.n["freeD"])
                        pe.nop(nofuse=True)
                        for k in range(KD):
                            mm = turn(b[:, k * 64:k * 64 + R], hid[0:R, k * P:k * P + P])
                            if k == KD - 1:
                                mm.then_inc(S("fullD"), 1)
                        pe.wait_ge(S("hidT_ready"), due("hidT_ready"))
                        r0 = next_slot()
                        pe.wait_ge(S(f"slot_landed{r0}"), due(f"slot_landed{r0}", 16))
                        r1 = next_slot()
                        pe.wait_ge(S(f"slot_landed{r1}"), due(f"slot_landed{r1}", 16))
                        pe.wait_ge(S("freeD"), due("freeD"))
                        b = bank_of("D", T.n["freeD"])
                        for k in range(KD):
                            for n, r in ((0, r0), (1, r1)):
                                mm = pe.matmul(b[64 * n:64 * n + R, :], hidT[:, k, 0:R], slot_view(r)[:, k, :],
                                               start=(k == 0), stop=(k == KD - 1))
                        mm.then_inc(S("fullD"), 1)
                        release("D", 2)
                    pe.wait_ge(S("out_ready"), due("out_ready", 4))
                T.leave(4)
                pe.wait_ge(S("puts_ready"), due("puts_ready"))
                scatter()

            pe.wait_ge(S("const_landed"), 16)
            pe.wait_ge(S("vecs_landed"), due("vecs_landed", 16 * N_VEC))
            pe.wait_ge(S("small_ready"), due("small_ready"))
            pe.wait_ge(S("freeD"), due("freeD"))
            b = bank_of("D", T.n["freeD"])
            for v in range(4):
                mm = turn(b[:, v * P:v * P + VEC_ROWS[v]], vec_in[0:VEC_ROWS[v], v, :])
                if v == 3:
                    mm.then_inc(S("fullD"), 1)
            pe.wait_ge(S("silu_c_ready"), due("silu_c_ready", 6))
            for step in EARLY_STEPS:
                mod_step(*step)
            for l in range(DEPTH):
                mixer(l)
                experts(l)
            pe_block2(pe, T, next_slot, release, turn, turn_streams, dense, broadcast_gate)

        @block.sync
        def _(sp):
            T = Tally()
            due = T.step

            def load(*pieces, in_loop=False, turn=None):
                n = T.step("ring")
                n = T.n["ring"]
                if n > RING:
                    pool, jobs, per = released[n - RING - 1]
                    sp.wait_ge(S("full" + pool), jobs + (per or 0) * (turn if in_loop else 3 if per else 0))
                r = (T.n["ring"] - 1) % RING
                for dst, src in pieces:
                    sp.dma_start(dst(r), src).then_inc(S(f"slot_landed{r}"), 16)

            def load_cols(w, c0, c1):
                wd = c1 - c0
                load((lambda r: slot_view(r)[:, :, 0:wd], big(w, c0, c1)))

            def load_mod_step(cur, turned):
                if cur:
                    for h in range(2):
                        c0 = cur[1] * D + 512 * h
                        load_cols(LAYERS[cur[0]]["w_mod"], c0, c0 + 512)

            for dst, src in vec_loads:
                sp.dma_start(dst, src).then_inc(S("vecs_landed"), 16)
            for step in EARLY_STEPS:
                load_mod_step(*step)
            for l, L in enumerate(LAYERS):
                for g in range(2):
                    src = L["b_mod"][L["row"], (2 + 3 * g) * D:(3 + 3 * g) * D]
                    sp.dma_start(gate_rows[32 * l:32 * l + 2, g, :], src.partition_broadcast(2)).then_inc(S("gate_bias_landed"), 16)
            for l in range(DEPTH):
                w = A["w_in"][l]
                for u in range(3):
                    load_cols(w, 512 * u, 512 * u + 512)
                for step in LATE_STEPS[l]:
                    load_mod_step(*step)
                wb = {"w_br_fourier": 2, "w_br_global": 4, "w_br_window": 2}
                for n in range(2):
                    for b, (name, k) in enumerate(wb.items()):
                        load_cols(w, Z_W + b * D + n * 512, Z_W + b * D + n * 512 + 512)
                        load((lambda r, k=k: slot_view(r)[:, 0:k, :],
                              A[name][l][:, n * 512:n * 512 + 512].rearrange("(k p) n -> p k n", p=P)))
                for n in range(2):
                    load_cols(A["w_out"][l], 512 * n, 512 * n + 512)
                def expert_unit(g, q, turn=None):
                    j, name, n = q // 6, ("w_gate_e", "w_up_e", "w_gate_e", "w_up_e", "w_down_e", "w_down_e")[q % 6], (0, 0, 1, 1, 0, 1)[q % 6]
                    src = A[name][l].rearrange("(g j) (k p) n -> g j p k n", j=4, p=P)
                    load((lambda r: slot_view(r), src[g, j, :, :, n * 512:n * 512 + 512]), in_loop=turn is not None, turn=turn)

                for q in range(RING):
                    expert_unit(0, q)
                with sp.Fori(0, 3) as i:
                    for q in range(RING, 24):
                        expert_unit(i, q, turn=i)
                    for q in range(RING):
                        expert_unit(i + 1, q, turn=i)
                T.n["ring"] -= 24
                for q in range(RING, 24):
                    expert_unit(3, q)
            load_block2(sp, load, load_cols, T)

        @block.vector
        def _(dve):
            T = Tally()
            due = T.step

            def norm(dst, tiles, summed=False):
                for t in () if summed else tiles:
                    dve.tensor_tensor_reduce(dst[:, t, :], X[:, t, :], X[:, t, :], 1.0, 0.0, ALU.mult, ALU.add,
                                             ss[:, t:t + 1]).then_inc(S("dve_step"), 1)
                    dve.wait_ge(S("dve_step"), due("dve_step"))
                n = len(tiles)
                dve.tensor_scalar(inv[:, 0:n], ss[:, 0:n], 1.0 / D, EPS, ALU.mult, ALU.add).then_inc(S("dve_step"), 1)
                dve.wait_ge(S("dve_step"), due("dve_step"))
                dve.reciprocal(inv[:, 0:n], inv[:, 0:n]).then_inc(S("inv_ready"), 1)
                dve.wait_ge(S("inv_ready"), due("inv_ready"))
                dve.wait_ge(S("rstd_ready"), due("rstd_ready"))
                for t in tiles:
                    dve.tensor_scalar(dst[:, t, :], X[:, t, :], rstd[:, t:t + 1], None, ALU.mult).then_inc(S("xn_ready"), 1)
                    dve.wait_ge(S("xn_ready"), due("xn_ready"))

            def mod_step(cur, turned):
                if cur:
                    l, seg = cur
                    dve.wait_ge(S("fullD"), due("fullD"))
                    b = bank_of("D", T.n["fullD"])
                    if cur == (0, 2):
                        dve.wait_ge(S("gate_bias_landed"), due("gate_bias_landed", 96))
                    for h in range(2):
                        src = b[64 * h:64 * h + 2, :]
                        if seg % 3 == 2:
                            g = gate_rows[32 * l:32 * l + 2, seg // 3, h * 512:h * 512 + 512]
                            signal = "freeD" if h == 1 else "dve_step"
                            dve.tensor_tensor(g, src, g, ALU.add).then_inc(S(signal), 1)
                            dve.wait_ge(S(signal), due(signal))
                        else:
                            signal = "freeD" if h == 1 else "dve_step"
                            dve.tensor_copy(row_tmp[:, seg % 3, h * 512:h * 512 + 512], src).then_inc(S(signal), 1)
                            dve.wait_ge(S(signal), due(signal))
                    if seg % 3 != 2:
                        dve.memset(flag, 0.0).then_inc(S("seg_row_ready"), 1)
                        dve.wait_ge(S("seg_row_ready"), due("seg_row_ready"))
                if turned:
                    l, seg = turned
                    dve.wait_ge(S("fullD"), due("fullD"))
                    b = bank_of("D", T.n["fullD"])
                    col = mod_cols[:, 2 * l + seg // 3, 1 - seg % 3, :, :]
                    bias = vecs[:, l, 32 + 8 * seg:40 + 8 * seg].unsqueeze(2).to_broadcast([P, KD, 2])
                    dve.tensor_tensor(col, b[:, 0:16].rearrange("p (k s) -> p k s", s=2), bias, ALU.add).then_inc(S("freeD"), 1)
                    dve.wait_ge(S("freeD"), due("freeD"))
                    if seg % 3 == 1:
                        gain = vecs[:, l, 8 * (seg // 3):8 * (seg // 3) + 8].unsqueeze(2).to_broadcast([P, KD, 2])
                        dve.scalar_tensor_tensor(out=col, in0=col, scalar=1.0, in1=gain, op0=ALU.add, op1=ALU.mult).then_inc(S("dve_step"), 1)
                        dve.wait_ge(S("dve_step"), due("dve_step"))

            def modulate(dst, which, streams):
                for k in range(0, KD, 2):
                    dve.wait_ge(S("fullD"), due("fullD"))
                    b = bank_of("D", T.n["fullD"])
                    for s in range(streams):
                        signal = "freeD" if s == streams - 1 else "dve_step"
                        dve.tensor_scalar(dst[:, k, s * SEQ:s * SEQ + SEQ], b[:, s * SEQ:s * SEQ + SEQ],
                                          mod_cols[:, which, 0, k, s:s + 1], mod_cols[:, which, 1, k, s:s + 1],
                                          ALU.mult, ALU.add).then_inc(S(signal), 1)
                        dve.wait_ge(S(signal), due(signal))
                    dve.memset(flag, 0.0).then_inc(S("hT_ready_dve"), 1)
                    dve.wait_ge(S("hT_ready_dve"), due("hT_ready_dve"))

            def heads_norm(t, c0, n, l, which):
                z = Z[:, t, c0:c0 + n * HD]
                z3 = z.rearrange("p (h d) -> p h d", d=HD)
                sq = head_sq[:, 0:n * HD]
                dve.tensor_tensor(sq, z, z, ALU.mult).then_inc(S("dve_step"), 1)
                dve.wait_ge(S("dve_step"), due("dve_step"))
                dve.tensor_reduce(head_ss[:, 0:n], sq.rearrange("p (h d) -> p h d", d=HD), AX, ALU.add).then_inc(S("dve_step"), 1)
                dve.wait_ge(S("dve_step"), due("dve_step"))
                dve.tensor_scalar(head_inv[:, 0:n], head_ss[:, 0:n], 1.0 / HD, EPS, ALU.mult, ALU.add).then_inc(S("dve_step"), 1)
                dve.wait_ge(S("dve_step"), due("dve_step"))
                dve.reciprocal(head_inv[:, 0:n], head_inv[:, 0:n]).then_inc(S("inv_ready"), 1)
                dve.wait_ge(S("inv_ready"), due("inv_ready"))
                dve.wait_ge(S("rstd_ready"), due("rstd_ready"))
                dve.tensor_tensor(z3, z3, head_rstd[:, 0:n].unsqueeze(2).to_broadcast([P, n, HD]), ALU.mult).then_inc(S("dve_step"), 1)
                dve.wait_ge(S("dve_step"), due("dve_step"))
                dve.tensor_tensor(z3, z3, qk_gain[:, l, which, :].unsqueeze(1).to_broadcast([P, n, HD]), ALU.mult).then_inc(S("dve_step"), 1)
                dve.wait_ge(S("dve_step"), due("dve_step"))

            def rope(t, c0, n):
                z = Z[:, t, c0:c0 + n * HD].rearrange("p (h i two) -> p h i two", two=2, i=32)
                x0, x1 = z[:, :, :, 0], z[:, :, :, 1]
                cos = C("rope_cos", 2, 32)[:, t, :].unsqueeze(1).to_broadcast([P, n, 32])
                sin = C("rope_sin", 2, 32)[:, t, :].unsqueeze(1).to_broadcast([P, n, 32])
                tmp = [rope_tmp[:, i, 0:n * 32].rearrange("p (h i) -> p h i", i=32) for i in range(4)]
                for d, (x, c) in zip(tmp, ((x0, cos), (x1, sin), (x0, sin), (x1, cos))):
                    dve.tensor_tensor(d, x, c, ALU.mult).then_inc(S("dve_step"), 1)
                    dve.wait_ge(S("dve_step"), due("dve_step"))
                dve.tensor_tensor(x0, tmp[0], tmp[1], ALU.subtract).then_inc(S("dve_step"), 1)
                dve.wait_ge(S("dve_step"), due("dve_step"))
                dve.tensor_tensor(x1, tmp[2], tmp[3], ALU.add).then_inc(S("dve_step"), 1)
                dve.wait_ge(S("dve_step"), due("dve_step"))

            def split_heads(b, pairs, dst, h0, cols, p0):
                for odd in range(2):
                    src = b[64 * odd:64 * odd + 64, 0:pairs * P].rearrange("p (h i) -> p h i", i=P)
                    yield dst[p0:p0 + HD, h0 + odd:h0 + 2 * pairs:2, cols:cols + P], src

            def take_q(t):
                for pairs, h0 in ((4, 0), (2, 8)):
                    dve.wait_ge(S("fullD"), due("fullD"))
                    b = bank_of("D", T.n["fullD"])
                    for n, (d, s) in enumerate(split_heads(b, pairs, qT, h0, (t % 2) * P, 64 * (t // 2))):
                        signal = "freeD" if n else "dve_step"
                        dve.tensor_copy(d, s).then_inc(S(signal), 1)
                        dve.wait_ge(S(signal), due(signal))
                        dve.memset(flag, 0.0).then_inc(S("qT_ready"), 1)
                        dve.wait_ge(S("qT_ready"), due("qT_ready"))

            def take_k(t):
                dve.wait_ge(S("fullD"), due("fullD"))
                b = bank_of("D", T.n["fullD"])
                for p0 in ((0,) if t < 2 else (0, 64)):
                    for n, (d, s) in enumerate(split_heads(b, 2, kT, 0, t * P, p0)):
                        dve.tensor_copy(d, s).then_inc(S("dve_step"), 1)
                        dve.wait_ge(S("dve_step"), due("dve_step"))
                dve.memset(flag, 0.0).then_inc(S("freeD"), 1)
                dve.wait_ge(S("freeD"), due("freeD"))
                for _ in range(2 if t < 2 else 4):
                    dve.memset(flag, 0.0).then_inc(S("kT_ready"), 1)
                    dve.wait_ge(S("kT_ready"), due("kT_ready"))

            def attention(l, streams):
                groups = [(t // 2, t, grp) for t in range(2 * streams) for grp in range(3)]

                def take_scores(step, s, t, grp):
                    nk = 512 - 256 * s
                    if step >= 2:
                        dve.wait_ge(S("probs_turned"), due("probs_turned"))
                    for h in range(4):
                        dve.wait_ge(S("fullD"), due("fullD"))
                        b = bank_of("D", T.n["fullD"])
                        if grp == 2 and s == 0:
                            mask = C("band", 2, 512)[:, t, :]
                        else:
                            mask = zero.to_broadcast([P, nk])
                        low = sinks[:, l, h:h + 1] if grp == 2 else -3.0e38
                        dve.tensor_tensor_reduce(probs_buf[step % 2][:, h, 0:nk], b[:, 0:nk], mask, SCALE, low, ALU.add,
                                                 ALU.max, row_max[:, h:h + 1]).then_inc(S("freeD"), 1)
                        dve.wait_ge(S("freeD"), due("freeD"))
                    dve.tensor_scalar(row_neg[step % 2], row_max, -1.0, None, ALU.mult).then_inc(S("scores_ready"), 1)
                    dve.wait_ge(S("scores_ready"), due("scores_ready"))

                take_scores(0, *groups[0])
                for step, (s, t, grp) in enumerate(groups):
                    if step + 1 < len(groups):
                        take_scores(step + 1, *groups[step + 1])
                    probs, nk = probs_buf[step % 2], 512 - 256 * s
                    dve.wait_ge(S("exp_ready"), due("exp_ready"))
                    if grp == 2:
                        dve.tensor_tensor(row_sum, row_sum, sink_e, ALU.add).then_inc(S("dve_step"), 1)
                        dve.wait_ge(S("dve_step"), due("dve_step"))
                    dve.reciprocal(row_inv, row_sum).then_inc(S("dve_step"), 1)
                    dve.wait_ge(S("dve_step"), due("dve_step"))
                    for h in range(4):
                        dve.tensor_scalar(probs[:, h, 0:nk], probs[:, h, 0:nk], row_inv[:, h:h + 1], None, ALU.mult).then_inc(S("probs_ready"), 1)
                        dve.wait_ge(S("probs_ready"), due("probs_ready"))
                    if step < len(LATE_STEPS[l]):
                        mod_step(*LATE_STEPS[l][step])
                dve.wait_ge(S("probs_turned"), due("probs_turned", min(2, len(groups))))

            def mixer(l):
                own = range(TILES) if l == 0 else range(2)
                if l:
                    norm(xn, range(TILES))
                modulate(hT, 2 * l, 2)
                def take_z(u):
                    for t in range(0, TILES, 2):
                        if t in own:
                            dve.wait_ge(S("fullD"), due("fullD"))
                            b = bank_of("D", T.n["fullD"])
                            dve.tensor_copy(Z[:, t, u * 512:u * 512 + 512], b[:, :]).then_inc(S("freeD"), 1)
                            dve.wait_ge(S("freeD"), due("freeD"))
                        elif u:
                            dve.wait_ge(S("fullD"), due("fullD"))
                            b = bank_of("D", T.n["fullD"])
                            dve.tensor_copy(Z[:, t, u * 512 + 256:u * 512 + 512], b[:, 0:256]).then_inc(S("freeD"), 1)
                            dve.wait_ge(S("freeD"), due("freeD"))

                take_z(0)
                take_z(1)
                dve.wait_ge(S("z1_ready_act"), due("z1_ready_act"))
                for t in range(TILES):
                    if t in own:
                        heads_norm(t, GQ, 8, l, 0)
                    heads_norm(t, GK, 2, l, 1)
                    if t < 2:
                        rope(t, GQ, 10)
                take_z(2)
                dve.memset(flag, 0.0).then_inc(S("z_ready_dve"), 1)
                dve.wait_ge(S("z_ready_dve"), due("z_ready_dve"))
                dve.wait_ge(S("z_ready_act_v"), due("z_ready_act_v"))
                for t in range(2):
                    rope(t, WQ, 6)
                dve.memset(flag, 0.0).then_inc(S("rope_ready"), 1)
                dve.wait_ge(S("rope_ready"), due("rope_ready"))
                for s in range(len(own) // 2):
                    for c in range(2):
                        dve.wait_ge(S("fullD"), due("fullD"))
                        b = bank_of("D", T.n["fullD"])
                        dve.tensor_copy(four[:, c, :], b[:, :]).then_inc(S("freeD"), 1)
                        dve.wait_ge(S("freeD"), due("freeD"))
                        dve.memset(flag, 0.0).then_inc(S("four_ready"), 1)
                        dve.wait_ge(S("four_ready"), due("four_ready"))
                    dve.wait_ge(S("fT_done"), due("fT_done", 2))
                for t in own:
                    take_q(t)
                for t in range(TILES):
                    take_k(t)
                attention(l, len(own) // 2)
                for n in range(2):
                    for br in range(3):
                        for t in own:
                            dve.wait_ge(S("sig_ready"), due("sig_ready"))
                            dve.wait_ge(S("fullD"), due("fullD"))
                            b = bank_of("D", T.n["fullD"])
                            dst = m_sum[:, t, n * 512:n * 512 + 512]
                            if br == 0:
                                dve.tensor_tensor(dst, b[:, :], sig[:, t, :], ALU.mult).then_inc(S("freeD"), 1)
                                dve.wait_ge(S("freeD"), due("freeD"))
                            else:
                                dve.tensor_tensor(prod[:, t, :], b[:, :], sig[:, t, :], ALU.mult).then_inc(S("freeD"), 1)
                                dve.wait_ge(S("freeD"), due("freeD"))
                                dve.tensor_tensor(dst, dst, prod[:, t, :], ALU.add).then_inc(S("dve_step"), 1)
                                dve.wait_ge(S("dve_step"), due("dve_step"))
                            dve.memset(flag, 0.0).then_inc(S("sig_used"), 1)
                            dve.wait_ge(S("sig_used"), due("sig_used"))
                for s in range(len(own) // 2):
                    for n in range(2):
                        dve.wait_ge(S("fullD"), due("fullD"))
                        b = bank_of("D", T.n["fullD"])
                        dve.tensor_copy(gate_b[:, s, n * 512:n * 512 + 512], b[:, :]).then_inc(S("freeD"), 1)
                        dve.wait_ge(S("freeD"), due("freeD"))
                dve.memset(flag, 0.0).then_inc(S("m_ready"), 1)
                dve.wait_ge(S("m_ready"), due("m_ready"))
                for k in range(0, KD, 2):
                    dve.wait_ge(S("fullD"), due("fullD"))
                    b = bank_of("D", T.n["fullD"])
                    dve.tensor_copy(mT[:, k, 0:P * len(own)], b[:, 0:P * len(own)]).then_inc(S("freeD"), 1)
                    dve.wait_ge(S("freeD"), due("freeD"))
                    dve.memset(flag, 0.0).then_inc(S("mT_ready_dve"), 1)
                    dve.wait_ge(S("mT_ready_dve"), due("mT_ready_dve"))
                for t in own:
                    for n in range(2):
                        dve.wait_ge(S("fullD"), due("fullD"))
                        b = bank_of("D", T.n["fullD"])
                        add_gated(b, gate_b, prod[:, t, :], t, n)
                    dve.tensor_tensor_reduce(sq, X[:, t, :], X[:, t, :], 1.0, 0.0, ALU.mult, ALU.add, ss[:, t:t + 1]).then_inc(S("dve_step"), 1)
                    dve.wait_ge(S("dve_step"), due("dve_step"))

            def add_gated(b, gate, tmp, t, n):
                x = X[:, t, n * 512:n * 512 + 512]
                dve.tensor_tensor(tmp, b[:, :], gate[:, stream_of(t), n * 512:n * 512 + 512], ALU.mult).then_inc(S("freeD"), 1)
                dve.wait_ge(S("freeD"), due("freeD"))
                dve.tensor_tensor(x, x, tmp, ALU.add).then_inc(S("dve_step"), 1)
                dve.wait_ge(S("dve_step"), due("dve_step"))

            def experts(l):
                ns = 2 if l == 0 else 1
                nt = 2 * ns
                norm(xn2, range(nt), summed=True)
                modulate(h2T, 2 * l + 1, ns)
                dve.wait_ge(S("fullD"), due("fullD"))
                b = bank_of("D", T.n["fullD"])
                lg = b[:, 0:nt * E].rearrange("p (t e) -> p t e", e=E)
                dve.tensor_reduce(aff_m[:, 0:nt], lg, AX, ALU.max).then_inc(S("dve_step"), 1)
                dve.wait_ge(S("dve_step"), due("dve_step"))
                dve.tensor_tensor(logit[:, 0:nt, :], lg, aff_m[:, 0:nt].unsqueeze(2).to_broadcast([P, nt, E]),
                                  ALU.subtract).then_inc(S("freeD"), 1)
                dve.wait_ge(S("freeD"), due("freeD"))
                dve.memset(flag, 0.0).then_inc(S("logits_ready"), 1)
                dve.wait_ge(S("logits_ready"), due("logits_ready"))
                for s in range(ns):
                    for n in range(2):
                        dve.wait_ge(S("fullD"), due("fullD"))
                        b = bank_of("D", T.n["fullD"])
                        dve.tensor_copy(gate2_b[:, s, n * 512:n * 512 + 512], b[:, :]).then_inc(S("freeD"), 1)
                        dve.wait_ge(S("freeD"), due("freeD"))
                dve.wait_ge(S("aff_exp_ready"), due("aff_exp_ready"))
                dve.tensor_reduce(aff_s[:, 0:nt], logit[:, 0:nt, :], AX, ALU.add).then_inc(S("dve_step"), 1)
                dve.wait_ge(S("dve_step"), due("dve_step"))
                dve.reciprocal(aff_i[:, 0:nt], aff_s[:, 0:nt]).then_inc(S("dve_step"), 1)
                dve.wait_ge(S("dve_step"), due("dve_step"))
                dve.tensor_tensor(aff[:, 0:nt, :], logit[:, 0:nt, :],
                                  aff_i[:, 0:nt].unsqueeze(2).to_broadcast([P, nt, E]), ALU.mult).then_inc(S("aff_ready"), 1)
                dve.wait_ge(S("aff_ready"), due("aff_ready"))
                dve.wait_ge(S("fullD"), due("fullD"))
                b = bank_of("D", T.n["fullD"])
                dve.tensor_copy(work[0:E, 0:nt * P], b[0:E, 0:nt * P]).then_inc(S("freeD"), 1)
                dve.wait_ge(S("freeD"), due("freeD"))
                for s in range(ns):
                    w = work[0:E, s * SEQ:s * SEQ + SEQ]
                    for _ in range(CAP // 8):
                        dve.max(best[0:E, :], w).then_inc(S("dve_step"), 1)
                        dve.wait_ge(S("dve_step"), due("dve_step"))
                        dve.match_replace(w, best[0:E, :], w, -1.0).then_inc(S("dve_step"), 1)
                        dve.wait_ge(S("dve_step"), due("dve_step"))
                    dve.tensor_scalar(w, w, 0.0, None, ALU.is_lt).then_inc(S("dve_step"), 1)
                    dve.wait_ge(S("dve_step"), due("dve_step"))
                    c = cum[0:E, s * SEQ:s * SEQ + SEQ]
                    dve.tensor_tensor_scan(affT[0:E, s * SEQ:s * SEQ + SEQ], w, w, 0.0, ALU.add, ALU.max).then_inc(S("dve_step"), 1)
                    dve.wait_ge(S("dve_step"), due("dve_step"))
                    dve.tensor_tensor(c, affT[0:E, s * SEQ:s * SEQ + SEQ], w, ALU.mult).then_inc(S("dve_step"), 1)
                    dve.wait_ge(S("dve_step"), due("dve_step"))
                    dve.tensor_scalar(c, c, -1.0, None, ALU.add).then_inc(S("dve_step"), 1)
                    dve.wait_ge(S("dve_step"), due("dve_step"))
                dve.memset(flag, 0.0).then_inc(S("slots_ready"), 1)
                dve.wait_ge(S("slots_ready"), due("slots_ready"))
                dve.wait_ge(S("fullD"), due("fullD"))
                b = bank_of("D", T.n["fullD"])
                dve.tensor_copy(slot_t[:, 0:nt, :], b[:, 0:nt * E].rearrange("p (t e) -> p t e", e=E)).then_inc(S("freeD"), 1)
                dve.wait_ge(S("freeD"), due("freeD"))
                for t in range(nt):
                    pk = pick[:, t, :].rearrange("p (e c) -> p e c", c=CAP)
                    dve.tensor_tensor(pk, slot_t[:, t, :].unsqueeze(2).to_broadcast([P, E, CAP]),
                                      C("iota").unsqueeze(1).to_broadcast([P, E, CAP]), ALU.is_equal).then_inc(S("dve_step"), 1)
                    dve.wait_ge(S("dve_step"), due("dve_step"))
                    dve.tensor_tensor(pick_g[:, t, :].rearrange("p (e c) -> p e c", c=CAP), pk,
                                      aff[:, t, :].unsqueeze(2).to_broadcast([P, E, CAP]), ALU.mult).then_inc(S("dve_step"), 1)
                    dve.wait_ge(S("dve_step"), due("dve_step"))
                dve.memset(flag, 0.0).then_inc(S("pick_ready"), 1)
                dve.wait_ge(S("pick_ready"), due("pick_ready"))
                for k in range(KD):
                    if ns == 1 and k % 2:
                        continue
                    dve.wait_ge(S("fullD"), due("fullD"))
                    b = bank_of("D", T.n["fullD"])
                    dve.tensor_scalar(xgT[:, k, :, 0:CAP], b[:, :].rearrange("p (e c) -> p e c", c=CAP),
                                      mod_cols[:, 2 * l + 1, 0, k, 0:1], mod_cols[:, 2 * l + 1, 1, k, 0:1], ALU.mult, ALU.add).then_inc(S("freeD"), 1)
                    dve.wait_ge(S("freeD"), due("freeD"))
                dve.wait_ge(S("xgT_done"), due("xgT_done"))
                for t in range(nt):
                    dve.wait_ge(S("fullD"), due("fullD"))
                    b = bank_of("D", T.n["fullD"])
                    dve.tensor_copy(putT[:, t, :, :], b[:, :].rearrange("p (g i) -> p g i", g=4)).then_inc(S("freeD"), 1)
                    dve.wait_ge(S("freeD"), due("freeD"))
                dve.memset(out_g, 0.0).then_inc(S("dve_step"), 1)
                dve.wait_ge(S("dve_step"), due("dve_step"))
                dve.memset(puts, 0.0).then_inc(S("puts_ready"), 1)
                dve.wait_ge(S("puts_ready"), due("puts_ready"))
                R = CAP * ns

                def take_scatter():
                    for t in range(nt):
                        for n in range(2):
                            x = X[:, t, n * 512:n * 512 + 512]
                            dve.wait_ge(S("fullD"), due("fullD"))
                            b = bank_of("D", T.n["fullD"])
                            dve.tensor_tensor(x, b[:, :], x, ALU.add).then_inc(S("freeD"), 1)
                            dve.wait_ge(S("freeD"), due("freeD"))

                per = {"fullD": 16 + 4 * ns, "silu_ready": 8, "dve_step": 4 * (2 * ns - 1), "freeD": 16 + 4 * ns,
                       "xgs_ready": 1, "puts_ready": 1, "hid_ready": 8, "hidT_ready": 4, "out_ready": 4}
                with dve.Fori(0, 4) as i:
                    T.enter(i, per)
                    src = xgT.rearrange("p k (g j) r -> p k g j r", j=4)
                    dve.tensor_copy(xgs[:, :, :, 0:R], src[:, :, i, :, 0:R]).then_inc(S("xgs_ready"), 1)
                    dve.wait_ge(S("xgs_ready"), due("xgs_ready"))
                    for j in range(4):
                        for n in range(2):
                            dve.wait_ge(S("silu_ready"), due("silu_ready"))
                            dve.wait_ge(S("fullD"), due("fullD"))
                            b = bank_of("D", T.n["fullD"])
                            dve.tensor_tensor(hid[0:R, n * 512:n * 512 + 512], b[64:64 + R, :], silu_g[0:R, n, :], ALU.mult).then_inc(S("hid_ready"), 1)
                            dve.wait_ge(S("hid_ready"), due("hid_ready"))
                            dve.memset(flag, 0.0).then_inc(S("freeD"), 1)
                            dve.wait_ge(S("freeD"), due("freeD"))
                        if j == 0:
                            take_scatter()
                            dve.tensor_copy(puts[:, 0:nt, :], putT[:, 0:nt, i, :]).then_inc(S("puts_ready"), 1)
                            dve.wait_ge(S("puts_ready"), due("puts_ready"))
                        dve.wait_ge(S("fullD"), due("fullD"))
                        b = bank_of("D", T.n["fullD"])
                        dve.tensor_copy(hidT[:, :, 0:R], b[:, :].rearrange("p (k r) -> p k r", r=64)[:, :, 0:R]).then_inc(S("hidT_ready"), 1)
                        dve.wait_ge(S("hidT_ready"), due("hidT_ready"))
                        dve.memset(flag, 0.0).then_inc(S("freeD"), 1)
                        dve.wait_ge(S("freeD"), due("freeD"))
                        dve.wait_ge(S("fullD"), due("fullD"))
                        b = bank_of("D", T.n["fullD"])
                        rows_ = slice(CAP * j, CAP * j + CAP)
                        for n in range(2):
                            for s in range(ns):
                                last = n == 1 and s == ns - 1
                                signal = "freeD" if last else "dve_step"
                                dve.tensor_tensor(out_g[rows_, s, n * 512:n * 512 + 512],
                                                  b[64 * n + CAP * s:64 * n + CAP * s + CAP, :],
                                                  gate2_b[rows_, s, n * 512:n * 512 + 512], ALU.mult).then_inc(S(signal), 1)
                                dve.wait_ge(S(signal), due(signal))
                        dve.memset(flag, 0.0).then_inc(S("out_ready"), 1)
                        dve.wait_ge(S("out_ready"), due("out_ready"))
                T.leave(4)
                take_scatter()

            dve.memset(small[:, :], 0.0).then_inc(S("dve_step"), 1)
            dve.wait_ge(S("dve_step"), due("dve_step"))
            for _ in range(POOL):
                dve.memset(flag, 0.0).then_inc(S("freeD"), 1)
                dve.wait_ge(S("freeD"), due("freeD"))
            dve.memset(ones, 1.0).then_inc(S("small_ready"), 1)
            dve.wait_ge(S("small_ready"), due("small_ready"))
            dve.memset(flag, 0.0).then_inc(S("small_ready_a"), 1)
            dve.wait_ge(S("small_ready_a"), due("small_ready_a"))
            dve.wait_ge(S("const_landed"), 16)
            dve.wait_ge(S("fullD"), due("fullD"))
            b = bank_of("D", T.n["fullD"])
            for v in range(4):
                dve.tensor_copy(vecs[:, v, 0:VEC_ROWS[v]], b[:, v * P:v * P + VEC_ROWS[v]]).then_inc(S("dve_step"), 1)
                dve.wait_ge(S("dve_step"), due("dve_step"))
            dve.memset(flag, 0.0).then_inc(S("vecs_ready"), 1)
            dve.wait_ge(S("vecs_ready"), due("vecs_ready"))
            dve.wait_ge(S("smalls_landed"), 16 * N_SMALL)
            dve.wait_ge(S("x_landed"), 16 * 2)
            dve.memset(flag, 0.0).then_inc(S("freeD"), 1)
            dve.wait_ge(S("freeD"), due("freeD"))
            norm(xn, range(TILES))
            for step in EARLY_STEPS:
                mod_step(*step)
            dve.memset(flag, 0.0).then_inc(S("mod_cols_ready"), 1)
            dve.wait_ge(S("mod_cols_ready"), due("mod_cols_ready"))
            for l in range(DEPTH):
                mixer(l)
                experts(l)
            dve_block2(dve, T, norm, modulate, add_gated)

        @block.scalar
        def _(act):
            T = Tally()
            due = T.step

            def norm(n):
                act.wait_ge(S("inv_ready"), due("inv_ready"))
                act.activation(rstd[:, 0:n], inv[:, 0:n], ACT.Sqrt).then_inc(S("rstd_ready"), 1)
                act.wait_ge(S("rstd_ready"), due("rstd_ready"))

            def heads_norm(n):
                act.wait_ge(S("inv_ready"), due("inv_ready"))
                act.activation(head_rstd[:, 0:n], head_inv[:, 0:n], ACT.Sqrt).then_inc(S("rstd_ready"), 1)
                act.wait_ge(S("rstd_ready"), due("rstd_ready"))

            def modulate(dst, which, streams):
                for k in range(1, KD, 2):
                    act.wait_ge(S("fullA"), due("fullA"))
                    b = bank_of("A", T.n["fullA"])
                    for s in range(streams):
                        signal = "freeA" if s == streams - 1 else "act_step"
                        act.activation(dst[:, k, s * SEQ:s * SEQ + SEQ], b[:, s * SEQ:s * SEQ + SEQ], ACT.Identity,
                                       scale=mod_cols[:, which, 0, k, s:s + 1], bias=mod_cols[:, which, 1, k, s:s + 1]).then_inc(S(signal), 1)
                        act.wait_ge(S(signal), due(signal))
                    act.activation(flag_a, zero, ACT.Copy).then_inc(S("hT_ready_act"), 1)
                    act.wait_ge(S("hT_ready_act"), due("hT_ready_act"))

            def attention(l, streams):
                groups = [(t // 2, t, grp) for t in range(2 * streams) for grp in range(3)]
                for step, (s, t, grp) in enumerate(groups):
                    probs, neg = probs_buf[step % 2], row_neg[step % 2]
                    nk = 512 - 256 * s
                    keys = range(2 * s, TILES)
                    act.wait_ge(S("scores_ready"), due("scores_ready"))
                    for h in range(4):
                        act.activation(probs[:, h, 0:nk], probs[:, h, 0:nk], ACT.Exp, bias=neg[:, h:h + 1],
                                       accum_out=row_sum[:, h:h + 1]).then_inc(S("act_step"), 1)
                        act.wait_ge(S("act_step"), due("act_step"))
                        if grp == 2:
                            act.activation(sink_e[:, h:h + 1], sinks[:, l, h:h + 1], ACT.Exp, bias=neg[:, h:h + 1]).then_inc(S("act_step"), 1)
                            act.wait_ge(S("act_step"), due("act_step"))
                    act.activation(flag_a, zero, ACT.Copy).then_inc(S("exp_ready"), 1)
                    act.wait_ge(S("exp_ready"), due("exp_ready"))
                    for kt in keys:
                        act.wait_ge(S("fullA"), due("fullA"))
                        b = bank_of("A", T.n["fullA"])
                        act.activation(probsT[:, kt, :], b[:, :], ACT.Copy).then_inc(S("freeA"), 1)
                        act.wait_ge(S("freeA"), due("freeA"))
                        if kt == keys[-1]:
                            act.activation(flag_a, zero, ACT.Copy).then_inc(S("probs_turned"), 1)
                            act.wait_ge(S("probs_turned"), due("probs_turned"))
                        act.activation(flag_a, zero, ACT.Copy).then_inc(S("probsT_ready"), 1)
                        act.wait_ge(S("probsT_ready"), due("probsT_ready"))
                    act.wait_ge(S("fullA"), due("fullA"))
                    b = bank_of("A", T.n["fullA"])
                    act.activation(oT[:, 2 * grp:2 * grp + 2, t * P:t * P + P],
                                   b[:, 0:256].rearrange("p (a i) -> p a i", a=2), ACT.Copy).then_inc(S("freeA"), 1)
                    act.wait_ge(S("freeA"), due("freeA"))
                    act.activation(flag_a, zero, ACT.Copy).then_inc(S("oT_ready"), 1)
                    act.wait_ge(S("oT_ready"), due("oT_ready"))

            def mixer(l):
                own = range(TILES) if l == 0 else range(2)
                norm(TILES)
                if l == 0:
                    act.wait_ge(S("mod_cols_ready"), due("mod_cols_ready"))
                modulate(hT, 2 * l, 2)
                def take_z(u):
                    for t in range(1, TILES, 2):
                        if t in own:
                            act.wait_ge(S("fullA"), due("fullA"))
                            b = bank_of("A", T.n["fullA"])
                            act.activation(Z[:, t, u * 512:u * 512 + 512], b[:, :], ACT.Copy).then_inc(S("freeA"), 1)
                            act.wait_ge(S("freeA"), due("freeA"))
                        elif u:
                            act.wait_ge(S("fullA"), due("fullA"))
                            b = bank_of("A", T.n["fullA"])
                            act.activation(Z[:, t, u * 512 + 256:u * 512 + 512], b[:, 0:256], ACT.Copy).then_inc(S("freeA"), 1)
                            act.wait_ge(S("freeA"), due("freeA"))

                take_z(0)
                take_z(1)
                act.activation(flag_a, zero, ACT.Copy).then_inc(S("z1_ready_act"), 1)
                act.wait_ge(S("z1_ready_act"), due("z1_ready_act"))
                for t in range(TILES):
                    if t in own:
                        heads_norm(8)
                    heads_norm(2)
                take_z(2)
                act.activation(flag_a, zero, ACT.Copy).then_inc(S("z_ready_act"), 1)
                act.wait_ge(S("z_ready_act"), due("z_ready_act"))
                act.activation(flag_a, zero, ACT.Copy).then_inc(S("z_ready_act_v"), 1)
                act.wait_ge(S("z_ready_act_v"), due("z_ready_act_v"))
                for s in range(len(own) // 2):
                    for c in range(2):
                        act.wait_ge(S("fullA"), due("fullA"))
                        b = bank_of("A", T.n["fullA"])
                        act.activation(fT[:, c, s * SEQ:s * SEQ + SEQ], b[:, 0:SEQ], ACT.Copy).then_inc(S("freeA"), 1)
                        act.wait_ge(S("freeA"), due("freeA"))
                        act.activation(flag_a, zero, ACT.Copy).then_inc(S("fT_done"), 1)
                        act.wait_ge(S("fT_done"), due("fT_done"))
                        act.activation(flag_a, zero, ACT.Copy).then_inc(S("fT_ready"), 1)
                        act.wait_ge(S("fT_ready"), due("fT_ready"))
                attention(l, len(own) // 2)
                for n in range(2):
                    for br in range(3):
                        for t in own:
                            if n or br:
                                act.wait_ge(S("sig_used"), due("sig_used"))
                            act.wait_ge(S("fullA"), due("fullA"))
                            b = bank_of("A", T.n["fullA"])
                            act.activation(sig[:, t, :], b[:, :], ACT.Sigmoid).then_inc(S("freeA"), 1)
                            act.wait_ge(S("freeA"), due("freeA"))
                            act.activation(flag_a, zero, ACT.Copy).then_inc(S("sig_ready"), 1)
                            act.wait_ge(S("sig_ready"), due("sig_ready"))
                act.wait_ge(S("sig_used"), due("sig_used", len(own)))
                for k in range(1, KD, 2):
                    act.wait_ge(S("fullA"), due("fullA"))
                    b = bank_of("A", T.n["fullA"])
                    act.activation(mT[:, k, 0:P * len(own)], b[:, 0:P * len(own)], ACT.Copy).then_inc(S("freeA"), 1)
                    act.wait_ge(S("freeA"), due("freeA"))
                    act.activation(flag_a, zero, ACT.Copy).then_inc(S("mT_ready_act"), 1)
                    act.wait_ge(S("mT_ready_act"), due("mT_ready_act"))

            def experts(l):
                ns = 2 if l == 0 else 1
                nt = 2 * ns
                norm(nt)
                modulate(h2T, 2 * l + 1, ns)
                act.wait_ge(S("logits_ready"), due("logits_ready"))
                act.activation(logit[:, 0:nt, :], logit[:, 0:nt, :], ACT.Exp).then_inc(S("aff_exp_ready"), 1)
                act.wait_ge(S("aff_exp_ready"), due("aff_exp_ready"))
                for k in range(KD):
                    if ns == 1 and k % 2 == 0:
                        continue
                    s = ns - 1
                    act.wait_ge(S("fullA"), due("fullA"))
                    b = bank_of("A", T.n["fullA"])
                    act.activation(xgT[:, k, :, CAP * s:CAP * s + CAP], b[:, :].rearrange("p (e c) -> p e c", c=CAP),
                                   ACT.Identity, scale=mod_cols[:, 2 * l + 1, 0, k, s:s + 1], bias=mod_cols[:, 2 * l + 1, 1, k, s:s + 1]).then_inc(S("freeA"), 1)
                    act.wait_ge(S("freeA"), due("freeA"))
                act.activation(flag_a, zero, ACT.Copy).then_inc(S("xgT_done"), 1)
                act.wait_ge(S("xgT_done"), due("xgT_done"))
                R = CAP * ns
                per = {"silu_ready": 8}
                with act.Fori(0, 4) as i:
                    T.enter(i, per)
                    for j in range(4):
                        for n in range(2):
                            job = expert_start[l] + 4 * j + n + (4 * ns if j else 0)
                            act.wait_ge(S("fullD"), i * (16 + 4 * ns) + job + 1)
                            bD = pool_banks["D"][job % POOL]
                            act.activation(silu_g[0:R, n, :], bD[0:R, :], ACT.Silu).then_inc(S("silu_ready"), 1)
                            act.wait_ge(S("silu_ready"), due("silu_ready"))
                T.leave(4)

            act.dma_start(const[:, :], A["const"]).then_inc(S("const_landed"), 16)
            act.dma_start(X[:, 0:2, :], A["x"][0].rearrange("(t p) n -> p t n", p=P)).then_inc(S("x_landed"), 16)
            act.dma_start(X[:, 2:4, :], A["ctx"][0].rearrange("(t p) n -> p t n", p=P)).then_inc(S("x_landed"), 16)
            for dst, src in small_loads:
                act.dma_start(dst, src).then_inc(S("smalls_landed"), 16)
            act.wait_ge(S("small_ready_a"), due("small_ready_a"))
            for _ in range(POOL):
                act.activation(flag_a, zero, ACT.Copy).then_inc(S("freeA"), 1)
                act.wait_ge(S("freeA"), due("freeA"))
            act.wait_ge(S("vecs_ready"), due("vecs_ready"))
            for l in range(3):
                for s in range(2):
                    act.activation(silu_c[:, l, :, s], vecs[:, l, 16 + 8 * s:24 + 8 * s], ACT.Silu).then_inc(S("silu_c_ready"), 1)
                    act.wait_ge(S("silu_c_ready"), due("silu_c_ready"))
            for l in range(DEPTH):
                mixer(l)
                experts(l)
            act_block2(act, T, norm, modulate)


_INS = ("x c ctx c_ctx w_ada b_ada norm1_g w_in q_norm_g k_norm_g sink w_br_fourier w_br_global w_br_window w_out "
        "norm2_g w_router w_gate_e w_up_e w_down_e final_g c_2 ctx_2 c_ctx_2 w_mod_2 b_mod_2 norm_mix_pre_2 "
        "norm_mix_post_2 norm_ffn_pre_2 norm_ffn_post_2 w_in_2 conv_w_2 conv_b_2 gla_wg_f_2 gla_bg_f_2 gla_wg_b_2 "
        "gla_bg_b_2 gla_norm_2 a_log_f_2 a_log_b_2 dt_bias_f_2 dt_bias_b_2 d_skip_2 ssd_norm_2 w_out_2 w_gate_2 "
        "w_up_2 w_down_2").split()


def kernel(**inputs):
    import concourse.bacc as _bacc
    from concourse.bass_utils import run_bass_kernel_spmd as _run

    nc = _bacc.Bacc("TRN2", target_bir_lowering=False, num_devices=1)
    arrays, A = {}, {}
    for name, a in [("const", constants())] + [(n, inputs[n]) for n in _INS]:
        a = np.ascontiguousarray(a)
        arrays[f"in_{name}"] = a
        A[name] = nc.dram_tensor(f"in_{name}", a.shape, mybir.dt.from_np(a.dtype), kind="ExternalInput").ap()
    out = nc.dram_tensor("out", (1, SEQ, D), F32, kind="ExternalOutput").ap()
    build(nc, A, out)
    r = _run(nc, [arrays], core_ids=[0])
    return r.results[0]["out"]
```
